# Optimizing a Trainium2 kernel written in Bass

```python
import jax, jax.numpy as jnp
from jax import lax
import numpy as np

D_MODEL = 1024
BATCH = 1
SEQ = 1024
DEPTH = 2

D_A = D_MODEL
CONV_W = 3
D_B = D_MODEL
DH_B = 128
G_B = D_B // DH_B
CHUNK = 128
D_C = D_MODEL
DH_C = 64
H_C = D_C // DH_C
QBLK = 128

IN_AB = 4 * D_A + 3 * D_B
IN_C = 4 * D_C
N_EVEN = (DEPTH + 1) // 2
N_ODD = DEPTH // 2
EPS = 1e-6

kernel_name = "hybrid_conv_sgmlp_stickbreak_adaln"

def rms_norm(x, g):
    xf = x.astype(jnp.float32)
    y = xf * lax.rsqrt(jnp.mean(xf * xf, axis=-1, keepdims=True) + EPS)
    return (y * g.astype(jnp.float32)).astype(x.dtype)

def conv_sgmlp_mixer(h, w_in, conv_w, sg_norm, sg_w, sg_b, w_out):
    bsz, s, _ = h.shape
    proj = h @ w_in
    cuts = [D_A, 2 * D_A, 3 * D_A, 4 * D_A, 4 * D_A + D_B, 4 * D_A + 2 * D_B]
    a_b, a_c, a_x, a_z, b_u, b_v, b_z = jnp.split(proj, cuts, axis=-1)
    conv = lax.conv_general_dilated(
        a_c * a_x, conv_w[:, None, :].astype(h.dtype), window_strides=(1,),
        padding=[(CONV_W - 1, 0)], dimension_numbers=('NWC', 'WIO', 'NWC'),
        feature_group_count=D_A)
    y_a = a_b * conv * jax.nn.silu(a_z)
    nc = s // CHUNK
    v = rms_norm(b_v.reshape(bsz, nc, CHUNK, G_B, DH_B), sg_norm)
    mask = jnp.tril(jnp.ones((CHUNK, CHUNK), dtype=bool))
    w_s = jnp.where(mask[None], sg_w, 0.0)
    sgate = jnp.einsum('gts,bcsgd->bctgd', w_s, v) + sg_b.T[:, :, None]
    y_b = b_u * sgate.reshape(bsz, s, D_B) * jax.nn.silu(b_z)
    return jnp.concatenate([y_a, y_b], axis=-1) @ w_out

def stick_breaking_attention(q, k, v):
    bsz, s, h, dh = q.shape
    nb = s // QBLK
    qf = q.astype(jnp.float32) * (dh ** -0.5)
    kf = k.astype(jnp.float32)
    vf = v.astype(jnp.float32)
    q_blocks = qf.reshape(bsz, nb, QBLK, h, dh).transpose(1, 0, 2, 3, 4)
    key_pos = jnp.arange(s)

    def block(args):
        qb, i = args
        qpos = i * QBLK + jnp.arange(QBLK)
        z = jnp.einsum('bthd,bshd->bhts', qb, kf)
        causal = key_pos[None, :] < qpos[:, None]
        log_beta = jax.nn.log_sigmoid(z)
        log_1mb = jnp.where(causal, log_beta - z, 0.0)
        suffix = lax.cumsum(log_1mb, axis=3, reverse=True) - log_1mb
        w = jnp.where(causal, jnp.exp(log_beta + suffix), 0.0)
        return jnp.einsum('bhts,bshd->bthd', w, vf)

    out = lax.map(block, (q_blocks, jnp.arange(nb)))
    return out.transpose(1, 0, 2, 3, 4).reshape(bsz, s, h, dh).astype(q.dtype)

def stick_breaking_mixer(h, w_in, q_norm, k_norm, w_out):
    bsz, s, _ = h.shape
    q, k, v, z = jnp.split(h @ w_in, 4, axis=-1)
    q = rms_norm(q.reshape(bsz, s, H_C, DH_C), q_norm)
    k = rms_norm(k.reshape(bsz, s, H_C, DH_C), k_norm)
    v = v.reshape(bsz, s, H_C, DH_C)
    o = stick_breaking_attention(q, k, v).reshape(bsz, s, D_C)
    return (o * jax.nn.silu(z)) @ w_out

def setup_inputs(seed: int = 0) -> dict:
    key = jax.random.key(seed)
    ks = jax.random.split(key, 16)

    def nrm(k, shape, scale):
        return jax.random.normal(k, shape, jnp.float32) * scale

    return {
        "x": nrm(ks[0], (BATCH, SEQ, D_MODEL), 1.0),
        "c": nrm(ks[1], (BATCH, D_MODEL), 1.0),
        "ln_g": 1.0 + nrm(ks[2], (DEPTH, D_MODEL), 0.1),
        "ada_w": nrm(ks[3], (DEPTH, D_MODEL, 3 * D_MODEL), D_MODEL ** -0.5),
        "ada_b": nrm(ks[4], (DEPTH, 3 * D_MODEL), 0.1),
        "w_in_ab": nrm(ks[5], (N_EVEN, D_MODEL, IN_AB), D_MODEL ** -0.5),
        "conv_w": nrm(ks[6], (N_EVEN, CONV_W, D_A), CONV_W ** -0.5),
        "sg_norm": 1.0 + nrm(ks[7], (N_EVEN, G_B, DH_B), 0.1),
        "sg_w": nrm(ks[8], (N_EVEN, G_B, CHUNK, CHUNK), CHUNK ** -0.5),
        "sg_b": 1.0 + nrm(ks[9], (N_EVEN, G_B, CHUNK), 0.1),
        "w_out_ab": nrm(ks[10], (N_EVEN, D_A + D_B, D_MODEL), (D_A + D_B) ** -0.5),
        "w_in_c": nrm(ks[11], (N_ODD, D_MODEL, IN_C), D_MODEL ** -0.5),
        "q_norm": 1.0 + nrm(ks[12], (N_ODD, DH_C), 0.1),
        "k_norm": 1.0 + nrm(ks[13], (N_ODD, DH_C), 0.1),
        "w_out_c": nrm(ks[14], (N_ODD, D_C, D_MODEL), D_C ** -0.5),
    }

def reference(x, c, ln_g, ada_w, ada_b, w_in_ab, conv_w, sg_norm, sg_w, sg_b,
              w_out_ab, w_in_c, q_norm, k_norm, w_out_c):
    c_act = jax.nn.silu(c)
    for l in range(DEPTH):
        mod = c_act @ ada_w[l] + ada_b[l]
        shift, scale, gate = jnp.split(mod, 3, axis=-1)
        h = rms_norm(x, ln_g[l]) * (1.0 + scale[:, None, :]) + shift[:, None, :]
        i = l // 2
        if l % 2 == 0:
            out = conv_sgmlp_mixer(h, w_in_ab[i], conv_w[i], sg_norm[i], sg_w[i],
                                   sg_b[i], w_out_ab[i])
        else:
            out = stick_breaking_mixer(h, w_in_c[i], q_norm[i], k_norm[i], w_out_c[i])
        x = x + gate[:, None, :] * out
    return x


_drawn_inputs = setup_inputs


def setup_inputs(seed=0):
    import zlib

    import numpy as np

    out = dict(_drawn_inputs(seed))
    spreads = {}
    factors = {'q_norm': 5.259, 'k_norm': 4.702}
    for name, (base, spread) in spreads.items():
        noise = np.random.default_rng([zlib.crc32(name.encode()), seed]).standard_normal(out[name].shape)
        drawn = base * np.exp(spread * noise) if base else spread * noise
        out[name] = __import__('jax').numpy.asarray(drawn.astype(out[name].dtype))
    for name, factor in factors.items():
        out[name] = (out[name] * factor).astype(out[name].dtype)
    return out
```

```python
from contextlib import ExitStack

import concourse.bass as bass
from concourse import mybir

F32 = mybir.dt.float32
F32R = mybir.dt.float32r
U32 = mybir.dt.uint32
ALU = mybir.AluOpType
ACT = mybir.ActivationFunctionType
AX_X = mybir.AxisListType.X

P = 128
SIGN = 0x80000000
LN_EXP_SET = "natural_log_exp_and_others"
SILU_SET = "silu_and_others"


class Lin:

    def __init__(self, base, turn=0, coef=0):
        self.base, self.turn, self.coef = base, turn, coef

    def __add__(self, n):
        return Lin(self.base + n, self.turn, self.coef)

    def __sub__(self, n):
        return self + -n

    def __mul__(self, n):
        return Lin(self.base * n, self.turn, self.coef * n)

    def half(self):
        assert self.coef % 2 == 0
        return Lin(self.base // 2, self.turn, self.coef // 2)

    @property
    def v(self):
        return self.turn * self.coef + self.base if self.coef else self.base


def hybrid_trunk(nc, x, c, ln_g, ada_w, ada_b, w_in_ab, conv_w, sg_norm, sg_w, sg_b,
                 w_out_ab, w_in_c, q_norm, k_norm, w_out_c, out):
    _, T, D = x.shape
    HT = T // 2
    NB = D // P
    NC = T // P
    CONV_W = conv_w.shape[1]
    G = sg_w.shape[1]
    DH = q_norm.shape[1]
    NP = D // (2 * DH)
    EPS = 1e-6
    NADA = 2 * 3 * NB
    NADA0 = 2 * NB
    assert T == 1024 and D == 1024 and DH == 64 and G == NB

    U_ADA, U_A = 0, NADA0
    U_A2 = U_A + 8 * NB
    U_B = U_A2 + NB
    U_B2 = U_B + 3 * G
    U_C = U_B2 + NB
    U_D = U_C + 4 * NP
    U_END = U_D + NB
    N_A = NC
    N_A2 = N_A + 4 * NB
    N_B = N_A2 + NB
    N_B2 = N_B + 3 * G
    N_C = N_B2 + NB
    C_FILLS = 7
    N_D = N_C + C_FILLS * NP
    STEPS = 24

    chains = [(head, half) for head in range(2) for half in range(2)]
    steps = []
    for ci, (head, half) in enumerate(chains):
        last_block = 4 * half + 3
        for j in range(last_block, -1, -1):
            steps.append(dict(chain=ci, head=head, half=half, j=j, c0=max(0, P * j - HT * half),
                              diagonal=j >= 4 * half, first=j == last_block, last=j == 0))
    assert len(steps) == STEPS

    with ExitStack() as ctx:
        def sb(name, shape, dt=F32):
            return ctx.enter_context(nc.sbuf_tensor(name, shape, dt))

        def sem(name):
            return ctx.enter_context(nc.semaphore(name))

        def dram(name, shape):
            return nc.dram_tensor(name, shape, F32, kind="Internal").ap()

        xd0, xd1, xd2 = (dram(f"x_t{i}", [NB, P, T]) for i in range(3))
        yd = dram("y_t", [NP, P, T])

        hH = sb("hH", [P, NB, T], F32R)
        hL = sb("hL", [P, NB, T], F32R)
        R2 = sb("R2", [P, 16 * T], F32R)
        yH = R2[:, 0:8 * T].rearrange("p (k t) -> p k t", k=NB)
        yL = R2[:, 8 * T:16 * T].rearrange("p (k t) -> p k t", k=NB)
        QP = 6 * T
        Q = [[[R2[:, par * QP + (2 * head + part) * T:par * QP + (2 * head + part + 1) * T]
               for part in range(2)] for head in range(2)] for par in range(2)]
        K = [[R2[:, par * QP + (4 + part) * T:par * QP + (5 + part) * T] for part in range(2)]
             for par in range(2)]
        V = [R2[:, 12 * T + par * 2 * T:12 * T + (par + 1) * 2 * T].rearrange(
            "p (j h d) -> p j h d", j=NC, h=2) for par in range(2)]
        raw = sb("raw", [P, 2, NB, P])
        wH = sb("wH", [P, 2, NB, P], F32R)
        wL = sb("wL", [P, 2, NB, P], F32R)
        spH = sb("spH", [P, 2, HT], F32R)
        spL = sb("spL", [P, 2, HT], F32R)
        pH = sb("pH", [P, HT], F32R)
        pL = sb("pL", [P, HT], F32R)
        sums_in = sb("sums_in", [P, 2, HT])
        FA = sb("FA", [P, 8 * T + 8])
        xT = FA[:, 0:8 * T].rearrange("p (k t) -> p k t", k=NB)
        cs = FA[:, 0:T]
        cx = FA[:, T:2 * T + 2]
        cv = FA[:, 2 * T + 4:3 * T + 4]
        sz = FA[:, 3 * T + 4:4 * T + 4]
        vT = cs
        vn = FA[:, T:2 * T].rearrange("p (c d) -> p c d", c=NC)
        us = FA[:, 4 * T + 4:5 * T + 4]
        xa = [FA[:, (4 + s) * T + 4:(5 + s) * T + 4] for s in range(2)]
        WT = FA[:, 6 * T + 4:7 * T + 4].rearrange("p (g t) -> p g t", g=G)
        sgb = FA[:, 7 * T + 4:8 * T + 4].rearrange("p (g t) -> p g t", g=G)
        zs = [FA[:, s * HT:(s + 1) * HT] for s in range(3)]
        e = [FA[:, (3 + s) * HT:(4 + s) * HT] for s in range(2)]
        osh = FA[:, 5 * HT:6 * HT]
        gz = [FA[:, (3 + s) * T:(4 + s) * T] for s in range(2)]
        qr = FA[:, 5 * T:6 * T]
        kr = FA[:, 6 * T:7 * T]
        ys = FA[:, 0:4 * T].rearrange("p (s t) -> p s t", s=4)
        xt = [FA[:, (4 + s) * T:(5 + s) * T] for s in range(2)]
        ot = [FA[:, (6 + s) * T:(7 + s) * T].rearrange("p (c d) -> p c d", c=NC) for s in range(2)]

        ident = sb("ident", [P, P])
        ones = sb("ones", [P, P])
        pair_ones = sb("pair_ones", [P, P])
        strict = sb("strict", [P, P])
        cap = sb("cap", [P, P])
        U_f = sb("U_f", [P, P])
        U_r = sb("U_r", [P, P], F32R)
        Uc_r = sb("Uc_r", [P, P], F32R)
        prm_rows = sb("prm_rows", [P, P])
        prm = sb("prm", [P, P])
        C_C, C_LN, C_ADA = 0, NB, 3 * NB
        C_CONV = C_ADA + NADA
        C_SGN = C_CONV + CONV_W * NB
        C_QN = C_SGN + G
        C_KN = C_QN + 1
        NPRM = C_KN + 1
        mod = sb("mod", [P, NADA])
        gs = sb("gs", [P, 2 * NB])
        ca = sb("ca", [P, 3, NB])
        cHL = sb("cHL", [P, NB, 2], F32R)
        ssq = sb("ssq", [P, NC])
        rv = sb("rv", [P, NC])
        minus_half = sb("minus_half", [P, NC])
        eps_t = sb("eps_t", [P, 1])
        qn_scaled = sb("qn_scaled", [P, 1])

        def bank(name):
            return ctx.enter_context(nc.psum_tensor(name, [P, HT], F32))

        PB = [bank("P0"), bank("P1")]
        ZB = [bank("Z0"), bank("Z1")]
        CB = [bank("C0"), bank("C1")]
        OB = [bank("O0"), bank("O1")]
        MB = OB[0]

        raw_in = [sem(f"raw_in{s}") for s in range(2)]
        w_hi, w_lo = sem("w_hi"), sem("w_lo")
        filled = [sem(f"filled{b}") for b in range(2)]
        emptied = [sem(f"emptied{b}") for b in range(2)]
        ada_done = sem("ada_done")
        mod_ready = sem("mod_ready")
        prm_in, prm_tr, prm_ready = sem("prm_in"), sem("prm_tr"), sem("prm_ready")
        consts, fr_ready = sem("consts"), sem("fr_ready")
        ce, ca_ready = sem("ce"), sem("ca_ready")
        sq_ready, sum_done, rs_ready = sem("sq_ready"), sem("sum_done"), sem("rs_ready")
        ht_ready, hh_ready, hl_ready = sem("ht_ready"), sem("hh_ready"), sem("hl_ready")
        x_saved = sem("x_saved")
        y_hi, y_lo = sem("y_hi"), sem("y_lo")
        xa_in = [sem(f"xa_in{s}") for s in range(2)]
        xa_out = [sem(f"xa_out{s}") for s in range(2)]
        sgw_in, sgw_masked, sgw_tr, wt_ready = sem("sgw_in"), sem("sgw_masked"), sem("sgw_tr"), sem("wt_ready")
        v_turned, ssq_ready, rv_ready, vn_ready = sem("v_turned"), sem("ssq_ready"), sem("rv_ready"), sem("vn_ready")
        sg_filled, sg_out = sem("sg_filled"), sem("sg_out")
        x1_in = sem("x1_in")
        y_prod, conv_step, gate_step, vn_step = sem("y_prod"), sem("conv_step"), sem("gate_step"), sem("vn_step")
        start_step, rms_ln, q_zeroed = sem("start_step"), sem("rms_ln"), sem("q_zeroed")
        gz_exp, e_exp, arg_raw, sp_raw, sp_free = (sem(n) for n in ("gz_exp", "e_exp", "arg_raw", "sp_raw", "sp_free"))
        o_sum, const_step, sgb_in = sem("o_sum"), sem("const_step"), sem("sgb_in")
        qk_sq, qk_rs, qk_n = sem("qk_sq"), sem("qk_rs"), sem("qk_n")
        q_hi, q_lo, k_hi, k_lo, v_hi = (sem(n) for n in ("q_hi", "q_lo", "k_hi", "k_lo", "v_hi"))
        gz_neg, gz_ln, gz_ls, gz_sig, gz_ready = (sem(n) for n in ("gz_neg", "gz_ln", "gz_ls", "gz_sig", "gz_ready"))
        z_filled, z_copied, e_neg, e_ln = sem("z_filled"), sem("z_copied"), sem("e_neg"), sem("e_ln")
        sp_ready, sp_hi, sp_lo = sem("sp_ready"), sem("sp_hi"), sem("sp_lo")
        u_done, arg_ready, w_ready = sem("u_done"), sem("arg_ready"), sem("w_ready")
        p_hi, p_lo, pv_done = sem("p_hi"), sem("p_lo"), sem("pv_done")
        o_shifted, y_ready = sem("o_shifted"), sem("y_ready")
        y_saved = sem("y_saved")
        ys_in = [sem(f"ys_in{s}") for s in range(4)]
        xt_in = [sem(f"xt_in{s}") for s in range(2)]
        t_filled, t_out = sem("t_filled"), sem("t_out")
        stored = [sem(f"stored{s}") for s in range(2)]

        HALF = [slice(0, HT), slice(HT, T)]
        ROWS = [slice(0, DH), slice(DH, P)]
        SUMS_AT, TURN_AT, SPLIT_AT, O_AT = (7, 10, 13, 16), (21, 22), (3, 9, 15, 21), (5, 13, 17)
        DIAGONALS = sum(s["diagonal"] for s in steps)
        LOWERS = sum(not s["last"] for s in steps)

        def diagonal_no(a):
            return sum(s["diagonal"] for s in steps[:a + 1])

        def lower_no(a):
            return sum(not s["last"] for s in steps[:a + 1])

        CHAINS_LEN = [sum(s["chain"] == ci for s in steps) for ci in range(4)]

        def cols(w, at, n=P):
            return w[:, bass.ds(at, n)].rearrange("(k p) n -> p k n", p=P)

        W_AB, W_C, W_OC = w_in_ab[0], w_in_c[0], w_out_c[0]
        W_OA, W_OB = w_out_ab[0, 0:D, :], w_out_ab[0, D:2 * D, :]
        A_B, A_C, A_X, A_Z, B_U, B_V, B_Z = (D * i for i in range(7))

        block = ctx.enter_context(nc.Block())

        @block.sync
        def _(sp):
            def load_unit(u, w, at):
                src = cols(w, at if isinstance(at, int) else sp.snap(at))
                slot = u.base % 2
                sp.wait_ge(w_hi, (u - 1).v)
                sp.wait_ge(w_lo, (u - 1).v)
                sp.dma_start(raw[:, slot], src).then_inc(raw_in[slot], 16)

            for ch in range(NC):
                if ch >= 2:
                    sp.wait_ge(filled[1], ch - 1)
                sp.dma_start(raw[:, ch % 2], x[0, ch * P:(ch + 1) * P, :].rearrange("t (k n) -> t k n", n=P)
                             ).then_inc(raw_in[ch % 2], 16)
            for m in range(NADA0):
                if m < 2:
                    sp.wait_ge(filled[1], NC - 1 + m)
                    sp.dma_start(raw[:, m], cols(ada_w[0], m * P)).then_inc(raw_in[m], 16)
                else:
                    load_unit(Lin(m), ada_w[0], m * P)

            def group_a(i, layer, first_turn, first_block):
                u = Lin(U_A - 8, i, 8)
                for k, w_at in enumerate((A_C, A_X, A_Z, A_B)):
                    load_unit(u + 2 * k, W_AB, i * P + (w_at - P))
                    load_unit(u + (2 * k + 1), ada_w[layer],
                              i * (4 * P) + (first_block + k - 4 * (first_turn + 1)) * P)

            with sp.Fori(1, 3) as i:
                group_a(i, 0, 0, NADA0)
            with sp.Fori(3, NB + 1) as i:
                group_a(i, 1, 2, 0)

            def load_pairs(u0, w):
                with sp.Fori(0, NB // 2) as i:
                    for a in range(2):
                        load_unit(Lin(u0 + a, i, 2), w, i * (2 * P) + a * P)

            load_pairs(U_A2, W_OA)
            with sp.Fori(0, G // 2) as i:
                for a in range(6):
                    w_at = (B_V, B_U, B_Z)[a % 3]
                    load_unit(Lin(U_B + a, i, 6), W_AB, i * (2 * P) + (w_at + (a // 3) * P))
            load_pairs(U_B2, W_OB)
            with sp.Fori(0, NP) as i:
                for a in range(4):
                    load_unit(Lin(U_C + a, i, 4), W_C, i * P + a * D)
            load_pairs(U_D, W_OC)

        @block.tensor
        def _(pe):
            mm, turn = nc.tensor.matmul, nc.tensor.transpose

            def products(half, slot, H, L, ks, split_by=None, split_base=0):
                h, acc = HALF[half], PB[half][:]
                for k in ks:
                    if split_by is not None:
                        pe.wait_ge(split_by, split_base + k + 1)
                    mm(acc, wH[:, slot, k], H[:, k, h], start=k == 0, stop=False)
                    mm(acc, wH[:, slot, k], L[:, k, h], start=False, stop=False)
                    last = mm(acc, wL[:, slot, k], H[:, k, h], start=False, stop=k == NB - 1)
                return last

            def wait_split(u):
                pe.wait_ge(w_hi, (u + 1).v)
                pe.wait_ge(w_lo, (u + 1).v)

            def unit(u, n, H, L, split_by=None, split_base=0):
                wait_split(u)
                for half in range(2):
                    pe.wait_ge(emptied[half], n.v)
                    products(half, u.base % 2, H, L, range(NB), split_by, split_base).then_inc(filled[half], 1)

            def ada(u, m):
                wait_split(u)
                slot = u.base % 2
                acc = MB[:, bass.ds((m * 2).v, 2)]
                for k in range(NB):
                    mm(acc, wH[:, slot, k], cHL[:, k, :], start=k == 0, stop=False)
                    last = mm(acc, wL[:, slot, k], cHL[:, k, :], start=False, stop=k == NB - 1)
                last.then_inc(ada_done, 1)

            def channel_sums(layer):
                for k in range(NB):
                    for half in range(2):
                        pe.wait_ge(sq_ready, 2 * NB * layer + 2 * k + half + 1)
                        mm(CB[half][:], ones[:], sums_in[:, half], start=k == 0,
                           stop=k == NB - 1).then_inc(sum_done, 1)

            pe.wait_ge(consts, 1)
            pe.wait_ge(prm_in, 16 * 9)
            turn(ZB[0][:, 0:NPRM], prm_rows[0:NPRM, :], ident[0:NPRM, 0:NPRM]).then_inc(prm_tr, 1)
            for ch in range(NC):
                pe.wait_ge(raw_in[ch % 2], 16 * (ch // 2 + 1))
                for half in range(2):
                    if ch:
                        pe.wait_ge(emptied[half], ch)
                    for k in range(4):
                        last = turn(PB[half][:, k * P:(k + 1) * P], raw[:, ch % 2, 4 * half + k, :], ident[:])
                    last.then_inc(filled[half], 1)
            pe.wait_ge(consts, 2)
            channel_sums(0)
            pe.wait_ge(ca_ready, 1)
            for m in range(NADA0):
                ada(Lin(m), Lin(m))

            pe.wait_ge(mod_ready, 1)
            pe.wait_ge(hl_ready, NB)
            with pe.Fori(0, NB) as i:
                for k in range(4):
                    unit(Lin(U_A + 2 * k, i, 8), Lin(N_A + k, i, 4), hH, hL)
                    ada(Lin(U_A + 2 * k + 1, i, 8), Lin(NADA0 + k, i, 4))
            pe.wait_ge(y_lo, 2 * NB)
            with pe.Fori(0, NB // 2) as i:
                for a in range(2):
                    unit(Lin(U_A2 + a, i, 2), Lin(N_A2 + a, i, 2), yH, yL)
            pe.wait_ge(sgw_masked, 1)
            for g in range(G):
                last = turn(ZB[g // 4][:, (g % 4) * P:(g % 4 + 1) * P], vn[:, g, :], ident[:])
                if g % 4 == 3:
                    last.then_inc(sgw_tr, 1)
            pe.wait_ge(wt_ready, 2)

            with pe.Fori(0, G // 2) as i:
                for a in range(2):
                    u, n = Lin(U_B + 3 * a, i, 6), Lin(N_B + 3 * a, i, 6)
                    g = Lin(a, i, 2)
                    unit(u, n, hH, hL)
                    unit(u + 1, n + 1, hH, hL)
                    pe.wait_ge(emptied[0], (n + 1).v)
                    pe.wait_ge(emptied[1], (n + 1).v)
                    for half in range(2):
                        for q in range(4):
                            ch = 4 * half + q
                            last = turn(ZB[half][:, q * P:(q + 1) * P], vT[:, ch * P:(ch + 1) * P], ident[:])
                        last.then_inc(v_turned, 1)
                    unit(u + 2, n + 2, hH, hL)
                    pe.wait_ge(vn_ready, (g + 1).v)
                    for half in range(2):
                        for q in range(4):
                            ch = 4 * half + q
                            last = mm(CB[half][:, q * P:(q + 1) * P], vn[:, ch, :], WT[:, bass.ds(g.v, 1), :],
                                      start=True, stop=True)
                        last.then_inc(sg_filled, 1)
            pe.wait_ge(y_lo, 4 * NB)
            with pe.Fori(0, NB // 2) as i:
                for a in range(2):
                    unit(Lin(U_B2 + a, i, 2), Lin(N_B2 + a, i, 2), yH, yL)
            channel_sums(1)

            def part(p, hu, third):
                kind, half = hu // 2, hu % 2
                if third == 0:
                    if half == 0:
                        wait_split(p * 4 + (U_C + kind))
                    pe.wait_ge(emptied[half], (p * C_FILLS + (N_C + (0, 1, 3, 5)[kind])).v)
                last = products(half, kind % 2, hH, hL, ((0, 1, 2), (3, 4, 5), (6, 7))[third])
                if third == 2:
                    last.then_inc(filled[half], 1)

            def norm_sum(p, which, half):
                pe.wait_ge(emptied[half], (p * C_FILLS + (N_C + (2, 4)[which])).v)
                pe.wait_ge(qk_sq, (p * 4 + (2 * which + half + 1)).v)
                mm(PB[half][:], pair_ones[:], sums_in[:, half], start=True, stop=True).then_inc(filled[half], 1)

            def turn_v(p, half):
                pe.wait_ge(emptied[half], (p * C_FILLS + (N_C + 6)).v)
                for q in range(4):
                    ch = 4 * half + q
                    last = turn(PB[half][:, q * P:(q + 1) * P], qr[:, ch * P:(ch + 1) * P], ident[:])
                last.then_inc(filled[half], 1)

            def scores(b, par, a):
                s = steps[a]
                if a >= 2:
                    pe.wait_ge(z_copied, (b * STEPS + (a - 1)).v)
                keys = slice(s["j"] * P, (s["j"] + 1) * P)
                qs = slice(s["half"] * HT + s["c0"], (s["half"] + 1) * HT)
                o = ZB[a % 2][:, s["c0"]:HT]
                (qh, ql), (kh, kl) = Q[par][s["head"]], K[par]
                mm(o, kh[:, keys], qh[:, qs], start=True, stop=False)
                mm(o, kh[:, keys], ql[:, qs], start=False, stop=False)
                mm(o, kl[:, keys], qh[:, qs], start=False, stop=True).then_inc(z_filled, 1)

            def suffix(b, a, upper):
                s = steps[a]
                if upper:
                    pe.wait_ge(sp_lo, (b * STEPS + (a + 1)).v)
                else:
                    pe.wait_ge(arg_ready, (b * STEPS + (a + 1)).v)
                o, w = CB[s["chain"] % 2][:, s["c0"]:HT], U_r if upper else Uc_r
                mm(o, w[:], spH[:, a % 2, s["c0"]:HT], start=upper and s["first"], stop=False, skip_group_check=True)
                mm(o, w[:], spL[:, a % 2, s["c0"]:HT], start=False, stop=upper and s["last"],
                   skip_group_check=True).then_inc(u_done if upper else sp_free, 1)

            def weighted_v(b, par, a):
                s = steps[a]
                pe.wait_ge(p_lo, (b * STEPS + (a + 1)).v)
                o, w = OB[s["chain"] % 2][:, s["c0"]:HT], V[par][:, s["j"], s["head"], :]
                mm(o, w, pH[:, s["c0"]:HT], start=s["first"], stop=False, skip_group_check=True)
                mm(o, w, pL[:, s["c0"]:HT], start=False, stop=s["last"],
                   skip_group_check=True).then_inc(pv_done, 1)

            def pair(p, par, project, attend):
                b = p - 1
                if attend:
                    pe.wait_ge(q_lo, (b * 4 + 4).v)
                    pe.wait_ge(k_lo, (b * 2 + 2).v)
                    pe.wait_ge(emptied[0], (b * C_FILLS + (N_C + C_FILLS)).v)
                    pe.wait_ge(emptied[1], (b * C_FILLS + (N_C + C_FILLS)).v)
                    scores(b, 1 - par, 0)
                    scores(b, 1 - par, 1)
                parts = [(hu, third) for hu in range(8) for third in range(3)]
                if project:
                    for hu, third in parts[:3]:
                        part(p, hu, third)
                for t in range(STEPS):
                    if attend:
                        suffix(b, t, True)
                        if t + 2 < STEPS:
                            scores(b, 1 - par, t + 2)
                    if project:
                        if t + 3 < len(parts):
                            part(p, *parts[t + 3])
                        if t in SUMS_AT:
                            norm_sum(p, *divmod(SUMS_AT.index(t), 2))
                        if t in TURN_AT:
                            turn_v(p, TURN_AT.index(t))
                    if attend:
                        if not steps[t]["last"]:
                            suffix(b, t, False)
                        if t:
                            weighted_v(b, 1 - par, t - 1)
                if attend:
                    weighted_v(b, 1 - par, STEPS - 1)

            pe.wait_ge(hl_ready, 2 * NB)
            pair(Lin(0), 0, True, False)
            pe.wait_ge(q_zeroed, 1)
            with pe.Fori(0, NP // 2 - 1) as i:
                pair(Lin(1, i, 2), 1, True, True)
                pair(Lin(2, i, 2), 0, True, True)
            pair(Lin(NP - 1), 1, True, True)
            pair(Lin(NP), 0, False, True)

            def turn_out(j):
                for half in range(2):
                    pe.wait_ge(emptied[half], (j + (N_D + 1)).v)
                for half in range(2):
                    if j.coef or j.base:
                        pe.wait_ge(t_out, (j * 2 + (half - 1)).v)
                    for q in range(4):
                        ch = 4 * half + q
                        last = turn(ZB[half][:, q * P:(q + 1) * P], xt[j.base % 2][:, ch * P:(ch + 1) * P], ident[:])
                    last.then_inc(t_filled, 1)

            unit(Lin(U_D), Lin(N_D), hH, hL, hl_ready, 2 * NB)
            unit(Lin(U_D + 1), Lin(N_D + 1), hH, hL)
            turn_out(Lin(0))
            with pe.Fori(1, NB // 2) as i:
                unit(Lin(U_D, i, 2), Lin(N_D, i, 2), hH, hL)
                turn_out(Lin(-1, i, 2))
                unit(Lin(U_D + 1, i, 2), Lin(N_D + 1, i, 2), hH, hL)
                turn_out(Lin(0, i, 2))
            turn_out(Lin(NB - 1))

        @block.scalar
        def _(act):
            f = nc.scalar.activation

            def copy(o, i):
                return nc.scalar.activation(o, i, ACT.Copy)

            def split_hi(u):
                slot = u.base % 2
                act.wait_ge(raw_in[slot], (u.half() * 16 + 16 * (NC // 2 + 1)).v)
                copy(wH[:, slot], raw[:, slot]).then_inc(w_hi, 1)

            def unit_done(n):
                act.wait_ge(filled[1], (n + 1).v)

            nc.scalar.preload_act_table_set(LN_EXP_SET)
            act.wait_ge(prm_ready, 1)
            f(ca[:, 0, :], prm[:, C_C:C_C + NB], ACT.Exp, scale=-1.0).then_inc(ce, 1)
            for ch in range(NC):
                act.wait_ge(filled[1], ch + 1)
                copy(xT[:, 4:8, ch * P:(ch + 1) * P], PB[1][:].rearrange("p (k t) -> p k t", k=4)
                     ).then_inc(emptied[1], 1)

            def rms_of_x(layer):
                for k in range(NB):
                    for half in range(2):
                        if k:
                            act.wait_ge(sum_done, 2 * NB * layer + 2 * (k - 1) + half + 1)
                        f(sums_in[:, half], xT[:, k, HALF[half]], ACT.Square).then_inc(sq_ready, 1)
                for half in range(2):
                    act.wait_ge(sum_done, 2 * NB * layer + 2 * NB - 1 + half)
                    f(sums_in[:, half], CB[half][:], ACT.Ln, bias=eps_t[:], scale=1.0 / D).then_inc(rms_ln, 1)
                    act.wait_ge(rms_ln, 2 * layer + half + 1)
                    f(sums_in[:, half], sums_in[:, half], ACT.Exp, scale=-0.5).then_inc(rs_ready, 1)

            def h_hi(layer):
                for k in range(NB):
                    act.wait_ge(ht_ready, NB * layer + k + 1)
                    at = 3 * NB * layer + k
                    f(hH[:, k], xT[:, k], ACT.Identity, bias=mod[:, at:at + 1]).then_inc(hh_ready, 1)

            act.wait_ge(emptied[0], NC)
            act.wait_ge(emptied[1], NC)
            act.wait_ge(consts, 2)
            rms_of_x(0)
            for m in range(NADA0):
                if m >= 2:
                    act.wait_ge(ada_done, m - 1)
                split_hi(Lin(m))
            nc.scalar.preload_act_table_set(SILU_SET)
            h_hi(0)
            for m in range(2):
                act.wait_ge(ada_done, NADA0 - 1 + m)
                split_hi(Lin(U_A + m))

            with act.Fori(0, NB) as i:
                u, n = Lin(U_A, i, 8), Lin(N_A, i, 4)

                def ada_split(k):
                    act.wait_ge(ada_done, Lin(NADA0 + k + 1, i, 4).v)
                    split_hi(u + (2 * k + 3))

                for half in range(2):
                    act.wait_ge(filled[half], (n + 1).v)
                    copy(cs[:, HALF[half]], PB[half][:]).then_inc(emptied[half], 1)
                split_hi(u + 2)
                ada_split(0)
                unit_done(n + 1)
                split_hi(u + 4)
                ada_split(1)
                for half in range(2):
                    act.wait_ge(filled[half], (n + 3).v)
                    f(sz[:, HALF[half]], PB[half][:], ACT.Silu).then_inc(emptied[half], 1)
                split_hi(u + 6)
                ada_split(2)
                unit_done(n + 3)
                split_hi(u + 8)
                for half in range(2):
                    act.wait_ge(emptied[half], (n + 4).v)
                    copy(yH[:, bass.ds(i, 1), HALF[half]], cv[:, HALF[half]]).then_inc(y_hi, 1)
                ada_split(3)
            with act.Fori(0, NB // 2) as i:
                for a in range(2):
                    unit_done(Lin(N_A2 + a, i, 2))
                    split_hi(Lin(U_A2 + a + 2, i, 2))
            with act.Fori(0, G // 2) as i:
                for a in range(2):
                    u, n = Lin(U_B + 3 * a, i, 6), Lin(N_B + 3 * a, i, 6)
                    for half in range(2):
                        act.wait_ge(filled[half], (n + 1).v)
                        copy(vT[:, HALF[half]], PB[half][:]).then_inc(emptied[half], 1)
                    split_hi(u + 2)
                    unit_done(n + 1)
                    split_hi(u + 3)
                    for half in range(2):
                        act.wait_ge(filled[half], (n + 3).v)
                        f(sz[:, HALF[half]], PB[half][:], ACT.Silu).then_inc(emptied[half], 1)
                    split_hi(u + 4)
                    for half in range(2):
                        act.wait_ge(y_prod, Lin(2 * a + half + 1, i, 4).v)
                        copy(yH[:, bass.ds(Lin(a, i, 2).v, 1), HALF[half]], cv[:, HALF[half]]).then_inc(y_hi, 1)
            with act.Fori(0, NB // 2) as i:
                for a in range(2):
                    unit_done(Lin(N_B2 + a, i, 2))
                    split_hi(Lin(U_B2 + a + 2, i, 2))
            nc.scalar.preload_act_table_set(LN_EXP_SET)
            act.wait_ge(emptied[0], N_C)
            act.wait_ge(emptied[1], N_C)
            rms_of_x(1)
            h_hi(1)
            act.wait_ge(y_saved, 16)

            def z_copy(b, a):
                s = steps[a]
                act.wait_ge(z_filled, (b * STEPS + (a + 1)).v)
                if a >= 3:
                    act.wait_ge(p_lo, (b * STEPS + (a - 2)).v)
                copy(zs[a % 3][:, s["c0"]:HT], ZB[a % 2][:, s["c0"]:HT]).then_inc(z_copied, 1)

            def ln_exp(b, a):
                v = e[a % 2][:, steps[a]["c0"]:HT]
                act.wait_ge(e_neg, (b * STEPS + (a + 1)).v)
                f(v, v, ACT.Exp).then_inc(e_exp, 1)
                act.wait_ge(e_exp, (b * STEPS + (a + 1)).v)
                f(v, v, ACT.Ln, bias=1.0).then_inc(e_ln, 1)

            def weight(b, a):
                v = zs[a % 3][:, steps[a]["c0"]:HT]
                act.wait_ge(arg_ready, (b * STEPS + (a + 1)).v)
                f(v, v, ACT.Exp).then_inc(w_ready, 1)

            def o_shift(b, ci):
                act.wait_ge(pv_done, (b * STEPS + sum(CHAINS_LEN[:ci + 1])).v)
                mine, other = ROWS[chains[ci][0]], ROWS[1 - chains[ci][0]]
                copy(osh[mine, :], OB[ci % 2][other, :]).then_inc(o_shifted, 1)

            def pair(p, par, project, attend):
                b = p - 1
                n = p * C_FILLS + N_C
                if attend:
                    z_copy(b, 0)
                    z_copy(b, 1)
                    ln_exp(b, 0)
                for t in range(STEPS):
                    if attend:
                        if t + 1 < STEPS:
                            ln_exp(b, t + 1)
                        weight(b, t)
                        if t + 2 < STEPS:
                            z_copy(b, t + 2)
                        if t in O_AT:
                            o_shift(b, O_AT.index(t))
                    if not project:
                        continue
                    if t in (0, 3):
                        half = (0, 3).index(t)
                        act.wait_ge(filled[half], (n + 1).v)
                        if p.coef or p.base:
                            act.wait_ge(gz_ready, (p * 2 + (half - 1)).v)
                        f(sums_in[:, half], PB[half][:], ACT.Square).then_inc(qk_sq, 1)
                        copy(qr[:, HALF[half]], PB[half][:]).then_inc(emptied[half], 1)
                    if t in (6, 9):
                        half = (6, 9).index(t)
                        act.wait_ge(filled[half], (n + 2).v)
                        copy(kr[:, HALF[half]], PB[half][:]).then_inc(emptied[half], 1)
                    if t in (8, 11, 14, 17):
                        which, half = divmod((8, 11, 14, 17).index(t), 2)
                        act.wait_ge(filled[half], (n + (3, 5)[which]).v)
                        f(sums_in[:, half], PB[half][:], ACT.Ln, bias=eps_t[:], scale=1.0 / DH
                          ).then_inc(emptied[half], 1)
                        act.wait_ge(emptied[half], (n + (3, 5)[which]).v)
                        f(sums_in[:, half], sums_in[:, half], ACT.Exp, scale=-0.5).then_inc(qk_rs, 1)
                    if t in (10, 13):
                        half = (10, 13).index(t)
                        act.wait_ge(qk_n, (p * 4 + (half + 1)).v)
                        act.wait_ge(emptied[half], (n + 2).v)
                        f(sums_in[:, half], kr[:, HALF[half]], ACT.Square).then_inc(qk_sq, 1)
                    if t in (12, 15):
                        half = (12, 15).index(t)
                        act.wait_ge(filled[half], (n + 4).v)
                        act.wait_ge(q_lo, (p * 4 + (2 * half + 2)).v)
                        copy(qr[:, HALF[half]], PB[half][:]).then_inc(emptied[half], 1)
                    if t in (18, 21):
                        half = (18, 21).index(t)
                        act.wait_ge(filled[half], (n + 6).v)
                        if p.coef or p.base > 1:
                            act.wait_ge(y_saved, (p * 16).v)
                        copy(gz[par][:, HALF[half]], PB[half][:]).then_inc(emptied[half], 1)
                    if t in (20, 22):
                        half = (20, 22).index(t)
                        act.wait_ge(gz_neg, (p * 2 + (half + 1)).v)
                        f(sums_in[:, half], sums_in[:, half], ACT.Exp).then_inc(gz_exp, 1)
                        act.wait_ge(gz_exp, (p * 2 + (half + 1)).v)
                        f(sums_in[:, half], sums_in[:, half], ACT.Ln, bias=1.0).then_inc(gz_ln, 1)
                    if t in (22, 23):
                        half = (22, 23).index(t)
                        act.wait_ge(gz_ls, (p * 2 + (half + 1)).v)
                        f(sums_in[:, half], sums_in[:, half], ACT.Exp).then_inc(gz_sig, 1)
                    if t in (22, 23):
                        half = (22, 23).index(t)
                        act.wait_ge(filled[half], (n + 7).v)
                        src = PB[half][:].rearrange("p (j h d) -> p j h d", j=4, h=2)
                        blocks = slice(4 * half, 4 * half + 4)
                        copy(V[par][:, blocks, 0, 0:DH], src[:, :, 0, :])
                        copy(V[par][:, blocks, 1, DH:P], src[:, :, 1, :]).then_inc(v_hi, 1)
                    if t in SPLIT_AT:
                        kind = SPLIT_AT.index(t)
                        unit_done(n + (0, 1, 3, 5)[kind])
                        split_hi(p * 4 + (U_C + kind + 2))
                if attend:
                    o_shift(b, 3)

            pair(Lin(0), 0, True, False)
            with act.Fori(0, NP // 2 - 1) as i:
                pair(Lin(1, i, 2), 1, True, True)
                pair(Lin(2, i, 2), 0, True, True)
            pair(Lin(NP - 1), 1, True, True)
            pair(Lin(NP), 0, False, True)

            for k in range(NP):
                act.wait_ge(ys_in[k % 4], 16 * (k // 4 + 1))
                copy(hH[:, k], ys[:, k % 4]).then_inc(hh_ready, 1)

            def copy_out(j):
                if j.coef or j.base > 1:
                    act.wait_ge(stored[j.base % 2], (j.half() * 16).v)
                for half in range(2):
                    act.wait_ge(t_filled, (j * 2 + (half + 1)).v)
                    copy(ot[j.base % 2][:, 4 * half:4 * half + 4, :],
                         ZB[half][:].rearrange("p (c d) -> p c d", c=4)).then_inc(t_out, 1)

            unit_done(Lin(N_D))
            split_hi(Lin(U_D + 2))
            unit_done(Lin(N_D + 1))
            split_hi(Lin(U_D + 3))
            copy_out(Lin(0))
            unit_done(Lin(N_D + 2))
            split_hi(Lin(U_D + 4))
            copy_out(Lin(1))
            unit_done(Lin(N_D + 3))
            split_hi(Lin(U_D + 5))
            copy_out(Lin(2))
            unit_done(Lin(N_D + 4))
            split_hi(Lin(U_D + 6))
            copy_out(Lin(3))
            unit_done(Lin(N_D + 5))
            split_hi(Lin(U_D + 7))
            for j in range(4, NB):
                copy_out(Lin(j))

        @block.vector
        def _(dve):
            tt, ts, stt, copy = (nc.vector.tensor_tensor, nc.vector.tensor_scalar,
                                 nc.vector.scalar_tensor_tensor, nc.vector.tensor_copy)

            def f32(ap):
                return ap.bitcast(F32)

            def split_lo(u):
                slot = u.base % 2
                dve.wait_ge(w_hi, (u + 1).v)
                tt(wL[:, slot], raw[:, slot], f32(wH[:, slot]), ALU.subtract).then_inc(w_lo, 1)

            for o, i, value in ((0, 0, 1.0), (0, 1, 0.0), (1, 0, 0.0), (1, 1, 1.0)):
                nc.vector.memset(pair_ones[ROWS[o], ROWS[i]], value)
            dve.wait_ge(consts, 2)
            copy(U_r[:], U_f[:]).then_inc(start_step, 1)
            ts(Uc_r[:], U_f[:], -1.0, 1.0, ALU.mult, ALU.add).then_inc(start_step, 1)
            dve.wait_ge(prm_tr, 1)
            copy(prm[:, 0:NPRM], ZB[0][:, 0:NPRM]).then_inc(prm_ready, 1)
            dve.wait_ge(prm_ready, 1)
            ts(qn_scaled[:], prm[:, C_QN:C_QN + 1], float(DH) ** -0.5, None, ALU.mult).then_inc(start_step, 1)
            for ch in range(NC):
                dve.wait_ge(filled[0], ch + 1)
                copy(xT[:, 0:4, ch * P:(ch + 1) * P], PB[0][:].rearrange("p (k t) -> p k t", k=4)
                     ).then_inc(emptied[0], 1)
            dve.wait_ge(ce, 1)
            ts(ca[:, 1, :], ca[:, 0, :], 1.0, None, ALU.add).then_inc(start_step, 1)
            dve.wait_ge(start_step, 4)
            nc.vector.reciprocal(ca[:, 2, :], ca[:, 1, :]).then_inc(start_step, 1)
            dve.wait_ge(start_step, 5)
            tt(ca[:, 0, :], ca[:, 2, :], prm[:, C_C:C_C + NB], ALU.mult).then_inc(start_step, 1)
            dve.wait_ge(start_step, 6)
            copy(cHL[:, :, 0], ca[:, 0, :]).then_inc(start_step, 1)
            dve.wait_ge(start_step, 7)
            tt(cHL[:, :, 1], ca[:, 0, :], f32(cHL[:, :, 0]), ALU.subtract).then_inc(ca_ready, 1)
            for m in range(NADA0):
                split_lo(Lin(m))

            def modulation(lo, hi, steps_before):
                M2 = MB[:, 2 * lo:2 * hi].rearrange("p (m two) -> p m two", two=2)
                dve.wait_ge(ada_done, hi)
                tt(mod[:, lo:hi], M2[:, :, 0], prm[:, C_ADA + lo:C_ADA + hi], ALU.add).then_inc(start_step, 1)
                dve.wait_ge(start_step, steps_before + 1)
                tt(mod[:, lo:hi], M2[:, :, 1], mod[:, lo:hi], ALU.add).then_inc(mod_ready, 1)

            def norm_gain(layer, ready):
                dve.wait_ge(mod_ready, ready)
                at = 3 * NB * layer + NB
                stt(gs[:, NB * layer:NB * layer + NB], mod[:, at:at + NB], 1.0,
                    prm[:, C_LN + NB * layer:C_LN + NB * layer + NB], ALU.add, ALU.mult).then_inc(start_step, 1)

            def h_of_x(layer, saved, steps_before):
                dve.wait_ge(start_step, steps_before)
                dve.wait_ge(rs_ready, 2 * layer + 2)
                dve.wait_ge(saved, 16)
                rs = sums_in[:].rearrange("p a t -> p (a t)")

                def lo(k):
                    dve.wait_ge(hh_ready, NB * layer + k + 1)
                    at = 3 * NB * layer + k
                    stt(hL[:, k], xT[:, k], mod[:, at:at + 1], f32(hH[:, k]), ALU.add, ALU.subtract
                        ).then_inc(hl_ready, 1)

                for k in range(NB):
                    at = NB * layer + k
                    stt(xT[:, k], xT[:, k], gs[:, at:at + 1], rs, ALU.mult, ALU.mult).then_inc(ht_ready, 1)
                    if k:
                        lo(k - 1)
                lo(NB - 1)

            modulation(0, NADA0, 7)
            norm_gain(0, 1)
            h_of_x(0, x_saved, 9)
            split_lo(Lin(U_A))
            split_lo(Lin(U_A + 1))
            nc.vector.memset(cx[:, 0:2], 0.0).then_inc(start_step, 1)
            dve.wait_ge(start_step, 10)

            with dve.Fori(0, NB) as i:
                u, n = Lin(U_A, i, 8), Lin(N_A, i, 4)

                def conv_done(k):
                    dve.wait_ge(conv_step, Lin(k, i, 4).v)

                def tap(w):
                    return prm[:, bass.ds(Lin(C_CONV + w * NB, i, 1).v, 1)]

                split_lo(u + 2)
                split_lo(u + 3)
                for half in range(2):
                    dve.wait_ge(filled[half], (n + 2).v)
                    tt(cx[:, 2 + half * HT:2 + (half + 1) * HT], cs[:, HALF[half]], PB[half][:], ALU.mult
                       ).then_inc(emptied[half], 1)
                split_lo(u + 4)
                dve.wait_ge(emptied[0], (n + 2).v)
                dve.wait_ge(emptied[1], (n + 2).v)
                ts(cv[:], cx[:, 0:T], tap(0), None, ALU.mult).then_inc(conv_step, 1)
                conv_done(1)
                stt(cv[:], cx[:, 1:T + 1], tap(1), cv[:], ALU.mult, ALU.add).then_inc(conv_step, 1)
                conv_done(2)
                stt(cv[:], cx[:, 2:T + 2], tap(2), cv[:], ALU.mult, ALU.add).then_inc(conv_step, 1)
                split_lo(u + 5)
                dve.wait_ge(emptied[0], (n + 3).v)
                dve.wait_ge(emptied[1], (n + 3).v)
                conv_done(3)
                tt(cv[:], cv[:], sz[:], ALU.mult).then_inc(conv_step, 1)
                split_lo(u + 6)
                split_lo(u + 7)
                conv_done(4)
                for half in range(2):
                    dve.wait_ge(filled[half], (n + 4).v)
                    tt(cv[:, HALF[half]], cv[:, HALF[half]], PB[half][:], ALU.mult).then_inc(emptied[half], 1)
                split_lo(u + 8)
                for half in range(2):
                    dve.wait_ge(y_hi, Lin(half + 1, i, 2).v)
                    tt(yL[:, bass.ds(i, 1), HALF[half]], cv[:, HALF[half]], f32(yH[:, bass.ds(i, 1), HALF[half]]),
                       ALU.subtract).then_inc(y_lo, 1)
                split_lo(u + 9)
            modulation(NADA0, NADA, 10)
            norm_gain(1, 2)

            def residual(j, n, dst, gate, loaded):
                for half in range(2):
                    dve.wait_ge(filled[half], (n + 1).v)
                    if half == 0:
                        loaded()
                    d = dst(HALF[half])
                    stt(d, PB[half][:], gate, d, ALU.mult, ALU.add).then_inc(emptied[half], 1)

            def mod_col(base, i, coef):
                return mod[:, bass.ds(Lin(base, i, coef).v, 1)]

            dve.wait_ge(mod_ready, 2)
            with dve.Fori(0, NB // 2) as i:
                for a in range(2):
                    residual(None, Lin(N_A2 + a, i, 2), lambda h, a=a: xa[a][:, h], mod_col(2 * NB + a, i, 2),
                             lambda a=a: dve.wait_ge(xa_in[a], Lin(16, i, 16).v))
                    split_lo(Lin(U_A2 + a + 2, i, 2))
            for half in range(2):
                dve.wait_ge(sgw_tr, half + 1)
                copy(WT[:, 4 * half:4 * half + 4, :], ZB[half][:].rearrange("p (g t) -> p g t", g=4)
                     ).then_inc(wt_ready, 1)
            dve.wait_ge(sgb_in, 16)
            for a in range(2):
                dve.wait_ge(xa_out[a], 16 * (NB // 2))

            with dve.Fori(0, G // 2) as i:
                for a in range(2):
                    u, n = Lin(U_B + 3 * a, i, 6), Lin(N_B + 3 * a, i, 6)
                    g = Lin(a, i, 2)
                    split_lo(u + 2)
                    for half in range(2):
                        dve.wait_ge(filled[half], (n + 2).v)
                        copy(us[:, HALF[half]], PB[half][:]).then_inc(emptied[half], 1)
                    split_lo(u + 3)
                    for half in range(2):
                        dve.wait_ge(v_turned, (g * 2 + (half + 1)).v)
                        copy(vn[:, 4 * half:4 * half + 4, :], ZB[half][:].rearrange("p (c d) -> p c d", c=4)
                             ).then_inc(vn_step, 1)
                    sq = vT[:].rearrange("p (c d) -> p c d", c=NC)
                    dve.wait_ge(vn_step, (g * 4 + 2).v)
                    tt(sq, vn[:], vn[:], ALU.mult).then_inc(vn_step, 1)
                    dve.wait_ge(vn_step, (g * 4 + 3).v)
                    nc.vector.tensor_reduce(ssq[:], sq, AX_X, ALU.add).then_inc(vn_step, 1)
                    dve.wait_ge(vn_step, (g * 4 + 4).v)
                    ts(ssq[:], ssq[:], 1.0 / P, EPS, ALU.mult, ALU.add).then_inc(ssq_ready, 1)
                    dve.wait_ge(rv_ready, (g + 1).v)
                    tt(vn[:], vn[:], rv[:].rearrange("p (c o) -> p c o", o=1).broadcast_to([P, NC, P]), ALU.mult
                       ).then_inc(vn_ready, 1)
                    dve.wait_ge(filled[1], (n + 3).v)
                    split_lo(u + 4)
                    for half in range(2):
                        dve.wait_ge(emptied[half], (n + 3).v)
                        tt(us[:, HALF[half]], us[:, HALF[half]], sz[:, HALF[half]], ALU.mult).then_inc(gate_step, 1)
                    for half in range(2):
                        dve.wait_ge(sg_filled, (g * 2 + (half + 1)).v)
                        v4 = cv[:, HALF[half]].rearrange("p (c t) -> p c t", c=4)
                        stt(v4, CB[half][:].rearrange("p (c t) -> p c t", c=4),
                            prm[:, bass.ds((g + C_SGN).v, 1)],
                            sgb[:, bass.ds(g.v, 1), :].broadcast_to([P, 4, P]), ALU.mult, ALU.add).then_inc(gate_step, 1)
                    for half in range(2):
                        dve.wait_ge(gate_step, (g * 4 + (half + 3)).v)
                        tt(cv[:, HALF[half]], cv[:, HALF[half]], us[:, HALF[half]], ALU.mult).then_inc(y_prod, 1)
                    for half in range(2):
                        dve.wait_ge(y_hi, (g * 2 + (2 * NB + half + 1)).v)
                        tt(yL[:, bass.ds(g.v, 1), HALF[half]], cv[:, HALF[half]],
                           f32(yH[:, bass.ds(g.v, 1), HALF[half]]), ALU.subtract).then_inc(y_lo, 1)
            dve.wait_ge(x1_in, 16)
            with dve.Fori(0, NB // 2) as i:
                for a in range(2):
                    residual(None, Lin(N_B2 + a, i, 2),
                             lambda h, a=a: xT[:, bass.ds(Lin(a, i, 2).v, 1), h], mod_col(2 * NB + a, i, 2),
                             lambda: None)
                    split_lo(Lin(U_B2 + a + 2, i, 2))
            for par in range(2):
                for head in range(2):
                    for prt in range(2):
                        last = nc.vector.memset(Q[par][head][prt][ROWS[1 - head], :].bitcast(F32), 0.0)
            last.then_inc(q_zeroed, 1)
            h_of_x(1, y_saved, 12)

            def negated(b, a):
                s = steps[a]
                dve.wait_ge(z_copied, (b * STEPS + (a + 1)).v)
                if a >= 2:
                    dve.wait_ge(sp_lo, (b * STEPS + (a - 1)).v)
                ts(e[a % 2][:, s["c0"]:HT].bitcast(U32), zs[a % 3][:, s["c0"]:HT].bitcast(U32), SIGN, None,
                   ALU.bitwise_or).then_inc(e_neg, 1)

            def softplus(b, a):
                s = steps[a]
                v = e[a % 2][:, s["c0"]:HT]
                dve.wait_ge(e_ln, (b * STEPS + (a + 1)).v)
                stt(v, zs[a % 3][:, s["c0"]:HT], 0.0, v, ALU.max, ALU.add
                    ).then_inc(sp_raw if s["diagonal"] else sp_ready, 1)
                if s["diagonal"]:
                    dve.wait_ge(sp_raw, (b * DIAGONALS + diagonal_no(a)).v)
                    d = e[a % 2][:, s["c0"]:s["c0"] + P]
                    tt(d, d, strict[:], ALU.mult).then_inc(sp_ready, 1)
                dve.wait_ge(sp_ready, (b * STEPS + (a + 1)).v)
                if a >= 2:
                    if steps[a - 2]["last"]:
                        dve.wait_ge(u_done, (b * STEPS + (a - 1)).v)
                    else:
                        dve.wait_ge(sp_free, (b * LOWERS + lower_no(a - 2)).v)
                copy(spH[:, a % 2, s["c0"]:HT], v).then_inc(sp_hi, 1)

            def exponent(b, a):
                s = steps[a]
                v = zs[a % 3][:, s["c0"]:HT]
                dve.wait_ge(u_done, (b * STEPS + (a + 1)).v)
                tt(v, v, CB[s["chain"] % 2][:, s["c0"]:HT], ALU.subtract
                   ).then_inc(arg_raw if s["diagonal"] else arg_ready, 1)
                if s["diagonal"]:
                    dve.wait_ge(arg_raw, (b * DIAGONALS + diagonal_no(a)).v)
                    d = zs[a % 3][:, s["c0"]:s["c0"] + P]
                    tt(d, d, cap[:], ALU.min).then_inc(arg_ready, 1)

            def weights(b, a):
                s = steps[a]
                v = zs[a % 3][:, s["c0"]:HT]
                dve.wait_ge(w_ready, (b * STEPS + (a + 1)).v)
                if a:
                    dve.wait_ge(pv_done, (b * STEPS + a).v)
                copy(pH[:, s["c0"]:HT], v).then_inc(p_hi, 1)
                dve.wait_ge(p_hi, (b * STEPS + (a + 1)).v)
                tt(pL[:, s["c0"]:HT], v, f32(pH[:, s["c0"]:HT]), ALU.subtract).then_inc(p_lo, 1)

            def gated(b, ci, par):
                mine, half = ROWS[chains[ci][0]], chains[ci][1]
                dve.wait_ge(o_shifted, (b * 4 + (ci + 1)).v)
                tt(osh[mine, :], OB[ci % 2][mine, :], osh[mine, :], ALU.add).then_inc(o_sum, 1)
                dve.wait_ge(o_sum, (b * 4 + (ci + 1)).v)
                if ci == 0:
                    dve.wait_ge(gz_ready, (b * 2 + 2).v)
                d = gz[par][mine, HALF[half]]
                tt(d, d, osh[mine, :], ALU.mult).then_inc(y_ready, 1)

            def pair(p, par, project, attend):
                b = p - 1
                n = p * C_FILLS + N_C
                if attend:
                    negated(b, 0)
                    negated(b, 1)
                    softplus(b, 0)
                for t in range(STEPS):
                    if attend:
                        exponent(b, t)
                        if t in O_AT:
                            gated(b, O_AT.index(t), 1 - par)
                    if project and t in (9, 12, 15, 18):
                        which, half = divmod((9, 12, 15, 18).index(t), 2)
                        h = HALF[half]
                        r = (qr, kr)[which]
                        gain = (qn_scaled[:], prm[:, C_KN:C_KN + 1])[which]
                        dve.wait_ge(qk_rs, (p * 4 + (2 * which + half + 1)).v)
                        stt(r[:, h], r[:, h], gain, sums_in[:, half], ALU.mult, ALU.mult).then_inc(qk_n, 1)
                        dve.wait_ge(qk_n, (p * 4 + (2 * which + half + 1)).v)
                        if which == 0:
                            for head in range(2):
                                copy(Q[par][head][0][ROWS[head], h], r[ROWS[head], h]).then_inc(q_hi, 1)
                            for head in range(2):
                                dve.wait_ge(q_hi, (p * 4 + (2 * half + head + 1)).v)
                                tt(Q[par][head][1][ROWS[head], h], r[ROWS[head], h],
                                   f32(Q[par][head][0][ROWS[head], h]), ALU.subtract).then_inc(q_lo, 1)
                        else:
                            copy(K[par][0][:, h], r[:, h]).then_inc(k_hi, 1)
                    if project and t == 21:
                        log_sigmoid(p, par, 0)
                    if project and t in (19, 21):
                        half = (19, 21).index(t)
                        dve.wait_ge(emptied[half], (n + 6).v)
                        ts(sums_in[:, half].bitcast(U32), gz[par][:, HALF[half]].bitcast(U32), SIGN, None,
                           ALU.bitwise_or).then_inc(gz_neg, 1)
                    if project and t == 22:
                        log_sigmoid(p, par, 1)
                    if project and t in (22, 23):
                        half = (22, 23).index(t)
                        dve.wait_ge(v_hi, (p * 2 + (half + 1)).v)
                        src = PB[half][:].rearrange("p (j h d) -> p j h d", j=4, h=2)
                        blocks = slice(4 * half, 4 * half + 4)
                        tt(V[par][:, blocks, 0, DH:P], src[:, :, 0, :], f32(V[par][:, blocks, 0, 0:DH]), ALU.subtract)
                        tt(V[par][:, blocks, 1, 0:DH], src[:, :, 1, :], f32(V[par][:, blocks, 1, DH:P]), ALU.subtract
                           ).then_inc(emptied[half], 1)
                    if attend:
                        weights(b, t)
                        if t + 1 < STEPS:
                            softplus(b, t + 1)
                        if t + 2 < STEPS:
                            negated(b, t + 2)
                if project:
                    for half in range(2):
                        d = gz[par][:, HALF[half]]
                        dve.wait_ge(gz_sig, (p * 2 + (half + 1)).v)
                        tt(d, d, sums_in[:, half], ALU.mult).then_inc(gz_ready, 1)
                if attend:
                    gated(b, 3, 1 - par)

            def log_sigmoid(p, par, half):
                v = sums_in[:, half]
                dve.wait_ge(gz_ln, (p * 2 + (half + 1)).v)
                stt(v, gz[par][:, HALF[half]], 0.0, v, ALU.min, ALU.subtract).then_inc(gz_ls, 1)

            pair(Lin(0), 0, True, False)
            with dve.Fori(0, NP // 2 - 1) as i:
                pair(Lin(1, i, 2), 1, True, True)
                pair(Lin(2, i, 2), 0, True, True)
            pair(Lin(NP - 1), 1, True, True)
            pair(Lin(NP), 0, False, True)

            for k in range(NP):
                dve.wait_ge(hh_ready, 2 * NB + k + 1)
                tt(hL[:, k], ys[:, k % 4], f32(hH[:, k]), ALU.subtract).then_inc(hl_ready, 1)
            for j in range(NB):
                residual(None, Lin(N_D + j), lambda h, j=j: xt[j % 2][:, h], mod[:, 5 * NB + j:5 * NB + j + 1],
                         lambda j=j: dve.wait_ge(xt_in[j % 2], 16 * (j // 2 + 1)))
                if j + 2 < NB:
                    split_lo(Lin(U_D + j + 2))

        @block.gpsimd
        def _(pool):
            g = nc.gpsimd

            def rows(at, src):
                pool.dma_start(prm_rows[at:at + src.shape[0], 0:src.shape[1]], src).then_inc(prm_in, 16)

            rows(C_C, c.rearrange("o (k p) -> (o k) p", p=P))
            rows(C_LN, ln_g.rearrange("l (k p) -> (l k) p", p=P))
            rows(C_ADA, ada_b.rearrange("l (k p) -> (l k) p", p=P))
            rows(C_CONV, conv_w[0].rearrange("w (k p) -> (w k) p", p=P))
            rows(C_SGN, sg_norm[0])
            for at, w in ((C_QN, q_norm), (C_KN, k_norm)):
                for head in range(2):
                    pool.dma_start(prm_rows[at:at + 1, head * DH:(head + 1) * DH], w).then_inc(prm_in, 16)

            steps_of = [0]

            def own(instruction):
                instruction.then_inc(const_step, 1)
                steps_of[0] += 1

            def own_wait():
                pool.wait_ge(const_step, steps_of[0])

            own(g.memset(ones[:], 1.0))
            own(g.memset(cap[:], 0.0))
            own_wait()
            g.affine_select(out=ident[:], in_=cap[:], compare_op=ALU.not_equal, fill=1.0, base=0,
                            pattern=[[-1, P]], channel_multiplier=1).then_inc(consts, 1)
            own(g.affine_select(out=U_f[:], in_=ones[:], compare_op=ALU.is_ge, fill=0.0, base=0,
                                pattern=[[-1, P]], channel_multiplier=1))
            own(g.affine_select(out=strict[:], in_=ones[:], compare_op=ALU.is_gt, fill=0.0, base=0,
                                pattern=[[1, P]], channel_multiplier=-1))
            own_wait()
            own(g.affine_select(out=cap[:], in_=ones[:], compare_op=ALU.is_gt, fill=-200.0, base=0,
                                pattern=[[1, P]], channel_multiplier=-1))
            own(g.memset(minus_half[:], -0.5))
            own_wait()
            g.memset(eps_t[:], EPS).then_inc(consts, 1)

            pool.wait_ge(emptied[0], NC)
            pool.wait_ge(emptied[1], NC)
            pool.dma_start(xd0.rearrange("k p t -> p k t"), xT[:]).then_inc(x_saved, 16)
            pool.wait_ge(x_saved, 16)
            pool.wait_ge(hl_ready, NB)

            def xa_load(j, at):
                s = j.base % 2
                pool.dma_start(xa[s][:], at).then_inc(xa_in[s], 16)

            xa_load(Lin(0), xd0[0])
            xa_load(Lin(1), xd0[1])
            pool.wait_ge(y_lo, 2 * NB)
            pool.dma_start(vn[:], sg_w[0].rearrange("g t s -> t g s")).then_inc(sgw_in, 16)
            pool.dma_start(sgb[:].rearrange("p g t -> p (g t)"),
                           sg_b.rearrange("o g t -> o (g t)").partition_broadcast(P)).then_inc(sgb_in, 16)
            pool.wait_ge(sgw_in, 16)
            g.affine_select(out=vn[:], in_=vn[:], compare_op=ALU.is_ge, fill=0.0, base=0,
                            pattern=[[0, G], [-1, P]], channel_multiplier=1).then_inc(sgw_masked, 1)

            def xa_store(n, at, s, turns):
                pool.wait_ge(emptied[0], (n + 1).v)
                pool.wait_ge(emptied[1], (n + 1).v)
                pool.dma_start(at, xa[s][:]).then_inc(xa_out[s], 16)

            with pool.Fori(0, NB // 2 - 1) as i:
                for a in range(2):
                    xa_store(Lin(N_A2 + a, i, 2), xd1[bass.ds(Lin(a, i, 2).v, 1)], a, i)
                    pool.wait_ge(xa_out[a], Lin(16, i, 16).v)
                    pool.dma_start(xa[a][:], xd0[bass.ds(Lin(a + 2, i, 2).v, 1)]).then_inc(xa_in[a], 16)
            for a in range(2):
                xa_store(Lin(N_A2 + NB - 2 + a), xd1[NB - 2 + a], a, 0)

            with pool.Fori(0, G) as i:
                pool.wait_ge(ssq_ready, Lin(1, i, 1).v)
                g.tensor_tensor(rv[:], ssq[:], minus_half[:], ALU.pow).then_inc(rv_ready, 1)
            pool.wait_ge(y_lo, 4 * NB)
            for a in range(2):
                pool.wait_ge(xa_out[a], 16 * (NB // 2))
            pool.dma_start(xT[:], xd1.rearrange("k p t -> p k t")).then_inc(x1_in, 16)
            pool.wait_ge(emptied[0], N_C)
            pool.wait_ge(emptied[1], N_C)
            pool.dma_start(xd2.rearrange("k p t -> p k t"), xT[:]).then_inc(y_saved, 16)


            def minus(o, i, hi):
                return g.tensor_tensor(o, i, hi.bitcast(F32), ALU.subtract)

            def softplus_lo(b, a):
                s = steps[a]
                v = slice(s["c0"], HT)
                pool.wait_ge(sp_hi, (b * STEPS + (a + 1)).v)
                minus(spL[:, a % 2, v], e[a % 2][:, v], spH[:, a % 2, v]).then_inc(sp_lo, 1)

            def pair(p, par, project, attend):
                b = p - 1
                n = p * C_FILLS + N_C
                if attend:
                    softplus_lo(b, 0)
                for t in range(STEPS):
                    if attend and t + 1 < STEPS:
                        softplus_lo(b, t + 1)
                    if not project:
                        continue
                    if t in (15, 18):
                        half = (15, 18).index(t)
                        h = HALF[half]
                        pool.wait_ge(k_hi, (p * 2 + (half + 1)).v)
                        minus(K[par][1][:, h], kr[:, h], K[par][0][:, h]).then_inc(k_lo, 1)
                    if t in SPLIT_AT:
                        kind = SPLIT_AT.index(t)
                        u = p * 4 + (U_C + kind + 2)
                        pool.wait_ge(w_hi, (u + 1).v)
                        minus(wL[:, kind % 2], raw[:, kind % 2], wH[:, kind % 2]).then_inc(w_lo, 1)
                if attend:
                    pool.wait_ge(y_ready, (b * 4 + 4).v)
                    pool.dma_start(yd[bass.ds(b.v, 1)] if b.coef else yd[b.base], gz[1 - par][:]).then_inc(y_saved, 16)

            pair(Lin(0), 0, True, False)
            with pool.Fori(0, NP // 2 - 1) as i:
                pair(Lin(1, i, 2), 1, True, True)
                pair(Lin(2, i, 2), 0, True, True)
            pair(Lin(NP - 1), 1, True, True)
            pair(Lin(NP), 0, False, True)

            pool.wait_ge(y_saved, 16 * (NP + 1))
            for k in range(NP):
                if k >= 4:
                    pool.wait_ge(hl_ready, 2 * NB + k - 3)
                pool.dma_start(ys[:, k % 4], yd[k]).then_inc(ys_in[k % 4], 16)
                if k < 2:
                    pool.dma_start(xt[k][:], xd2[k]).then_inc(xt_in[k], 16)
            for j in range(NB):
                s = j % 2
                if j + 2 < NB:
                    pool.wait_ge(t_filled, 2 * j + 2)
                    pool.dma_start(xt[s][:], xd2[j + 2]).then_inc(xt_in[s], 16)
                pool.wait_ge(t_out, 2 * j + 2)
                pool.dma_start(out[0, :, j * P:(j + 1) * P].rearrange("(c p) d -> p c d", p=P), ot[s]
                               ).then_inc(stored[s], 16)
            for s in range(2):
                pool.wait_ge(stored[s], 16 * (NB // 2))


_INS = ["x", "c", "ln_g", "ada_w", "ada_b", "w_in_ab", "conv_w", "sg_norm", "sg_w", "sg_b", "w_out_ab", "w_in_c",
        "q_norm", "k_norm", "w_out_c"]


def kernel(**inputs):
    import numpy as _np
    import concourse.bacc as _bacc
    from concourse.bass_utils import run_bass_kernel_spmd as _run

    nc = _bacc.Bacc("TRN2", target_bir_lowering=False, num_devices=1)
    arrays, args = {}, []
    for name in _INS:
        a = _np.ascontiguousarray(inputs[name])
        arrays[f"in_{name}"] = a
        args.append(nc.dram_tensor(f"in_{name}", a.shape, mybir.dt.from_np(a.dtype), kind="ExternalInput").ap())
    shape = tuple(inputs["x"].shape)
    args.append(nc.dram_tensor("out_x", shape, F32, kind="ExternalOutput").ap())
    hybrid_trunk(nc, *args)
    r = _run(nc, [arrays], core_ids=[0])
    return r.results[0]["out_x"]
```

```python
from contextlib import ExitStack

import concourse.bass as bass
from concourse import mybir

F32 = mybir.dt.float32
F32R = mybir.dt.float32r
U32 = mybir.dt.uint32
ALU = mybir.AluOpType
ACT = mybir.ActivationFunctionType
AX_X = mybir.AxisListType.X

P = 128
SIGN = 0x80000000
LN_EXP_SET = "natural_log_exp_and_others"
SILU_SET = "silu_and_others"


class Lin:

    def __init__(self, base, turn=0, coef=0):
        self.base, self.turn, self.coef = base, turn, coef

    def __add__(self, n):
        return Lin(self.base + n, self.turn, self.coef)

    def __sub__(self, n):
        return self + -n

    def __mul__(self, n):
        return Lin(self.base * n, self.turn, self.coef * n)

    def half(self):
        assert self.coef % 2 == 0
        return Lin(self.base // 2, self.turn, self.coef // 2)

    @property
    def v(self):
        return self.turn * self.coef + self.base if self.coef else self.base

    @property
    def positive(self):
        return self.base > 0


def hybrid_trunk(nc, x, c, ln_g, ada_w, ada_b, w_in_ab, conv_w, sg_norm, sg_w, sg_b,
                 w_out_ab, w_in_c, q_norm, k_norm, w_out_c, out):
    _, T, D = x.shape
    HT = T // 2
    NB = D // P
    NC = T // P
    CONV_W = conv_w.shape[1]
    G = sg_w.shape[1]
    DH = q_norm.shape[1]
    NP = D // (2 * DH)
    EPS = 1e-6
    NADA = 2 * 3 * NB
    NADA0 = 2 * NB
    assert T == 1024 and D == 1024 and DH == 64 and G == NB

    U_ADA, U_A = 0, NADA0
    U_A2 = U_A + 8 * NB
    U_B = U_A2 + NB
    U_B2 = U_B + 3 * G
    U_C = U_B2 + NB
    U_D = U_C + 4 * NP
    U_END = U_D + NB
    N_A = NC
    N_A2 = N_A + 4 * NB
    N_B = N_A2 + NB
    N_B2 = N_B + 3 * G
    N_C = N_B2 + NB
    C_FILLS = 7
    N_D = N_C + C_FILLS * NP
    STEPS = 24

    chains = [(head, half) for head in range(2) for half in range(2)]
    steps = []
    for ci, (head, half) in enumerate(chains):
        last_block = 4 * half + 3
        for j in range(last_block, -1, -1):
            steps.append(dict(chain=ci, head=head, half=half, j=j, c0=max(0, P * j - HT * half),
                              diagonal=j >= 4 * half, first=j == last_block, last=j == 0))
    assert len(steps) == STEPS

    with ExitStack() as ctx:
        def sb(name, shape, dt=F32):
            return ctx.enter_context(nc.sbuf_tensor(name, shape, dt))

        def sem(name):
            return ctx.enter_context(nc.semaphore(name))

        def dram(name, shape):
            return nc.dram_tensor(name, shape, F32, kind="Internal").ap()

        xd0, xd1, xd2 = (dram(f"x_t{i}", [NB, P, T]) for i in range(3))
        yd = dram("y_t", [NP, P, T])

        hH = sb("hH", [P, NB, T], F32R)
        hL = sb("hL", [P, NB, T], F32R)
        R2 = sb("R2", [P, 16 * T], F32R)
        yH = R2[:, 0:8 * T].rearrange("p (k t) -> p k t", k=NB)
        yL = R2[:, 8 * T:16 * T].rearrange("p (k t) -> p k t", k=NB)
        QP = 6 * T
        Q = [[[R2[:, par * QP + (2 * head + part) * T:par * QP + (2 * head + part + 1) * T]
               for part in range(2)] for head in range(2)] for par in range(2)]
        K = [[R2[:, par * QP + (4 + part) * T:par * QP + (5 + part) * T] for part in range(2)]
             for par in range(2)]
        V = [R2[:, 12 * T + par * 2 * T:12 * T + (par + 1) * 2 * T].rearrange(
            "p (j h d) -> p j h d", j=NC, h=2) for par in range(2)]
        raw = sb("raw", [P, 2, NB, P])
        wH = sb("wH", [P, 2, NB, P], F32R)
        wL = sb("wL", [P, 2, NB, P], F32R)
        spH = sb("spH", [P, 2, HT], F32R)
        spL = sb("spL", [P, 2, HT], F32R)
        pH = sb("pH", [P, HT], F32R)
        pL = sb("pL", [P, HT], F32R)
        sums_in = sb("sums_in", [P, 2, HT])
        FA = sb("FA", [P, 8 * T + 8])
        xT = FA[:, 0:8 * T].rearrange("p (k t) -> p k t", k=NB)
        cs = FA[:, 0:T]
        cx = FA[:, T:2 * T + 2]
        cv = FA[:, 2 * T + 4:3 * T + 4]
        sz = FA[:, 3 * T + 4:4 * T + 4]
        vT = cs
        vn = FA[:, T:2 * T].rearrange("p (c d) -> p c d", c=NC)
        us = FA[:, 4 * T + 4:5 * T + 4]
        xa = [FA[:, (4 + s) * T + 4:(5 + s) * T + 4] for s in range(2)]
        WT = FA[:, 6 * T + 4:7 * T + 4].rearrange("p (g t) -> p g t", g=G)
        sgb = FA[:, 7 * T + 4:8 * T + 4].rearrange("p (g t) -> p g t", g=G)
        zs = [FA[:, s * HT:(s + 1) * HT] for s in range(4)]
        e = [FA[:, (4 + s) * HT:(5 + s) * HT] for s in range(3)]
        osh = FA[:, 7 * HT:8 * HT]
        gz = [FA[:, (4 + s) * T:(5 + s) * T] for s in range(2)]
        qr = FA[:, 6 * T:7 * T]
        kr = FA[:, 7 * T:8 * T]
        ys = FA[:, 0:4 * T].rearrange("p (s t) -> p s t", s=4)
        xt = [FA[:, (4 + s) * T:(5 + s) * T] for s in range(2)]
        ot = [FA[:, (6 + s) * T:(7 + s) * T].rearrange("p (c d) -> p c d", c=NC) for s in range(2)]

        ident = sb("ident", [P, P])
        ones = sb("ones", [P, P])
        pair_ones = sb("pair_ones", [P, P])
        strict = sb("strict", [P, P])
        cap = sb("cap", [P, P])
        U_f = sb("U_f", [P, P])
        U_r = sb("U_r", [P, P], F32R)
        Uc_r = sb("Uc_r", [P, P], F32R)
        prm_rows = sb("prm_rows", [P, P])
        prm = sb("prm", [P, P])
        C_C, C_LN, C_ADA = 0, NB, 3 * NB
        C_CONV = C_ADA + NADA
        C_SGN = C_CONV + CONV_W * NB
        C_QN = C_SGN + G
        C_KN = C_QN + 1
        NPRM = C_KN + 1
        mod = sb("mod", [P, NADA])
        gs = sb("gs", [P, 2 * NB])
        ca = sb("ca", [P, 3, NB])
        cHL = sb("cHL", [P, NB, 2], F32R)
        ssq = sb("ssq", [P, NC])
        rv = sb("rv", [P, NC])
        minus_half = sb("minus_half", [P, NC])
        eps_t = sb("eps_t", [P, 1])
        qn_scaled = sb("qn_scaled", [P, 1])

        def bank(name):
            return ctx.enter_context(nc.psum_tensor(name, [P, HT], F32))

        PB = [bank("P0"), bank("P1")]
        ZB = [bank("Z0"), bank("Z1")]
        CB = [bank("C0"), bank("C1")]
        OB = [bank("O0"), bank("O1")]
        MB = OB[0]

        raw_in = [sem(f"raw_in{s}") for s in range(2)]
        w_hi, w_lo = sem("w_hi"), sem("w_lo")
        filled = [sem(f"filled{b}") for b in range(2)]
        emptied = [sem(f"emptied{b}") for b in range(2)]
        ada_done = sem("ada_done")
        mod_ready = sem("mod_ready")
        prm_in, prm_tr, prm_ready = sem("prm_in"), sem("prm_tr"), sem("prm_ready")
        consts, fr_ready = sem("consts"), sem("fr_ready")
        ce, ca_ready = sem("ce"), sem("ca_ready")
        sq_ready, sum_done, rs_ready = sem("sq_ready"), sem("sum_done"), sem("rs_ready")
        ht_ready, hh_ready, hl_ready = sem("ht_ready"), sem("hh_ready"), sem("hl_ready")
        x_saved = sem("x_saved")
        y_hi, y_lo = sem("y_hi"), sem("y_lo")
        xa_in = [sem(f"xa_in{s}") for s in range(2)]
        xa_out = [sem(f"xa_out{s}") for s in range(2)]
        sgw_in, sgw_masked, sgw_tr, wt_ready = sem("sgw_in"), sem("sgw_masked"), sem("sgw_tr"), sem("wt_ready")
        v_turned, ssq_ready, rv_ready, vn_ready = sem("v_turned"), sem("ssq_ready"), sem("rv_ready"), sem("vn_ready")
        sg_filled, sg_out = sem("sg_filled"), sem("sg_out")
        x1_in = sem("x1_in")
        y_prod, conv_step, gate_step, vn_step = sem("y_prod"), sem("conv_step"), sem("gate_step"), sem("vn_step")
        start_step, rms_ln, q_zeroed = sem("start_step"), sem("rms_ln"), sem("q_zeroed")
        gz_exp, e_exp, arg_raw, sp_raw, sp_free = (sem(n) for n in ("gz_exp", "e_exp", "arg_raw", "sp_raw", "sp_free"))
        o_sum, const_step, sgb_in = sem("o_sum"), sem("const_step"), sem("sgb_in")
        qk_sq, qk_rs, qk_n = sem("qk_sq"), sem("qk_rs"), sem("qk_n")
        q_hi, q_lo, k_hi, k_lo, v_hi = (sem(n) for n in ("q_hi", "q_lo", "k_hi", "k_lo", "v_hi"))
        gz_ln, gz_sig, gz_ready = sem("gz_ln"), sem("gz_sig"), sem("gz_ready")
        z_filled, z_copied, e_neg, e_ln = sem("z_filled"), sem("z_copied"), sem("e_neg"), sem("e_ln")
        sp_ready, sp_hi, sp_lo = sem("sp_ready"), sem("sp_hi"), sem("sp_lo")
        u_done, arg_ready, w_ready = sem("u_done"), sem("arg_ready"), sem("w_ready")
        p_hi, p_lo, pv_done = sem("p_hi"), sem("p_lo"), sem("pv_done")
        o_shifted, y_ready = sem("o_shifted"), sem("y_ready")
        y_saved = sem("y_saved")
        ys_in = [sem(f"ys_in{s}") for s in range(4)]
        xt_in = [sem(f"xt_in{s}") for s in range(2)]
        t_filled, t_out = sem("t_filled"), sem("t_out")
        stored = [sem(f"stored{s}") for s in range(2)]

        HALF = [slice(0, HT), slice(HT, T)]
        ROWS = [slice(0, DH), slice(DH, P)]
        SUMS_AT, TURN_AT, SPLIT_AT = (7, 10, 13, 16), (20, 22), (3, 9, 15, 21)
        DIAGONALS = sum(s["diagonal"] for s in steps)
        LOWERS = sum(not s["last"] for s in steps)

        def the_step(a):
            return steps[a % STEPS]

        def upto(b, a):
            return b * STEPS + (a + 1)

        def diagonals_upto(b, a):
            return (b + a // STEPS) * DIAGONALS + sum(s["diagonal"] for s in steps[:a % STEPS + 1])

        def lowers_upto(b, a):
            return (b + a // STEPS) * LOWERS + sum(not s["last"] for s in steps[:a % STEPS + 1])

        def par_of(par, a):
            return 1 - par if 0 <= a < STEPS else par

        def slots(end):
            return range(STEPS + 3) if end == STEPS else range(STEPS)



        def cols(w, at, n=P):
            return w[:, bass.ds(at, n)].rearrange("(k p) n -> p k n", p=P)

        W_AB, W_C, W_OC = w_in_ab[0], w_in_c[0], w_out_c[0]
        W_OA, W_OB = w_out_ab[0, 0:D, :], w_out_ab[0, D:2 * D, :]
        A_B, A_C, A_X, A_Z, B_U, B_V, B_Z = (D * i for i in range(7))

        block = ctx.enter_context(nc.Block())

        @block.sync
        def _(sp):
            def load_unit(u, w, at):
                src = cols(w, at if isinstance(at, int) else sp.snap(at))
                slot = u.base % 2
                sp.wait_ge(w_hi, (u - 1).v)
                sp.wait_ge(w_lo, (u - 1).v)
                sp.dma_start(raw[:, slot], src).then_inc(raw_in[slot], 16)

            for ch in range(NC):
                if ch >= 2:
                    sp.wait_ge(filled[1], ch - 1)
                sp.dma_start(raw[:, ch % 2], x[0, ch * P:(ch + 1) * P, :].rearrange("t (k n) -> t k n", n=P)
                             ).then_inc(raw_in[ch % 2], 16)
            for m in range(NADA0):
                if m < 2:
                    sp.wait_ge(filled[1], NC - 1 + m)
                    sp.dma_start(raw[:, m], cols(ada_w[0], m * P)).then_inc(raw_in[m], 16)
                else:
                    load_unit(Lin(m), ada_w[0], m * P)

            def group_a(i, layer, first_turn, first_block):
                u = Lin(U_A - 8, i, 8)
                for k, w_at in enumerate((A_C, A_X, A_Z, A_B)):
                    load_unit(u + 2 * k, W_AB, i * P + (w_at - P))
                    load_unit(u + (2 * k + 1), ada_w[layer],
                              i * (4 * P) + (first_block + k - 4 * (first_turn + 1)) * P)

            with sp.Fori(1, 3) as i:
                group_a(i, 0, 0, NADA0)
            with sp.Fori(3, NB + 1) as i:
                group_a(i, 1, 2, 0)

            def load_pairs(u0, w):
                with sp.Fori(0, NB // 2) as i:
                    for a in range(2):
                        load_unit(Lin(u0 + a, i, 2), w, i * (2 * P) + a * P)

            load_pairs(U_A2, W_OA)
            with sp.Fori(0, G // 2) as i:
                for a in range(6):
                    w_at = (B_V, B_U, B_Z)[a % 3]
                    load_unit(Lin(U_B + a, i, 6), W_AB, i * (2 * P) + (w_at + (a // 3) * P))
            load_pairs(U_B2, W_OB)
            with sp.Fori(0, NP) as i:
                for a in range(4):
                    load_unit(Lin(U_C + a, i, 4), W_C, i * P + a * D)
            load_pairs(U_D, W_OC)

        @block.tensor
        def _(pe):
            mm, turn = nc.tensor.matmul, nc.tensor.transpose

            def products(half, slot, H, L, ks, split_by=None, split_base=0):
                h, acc = HALF[half], PB[half][:]
                for k in ks:
                    if split_by is not None:
                        pe.wait_ge(split_by, split_base + k + 1)
                    mm(acc, wH[:, slot, k], H[:, k, h], start=k == 0, stop=False)
                    mm(acc, wH[:, slot, k], L[:, k, h], start=False, stop=False)
                    last = mm(acc, wL[:, slot, k], H[:, k, h], start=False, stop=k == NB - 1)
                return last

            def wait_split(u):
                pe.wait_ge(w_hi, (u + 1).v)
                pe.wait_ge(w_lo, (u + 1).v)

            def unit(u, n, H, L, split_by=None, split_base=0):
                wait_split(u)
                for half in range(2):
                    pe.wait_ge(emptied[half], n.v)
                    products(half, u.base % 2, H, L, range(NB), split_by, split_base).then_inc(filled[half], 1)

            def ada(u, m):
                wait_split(u)
                slot = u.base % 2
                acc = MB[:, bass.ds((m * 2).v, 2)]
                for k in range(NB):
                    mm(acc, wH[:, slot, k], cHL[:, k, :], start=k == 0, stop=False)
                    last = mm(acc, wL[:, slot, k], cHL[:, k, :], start=False, stop=k == NB - 1)
                last.then_inc(ada_done, 1)

            def channel_sums(layer):
                for k in range(NB):
                    for half in range(2):
                        pe.wait_ge(sq_ready, 2 * NB * layer + 2 * k + half + 1)
                        mm(CB[half][:], ones[:], sums_in[:, half], start=k == 0,
                           stop=k == NB - 1).then_inc(sum_done, 1)

            pe.wait_ge(consts, 1)
            pe.wait_ge(prm_in, 16 * 9)
            turn(ZB[0][:, 0:NPRM], prm_rows[0:NPRM, :], ident[0:NPRM, 0:NPRM]).then_inc(prm_tr, 1)
            for ch in range(NC):
                pe.wait_ge(raw_in[ch % 2], 16 * (ch // 2 + 1))
                for half in range(2):
                    if ch:
                        pe.wait_ge(emptied[half], ch)
                    for k in range(4):
                        last = turn(PB[half][:, k * P:(k + 1) * P], raw[:, ch % 2, 4 * half + k, :], ident[:])
                    last.then_inc(filled[half], 1)
            pe.wait_ge(consts, 2)
            channel_sums(0)
            pe.wait_ge(ca_ready, 1)
            for m in range(NADA0):
                ada(Lin(m), Lin(m))

            pe.wait_ge(mod_ready, 1)
            pe.wait_ge(hl_ready, NB)
            with pe.Fori(0, NB) as i:
                for k in range(4):
                    unit(Lin(U_A + 2 * k, i, 8), Lin(N_A + k, i, 4), hH, hL)
                    ada(Lin(U_A + 2 * k + 1, i, 8), Lin(NADA0 + k, i, 4))
            pe.wait_ge(y_lo, 2 * NB)
            with pe.Fori(0, NB // 2) as i:
                for a in range(2):
                    unit(Lin(U_A2 + a, i, 2), Lin(N_A2 + a, i, 2), yH, yL)
            pe.wait_ge(sgw_masked, 1)
            for g in range(G):
                last = turn(ZB[g // 4][:, (g % 4) * P:(g % 4 + 1) * P], vn[:, g, :], ident[:])
                if g % 4 == 3:
                    last.then_inc(sgw_tr, 1)
            pe.wait_ge(wt_ready, 2)

            with pe.Fori(0, G // 2) as i:
                for a in range(2):
                    u, n = Lin(U_B + 3 * a, i, 6), Lin(N_B + 3 * a, i, 6)
                    g = Lin(a, i, 2)
                    unit(u, n, hH, hL)
                    unit(u + 1, n + 1, hH, hL)
                    pe.wait_ge(emptied[0], (n + 1).v)
                    pe.wait_ge(emptied[1], (n + 1).v)
                    for half in range(2):
                        for q in range(4):
                            ch = 4 * half + q
                            last = turn(ZB[half][:, q * P:(q + 1) * P], vT[:, ch * P:(ch + 1) * P], ident[:])
                        last.then_inc(v_turned, 1)
                    unit(u + 2, n + 2, hH, hL)
                    pe.wait_ge(vn_ready, (g + 1).v)
                    for half in range(2):
                        for q in range(4):
                            ch = 4 * half + q
                            last = mm(CB[half][:, q * P:(q + 1) * P], vn[:, ch, :], WT[:, bass.ds(g.v, 1), :],
                                      start=True, stop=True)
                        last.then_inc(sg_filled, 1)
            pe.wait_ge(y_lo, 4 * NB)
            with pe.Fori(0, NB // 2) as i:
                for a in range(2):
                    unit(Lin(U_B2 + a, i, 2), Lin(N_B2 + a, i, 2), yH, yL)
            channel_sums(1)

            def part(p, hu, third):
                kind, half = hu // 2, hu % 2
                if third == 0:
                    if half == 0:
                        wait_split(p * 4 + (U_C + kind))
                    pe.wait_ge(emptied[half], (p * C_FILLS + (N_C + (0, 1, 3, 5)[kind])).v)
                last = products(half, kind % 2, hH, hL, ((0, 1, 2), (3, 4, 5), (6, 7))[third])
                if third == 2:
                    last.then_inc(filled[half], 1)

            def norm_sum(p, which, half):
                pe.wait_ge(emptied[half], (p * C_FILLS + (N_C + (2, 4)[which])).v)
                pe.wait_ge(qk_sq, (p * 4 + (2 * which + half + 1)).v)
                mm(PB[half][:], pair_ones[:], sums_in[:, half], start=True, stop=True).then_inc(filled[half], 1)

            def turn_v(p, half):
                pe.wait_ge(emptied[half], (p * C_FILLS + (N_C + 6)).v)
                for q in range(4):
                    ch = 4 * half + q
                    last = turn(PB[half][:, q * P:(q + 1) * P], qr[:, ch * P:(ch + 1) * P], ident[:])
                last.then_inc(filled[half], 1)

            def scores(b, par, a):
                s, own = the_step(a), b + a // STEPS
                if a % STEPS == 0:
                    pe.wait_ge(q_lo, (own * 4 + 4).v)
                    pe.wait_ge(k_lo, (own * 2 + 2).v)
                if upto(b, a - 2).positive:
                    pe.wait_ge(z_copied, upto(b, a - 2).v)
                keys = slice(s["j"] * P, (s["j"] + 1) * P)
                qs = slice(s["half"] * HT + s["c0"], (s["half"] + 1) * HT)
                o = ZB[a % 2][:, s["c0"]:HT]
                (qh, ql), (kh, kl) = Q[par][s["head"]], K[par]
                mm(o, kh[:, keys], qh[:, qs], start=True, stop=False)
                mm(o, kh[:, keys], ql[:, qs], start=False, stop=False)
                mm(o, kl[:, keys], qh[:, qs], start=False, stop=True).then_inc(z_filled, 1)

            def suffix(b, a, upper):
                s = the_step(a)
                if upper:
                    pe.wait_ge(sp_lo, upto(b, a).v)
                else:
                    pe.wait_ge(arg_ready, upto(b, a).v)
                o, w = CB[s["chain"] % 2][:, s["c0"]:HT], U_r if upper else Uc_r
                mm(o, w[:], spH[:, a % 2, s["c0"]:HT], start=upper and s["first"], stop=False, skip_group_check=True)
                mm(o, w[:], spL[:, a % 2, s["c0"]:HT], start=False, stop=upper and s["last"],
                   skip_group_check=True).then_inc(u_done if upper else sp_free, 1)

            def weighted_v(b, par, a):
                s, own = the_step(a), b + a // STEPS
                if a % STEPS == 0:
                    for half in range(2):
                        pe.wait_ge(emptied[half], (own * C_FILLS + (N_C + C_FILLS)).v)
                if s["first"] and (own * 4 + (s["chain"] - 1)).positive:
                    pe.wait_ge(o_sum, (own * 4 + (s["chain"] - 1)).v)
                pe.wait_ge(p_lo, upto(b, a).v)
                o, w = OB[s["chain"] % 2][:, s["c0"]:HT], V[par][:, s["j"], s["head"], :]
                mm(o, w, pH[:, s["c0"]:HT], start=s["first"], stop=False, skip_group_check=True)
                mm(o, w, pL[:, s["c0"]:HT], start=False, stop=s["last"],
                   skip_group_check=True).then_inc(pv_done, 1)

            parts = [(hu, third) for hu in range(8) for third in range(3)]

            def pair(p, par, first, end):
                b = p - 1
                for t in slots(end):
                    if first <= t - 2 < end:
                        weighted_v(b, par_of(par, t - 2), t - 2)
                    if first <= t < end:
                        suffix(b, t, True)
                    if first <= t + 3 < end:
                        scores(b, par_of(par, t + 3), t + 3)
                    if end > STEPS:
                        for hu, third in parts[2 * t:2 * t + 2] if t < 3 else parts[t + 3:t + 4]:
                            part(p, hu, third)
                        if t in SUMS_AT:
                            norm_sum(p, *divmod(SUMS_AT.index(t), 2))
                        if t in TURN_AT:
                            turn_v(p, TURN_AT.index(t))
                    if first <= t < end and not the_step(t)["last"]:
                        suffix(b, t, False)

            pe.wait_ge(hl_ready, 2 * NB)
            pe.wait_ge(q_zeroed, 1)
            pair(Lin(0), 0, STEPS, 2 * STEPS)
            pair(Lin(1), 1, 0, 2 * STEPS)
            with pe.Fori(0, NP // 2 - 1) as i:
                pair(Lin(2, i, 2), 0, -STEPS, 2 * STEPS)
                pair(Lin(3, i, 2), 1, -STEPS, 2 * STEPS)
            pair(Lin(NP), 0, -STEPS, STEPS)

            def turn_out(j):
                for half in range(2):
                    pe.wait_ge(emptied[half], (j + (N_D + 1)).v)
                for half in range(2):
                    if j.coef or j.base:
                        pe.wait_ge(t_out, (j * 2 + (half - 1)).v)
                    for q in range(4):
                        ch = 4 * half + q
                        last = turn(ZB[half][:, q * P:(q + 1) * P], xt[j.base % 2][:, ch * P:(ch + 1) * P], ident[:])
                    last.then_inc(t_filled, 1)

            unit(Lin(U_D), Lin(N_D), hH, hL, hl_ready, 2 * NB)
            unit(Lin(U_D + 1), Lin(N_D + 1), hH, hL)
            turn_out(Lin(0))
            with pe.Fori(1, NB // 2) as i:
                unit(Lin(U_D, i, 2), Lin(N_D, i, 2), hH, hL)
                turn_out(Lin(-1, i, 2))
                unit(Lin(U_D + 1, i, 2), Lin(N_D + 1, i, 2), hH, hL)
                turn_out(Lin(0, i, 2))
            turn_out(Lin(NB - 1))

        @block.scalar
        def _(act):
            f = nc.scalar.activation

            def copy(o, i):
                return nc.scalar.activation(o, i, ACT.Copy)

            def split_hi(u):
                slot = u.base % 2
                act.wait_ge(raw_in[slot], (u.half() * 16 + 16 * (NC // 2 + 1)).v)
                copy(wH[:, slot], raw[:, slot]).then_inc(w_hi, 1)

            def unit_done(n):
                act.wait_ge(filled[1], (n + 1).v)

            nc.scalar.preload_act_table_set(LN_EXP_SET)
            act.wait_ge(prm_ready, 1)
            f(ca[:, 0, :], prm[:, C_C:C_C + NB], ACT.Exp, scale=-1.0).then_inc(ce, 1)
            for ch in range(NC):
                act.wait_ge(filled[1], ch + 1)
                copy(xT[:, 4:8, ch * P:(ch + 1) * P], PB[1][:].rearrange("p (k t) -> p k t", k=4)
                     ).then_inc(emptied[1], 1)

            def rms_of_x(layer):
                for k in range(NB):
                    for half in range(2):
                        if k:
                            act.wait_ge(sum_done, 2 * NB * layer + 2 * (k - 1) + half + 1)
                        f(sums_in[:, half], xT[:, k, HALF[half]], ACT.Square).then_inc(sq_ready, 1)
                for half in range(2):
                    act.wait_ge(sum_done, 2 * NB * layer + 2 * NB - 1 + half)
                    f(sums_in[:, half], CB[half][:], ACT.Ln, bias=eps_t[:], scale=1.0 / D).then_inc(rms_ln, 1)
                    act.wait_ge(rms_ln, 2 * layer + half + 1)
                    f(sums_in[:, half], sums_in[:, half], ACT.Exp, scale=-0.5).then_inc(rs_ready, 1)

            def h_hi(layer):
                for k in range(NB):
                    act.wait_ge(ht_ready, NB * layer + k + 1)
                    at = 3 * NB * layer + k
                    f(hH[:, k], xT[:, k], ACT.Identity, bias=mod[:, at:at + 1]).then_inc(hh_ready, 1)

            act.wait_ge(emptied[0], NC)
            act.wait_ge(emptied[1], NC)
            act.wait_ge(consts, 2)
            rms_of_x(0)
            for m in range(NADA0):
                if m >= 2:
                    act.wait_ge(ada_done, m - 1)
                split_hi(Lin(m))
            nc.scalar.preload_act_table_set(SILU_SET)
            h_hi(0)
            for m in range(2):
                act.wait_ge(ada_done, NADA0 - 1 + m)
                split_hi(Lin(U_A + m))

            with act.Fori(0, NB) as i:
                u, n = Lin(U_A, i, 8), Lin(N_A, i, 4)

                def ada_split(k):
                    act.wait_ge(ada_done, Lin(NADA0 + k + 1, i, 4).v)
                    split_hi(u + (2 * k + 3))

                for half in range(2):
                    act.wait_ge(filled[half], (n + 1).v)
                    copy(cs[:, HALF[half]], PB[half][:]).then_inc(emptied[half], 1)
                split_hi(u + 2)
                ada_split(0)
                unit_done(n + 1)
                split_hi(u + 4)
                ada_split(1)
                for half in range(2):
                    act.wait_ge(filled[half], (n + 3).v)
                    f(sz[:, HALF[half]], PB[half][:], ACT.Silu).then_inc(emptied[half], 1)
                split_hi(u + 6)
                ada_split(2)
                unit_done(n + 3)
                split_hi(u + 8)
                for half in range(2):
                    act.wait_ge(emptied[half], (n + 4).v)
                    copy(yH[:, bass.ds(i, 1), HALF[half]], cv[:, HALF[half]]).then_inc(y_hi, 1)
                ada_split(3)
            with act.Fori(0, NB // 2) as i:
                for a in range(2):
                    unit_done(Lin(N_A2 + a, i, 2))
                    split_hi(Lin(U_A2 + a + 2, i, 2))
            with act.Fori(0, G // 2) as i:
                for a in range(2):
                    u, n = Lin(U_B + 3 * a, i, 6), Lin(N_B + 3 * a, i, 6)
                    for half in range(2):
                        act.wait_ge(filled[half], (n + 1).v)
                        copy(vT[:, HALF[half]], PB[half][:]).then_inc(emptied[half], 1)
                    split_hi(u + 2)
                    unit_done(n + 1)
                    split_hi(u + 3)
                    for half in range(2):
                        act.wait_ge(filled[half], (n + 3).v)
                        f(sz[:, HALF[half]], PB[half][:], ACT.Silu).then_inc(emptied[half], 1)
                    split_hi(u + 4)
                    for half in range(2):
                        act.wait_ge(y_prod, Lin(2 * a + half + 1, i, 4).v)
                        copy(yH[:, bass.ds(Lin(a, i, 2).v, 1), HALF[half]], cv[:, HALF[half]]).then_inc(y_hi, 1)
            with act.Fori(0, NB // 2) as i:
                for a in range(2):
                    unit_done(Lin(N_B2 + a, i, 2))
                    split_hi(Lin(U_B2 + a + 2, i, 2))
            nc.scalar.preload_act_table_set(LN_EXP_SET)
            act.wait_ge(emptied[0], N_C)
            act.wait_ge(emptied[1], N_C)
            rms_of_x(1)
            h_hi(1)
            act.wait_ge(y_saved, 16)

            def z_copy(b, a):
                s = the_step(a)
                act.wait_ge(z_filled, upto(b, a).v)
                if upto(b, a - 4).positive:
                    act.wait_ge(p_lo, upto(b, a - 4).v)
                copy(zs[a % 4][:, s["c0"]:HT], ZB[a % 2][:, s["c0"]:HT]).then_inc(z_copied, 1)

            def exp_abs(b, a):
                v = e[a % 3][:, the_step(a)["c0"]:HT]
                act.wait_ge(e_neg, upto(b, a).v)
                f(v, v, ACT.Exp).then_inc(e_exp, 1)

            def ln_abs(b, a):
                v = e[a % 3][:, the_step(a)["c0"]:HT]
                act.wait_ge(e_exp, upto(b, a).v)
                f(v, v, ACT.Ln, bias=1.0).then_inc(e_ln, 1)

            def weight(b, a):
                v = zs[a % 4][:, the_step(a)["c0"]:HT]
                act.wait_ge(arg_ready, upto(b, a).v)
                f(v, v, ACT.Exp).then_inc(w_ready, 1)

            def weight_hi(b, a):
                v = slice(the_step(a)["c0"], HT)
                act.wait_ge(w_ready, upto(b, a).v)
                if upto(b, a - 1).positive:
                    act.wait_ge(pv_done, upto(b, a - 1).v)
                copy(pH[:, v], zs[a % 4][:, v]).then_inc(p_hi, 1)

            def o_shift(b, a):
                s = the_step(a)
                act.wait_ge(pv_done, upto(b, a).v)
                mine, other = ROWS[s["head"]], ROWS[1 - s["head"]]
                copy(osh[mine, :], OB[s["chain"] % 2][other, :]).then_inc(o_shifted, 1)

            def pair(p, par, first, end):
                b = p - 1
                n = p * C_FILLS + N_C
                for t in slots(end):
                    if first <= t + 2 < end:
                        z_copy(b, t + 2)
                    if first <= t - 1 < end:
                        weight(b, t - 1)
                        weight_hi(b, t - 1)
                    if first <= t + 2 < end:
                        exp_abs(b, t + 2)
                        ln_abs(b, t + 2)
                    if first <= t - 2 < end and the_step(t - 2)["last"]:
                        o_shift(b, t - 2)
                    if end == STEPS:
                        continue
                    if t in (2, 3):
                        half = (2, 3).index(t)
                        act.wait_ge(filled[half], (n + 1).v)
                        if p.coef or p.base:
                            act.wait_ge(gz_ready, (p * 2 + (half - 1)).v)
                        f(sums_in[:, half], PB[half][:], ACT.Square).then_inc(qk_sq, 1)
                        copy(qr[:, HALF[half]], PB[half][:]).then_inc(emptied[half], 1)
                    if t in (6, 9):
                        half = (6, 9).index(t)
                        act.wait_ge(filled[half], (n + 2).v)
                        copy(kr[:, HALF[half]], PB[half][:]).then_inc(emptied[half], 1)
                    if t in (8, 11, 14, 17):
                        which, half = divmod((8, 11, 14, 17).index(t), 2)
                        act.wait_ge(filled[half], (n + (3, 5)[which]).v)
                        f(sums_in[:, half], PB[half][:], ACT.Ln, bias=eps_t[:], scale=1.0 / DH
                          ).then_inc(emptied[half], 1)
                        act.wait_ge(emptied[half], (n + (3, 5)[which]).v)
                        f(sums_in[:, half], sums_in[:, half], ACT.Exp, scale=-0.5).then_inc(qk_rs, 1)
                    if t in (10, 13):
                        half = (10, 13).index(t)
                        act.wait_ge(qk_n, (p * 4 + (half + 1)).v)
                        act.wait_ge(emptied[half], (n + 2).v)
                        f(sums_in[:, half], kr[:, HALF[half]], ACT.Square).then_inc(qk_sq, 1)
                    if t in (12, 15):
                        half = (12, 15).index(t)
                        act.wait_ge(filled[half], (n + 4).v)
                        act.wait_ge(q_lo, (p * 4 + (2 * half + 2)).v)
                        copy(qr[:, HALF[half]], PB[half][:]).then_inc(emptied[half], 1)
                    if t in (18, 21):
                        half = (18, 21).index(t)
                        act.wait_ge(filled[half], (n + 6).v)
                        act.wait_ge(qk_n, (p * 4 + (half + 3)).v)
                        f(sums_in[:, half], PB[half][:], ACT.Exp, scale=-1.0).then_inc(gz_exp, 1)
                        if p.base > 1:
                            act.wait_ge(y_saved, (p * 16).v)
                        copy(gz[par][:, HALF[half]], PB[half][:]).then_inc(emptied[half], 1)
                    if t in (19, 22):
                        half = (19, 22).index(t)
                        act.wait_ge(gz_exp, (p * 2 + (half + 1)).v)
                        f(sums_in[:, half], sums_in[:, half], ACT.Ln, bias=1.0).then_inc(gz_ln, 1)
                        act.wait_ge(gz_ln, (p * 2 + (half + 1)).v)
                        f(sums_in[:, half], sums_in[:, half], ACT.Exp, scale=-1.0).then_inc(gz_sig, 1)
                    if t in (21, 23):
                        half = (21, 23).index(t)
                        act.wait_ge(filled[half], (n + 7).v)
                        src = PB[half][:].rearrange("p (j h d) -> p j h d", j=4, h=2)
                        blocks = slice(4 * half, 4 * half + 4)
                        copy(V[par][:, blocks, 0, 0:DH], src[:, :, 0, :])
                        copy(V[par][:, blocks, 1, DH:P], src[:, :, 1, :]).then_inc(v_hi, 1)
                    if t in SPLIT_AT:
                        kind = SPLIT_AT.index(t)
                        unit_done(n + (0, 1, 3, 5)[kind])
                        split_hi(p * 4 + (U_C + kind + 2))

            pair(Lin(0), 0, STEPS, 2 * STEPS)
            pair(Lin(1), 1, 0, 2 * STEPS)
            with act.Fori(0, NP // 2 - 1) as i:
                pair(Lin(2, i, 2), 0, -STEPS, 2 * STEPS)
                pair(Lin(3, i, 2), 1, -STEPS, 2 * STEPS)
            pair(Lin(NP), 0, -STEPS, STEPS)

            for k in range(NP):
                act.wait_ge(ys_in[k % 4], 16 * (k // 4 + 1))
                copy(hH[:, k], ys[:, k % 4]).then_inc(hh_ready, 1)

            def copy_out(j):
                if j.coef or j.base > 1:
                    act.wait_ge(stored[j.base % 2], (j.half() * 16).v)
                for half in range(2):
                    act.wait_ge(t_filled, (j * 2 + (half + 1)).v)
                    copy(ot[j.base % 2][:, 4 * half:4 * half + 4, :],
                         ZB[half][:].rearrange("p (c d) -> p c d", c=4)).then_inc(t_out, 1)

            unit_done(Lin(N_D))
            split_hi(Lin(U_D + 2))
            unit_done(Lin(N_D + 1))
            split_hi(Lin(U_D + 3))
            copy_out(Lin(0))
            unit_done(Lin(N_D + 2))
            split_hi(Lin(U_D + 4))
            copy_out(Lin(1))
            unit_done(Lin(N_D + 3))
            split_hi(Lin(U_D + 5))
            copy_out(Lin(2))
            unit_done(Lin(N_D + 4))
            split_hi(Lin(U_D + 6))
            copy_out(Lin(3))
            unit_done(Lin(N_D + 5))
            split_hi(Lin(U_D + 7))
            for j in range(4, NB):
                copy_out(Lin(j))

        @block.vector
        def _(dve):
            tt, ts, stt, copy = (nc.vector.tensor_tensor, nc.vector.tensor_scalar,
                                 nc.vector.scalar_tensor_tensor, nc.vector.tensor_copy)

            def f32(ap):
                return ap.bitcast(F32)

            def split_lo(u):
                slot = u.base % 2
                dve.wait_ge(w_hi, (u + 1).v)
                tt(wL[:, slot], raw[:, slot], f32(wH[:, slot]), ALU.subtract).then_inc(w_lo, 1)

            for o, i, value in ((0, 0, 1.0), (0, 1, 0.0), (1, 0, 0.0), (1, 1, 1.0)):
                nc.vector.memset(pair_ones[ROWS[o], ROWS[i]], value)
            dve.wait_ge(consts, 2)
            copy(U_r[:], U_f[:]).then_inc(start_step, 1)
            ts(Uc_r[:], U_f[:], -1.0, 1.0, ALU.mult, ALU.add).then_inc(start_step, 1)
            dve.wait_ge(prm_tr, 1)
            copy(prm[:, 0:NPRM], ZB[0][:, 0:NPRM]).then_inc(prm_ready, 1)
            dve.wait_ge(prm_ready, 1)
            ts(qn_scaled[:], prm[:, C_QN:C_QN + 1], float(DH) ** -0.5, None, ALU.mult).then_inc(start_step, 1)
            for ch in range(NC):
                dve.wait_ge(filled[0], ch + 1)
                copy(xT[:, 0:4, ch * P:(ch + 1) * P], PB[0][:].rearrange("p (k t) -> p k t", k=4)
                     ).then_inc(emptied[0], 1)
            dve.wait_ge(ce, 1)
            ts(ca[:, 1, :], ca[:, 0, :], 1.0, None, ALU.add).then_inc(start_step, 1)
            dve.wait_ge(start_step, 4)
            nc.vector.reciprocal(ca[:, 2, :], ca[:, 1, :]).then_inc(start_step, 1)
            dve.wait_ge(start_step, 5)
            tt(ca[:, 0, :], ca[:, 2, :], prm[:, C_C:C_C + NB], ALU.mult).then_inc(start_step, 1)
            dve.wait_ge(start_step, 6)
            copy(cHL[:, :, 0], ca[:, 0, :]).then_inc(start_step, 1)
            dve.wait_ge(start_step, 7)
            tt(cHL[:, :, 1], ca[:, 0, :], f32(cHL[:, :, 0]), ALU.subtract).then_inc(ca_ready, 1)
            for m in range(NADA0):
                split_lo(Lin(m))

            def modulation(lo, hi, steps_before):
                M2 = MB[:, 2 * lo:2 * hi].rearrange("p (m two) -> p m two", two=2)
                dve.wait_ge(ada_done, hi)
                tt(mod[:, lo:hi], M2[:, :, 0], prm[:, C_ADA + lo:C_ADA + hi], ALU.add).then_inc(start_step, 1)
                dve.wait_ge(start_step, steps_before + 1)
                tt(mod[:, lo:hi], M2[:, :, 1], mod[:, lo:hi], ALU.add).then_inc(mod_ready, 1)

            def norm_gain(layer, ready):
                dve.wait_ge(mod_ready, ready)
                at = 3 * NB * layer + NB
                stt(gs[:, NB * layer:NB * layer + NB], mod[:, at:at + NB], 1.0,
                    prm[:, C_LN + NB * layer:C_LN + NB * layer + NB], ALU.add, ALU.mult).then_inc(start_step, 1)

            def h_of_x(layer, saved, steps_before):
                dve.wait_ge(start_step, steps_before)
                dve.wait_ge(rs_ready, 2 * layer + 2)
                dve.wait_ge(saved, 16)
                rs = sums_in[:].rearrange("p a t -> p (a t)")

                def lo(k):
                    dve.wait_ge(hh_ready, NB * layer + k + 1)
                    at = 3 * NB * layer + k
                    stt(hL[:, k], xT[:, k], mod[:, at:at + 1], f32(hH[:, k]), ALU.add, ALU.subtract
                        ).then_inc(hl_ready, 1)

                for k in range(NB):
                    at = NB * layer + k
                    stt(xT[:, k], xT[:, k], gs[:, at:at + 1], rs, ALU.mult, ALU.mult).then_inc(ht_ready, 1)
                    if k:
                        lo(k - 1)
                lo(NB - 1)

            modulation(0, NADA0, 7)
            norm_gain(0, 1)
            h_of_x(0, x_saved, 9)
            split_lo(Lin(U_A))
            split_lo(Lin(U_A + 1))
            nc.vector.memset(cx[:, 0:2], 0.0).then_inc(start_step, 1)
            dve.wait_ge(start_step, 10)

            with dve.Fori(0, NB) as i:
                u, n = Lin(U_A, i, 8), Lin(N_A, i, 4)

                def conv_done(k):
                    dve.wait_ge(conv_step, Lin(k, i, 4).v)

                def tap(w):
                    return prm[:, bass.ds(Lin(C_CONV + w * NB, i, 1).v, 1)]

                split_lo(u + 2)
                split_lo(u + 3)
                for half in range(2):
                    dve.wait_ge(filled[half], (n + 2).v)
                    tt(cx[:, 2 + half * HT:2 + (half + 1) * HT], cs[:, HALF[half]], PB[half][:], ALU.mult
                       ).then_inc(emptied[half], 1)
                split_lo(u + 4)
                dve.wait_ge(emptied[0], (n + 2).v)
                dve.wait_ge(emptied[1], (n + 2).v)
                ts(cv[:], cx[:, 0:T], tap(0), None, ALU.mult).then_inc(conv_step, 1)
                conv_done(1)
                stt(cv[:], cx[:, 1:T + 1], tap(1), cv[:], ALU.mult, ALU.add).then_inc(conv_step, 1)
                conv_done(2)
                stt(cv[:], cx[:, 2:T + 2], tap(2), cv[:], ALU.mult, ALU.add).then_inc(conv_step, 1)
                split_lo(u + 5)
                dve.wait_ge(emptied[0], (n + 3).v)
                dve.wait_ge(emptied[1], (n + 3).v)
                conv_done(3)
                tt(cv[:], cv[:], sz[:], ALU.mult).then_inc(conv_step, 1)
                split_lo(u + 6)
                split_lo(u + 7)
                conv_done(4)
                for half in range(2):
                    dve.wait_ge(filled[half], (n + 4).v)
                    tt(cv[:, HALF[half]], cv[:, HALF[half]], PB[half][:], ALU.mult).then_inc(emptied[half], 1)
                split_lo(u + 8)
                for half in range(2):
                    dve.wait_ge(y_hi, Lin(half + 1, i, 2).v)
                    tt(yL[:, bass.ds(i, 1), HALF[half]], cv[:, HALF[half]], f32(yH[:, bass.ds(i, 1), HALF[half]]),
                       ALU.subtract).then_inc(y_lo, 1)
                split_lo(u + 9)
            modulation(NADA0, NADA, 10)
            norm_gain(1, 2)

            def residual(j, n, dst, gate, loaded):
                for half in range(2):
                    dve.wait_ge(filled[half], (n + 1).v)
                    if half == 0:
                        loaded()
                    d = dst(HALF[half])
                    stt(d, PB[half][:], gate, d, ALU.mult, ALU.add).then_inc(emptied[half], 1)

            def mod_col(base, i, coef):
                return mod[:, bass.ds(Lin(base, i, coef).v, 1)]

            dve.wait_ge(mod_ready, 2)
            with dve.Fori(0, NB // 2) as i:
                for a in range(2):
                    residual(None, Lin(N_A2 + a, i, 2), lambda h, a=a: xa[a][:, h], mod_col(2 * NB + a, i, 2),
                             lambda a=a: dve.wait_ge(xa_in[a], Lin(16, i, 16).v))
                    split_lo(Lin(U_A2 + a + 2, i, 2))
            for half in range(2):
                dve.wait_ge(sgw_tr, half + 1)
                copy(WT[:, 4 * half:4 * half + 4, :], ZB[half][:].rearrange("p (g t) -> p g t", g=4)
                     ).then_inc(wt_ready, 1)
            dve.wait_ge(sgb_in, 16)
            for a in range(2):
                dve.wait_ge(xa_out[a], 16 * (NB // 2))

            with dve.Fori(0, G // 2) as i:
                for a in range(2):
                    u, n = Lin(U_B + 3 * a, i, 6), Lin(N_B + 3 * a, i, 6)
                    g = Lin(a, i, 2)
                    split_lo(u + 2)
                    for half in range(2):
                        dve.wait_ge(filled[half], (n + 2).v)
                        copy(us[:, HALF[half]], PB[half][:]).then_inc(emptied[half], 1)
                    split_lo(u + 3)
                    for half in range(2):
                        dve.wait_ge(v_turned, (g * 2 + (half + 1)).v)
                        copy(vn[:, 4 * half:4 * half + 4, :], ZB[half][:].rearrange("p (c d) -> p c d", c=4)
                             ).then_inc(vn_step, 1)
                    sq = vT[:].rearrange("p (c d) -> p c d", c=NC)
                    dve.wait_ge(vn_step, (g * 4 + 2).v)
                    tt(sq, vn[:], vn[:], ALU.mult).then_inc(vn_step, 1)
                    dve.wait_ge(vn_step, (g * 4 + 3).v)
                    nc.vector.tensor_reduce(ssq[:], sq, AX_X, ALU.add).then_inc(vn_step, 1)
                    dve.wait_ge(vn_step, (g * 4 + 4).v)
                    ts(ssq[:], ssq[:], 1.0 / P, EPS, ALU.mult, ALU.add).then_inc(ssq_ready, 1)
                    dve.wait_ge(rv_ready, (g + 1).v)
                    tt(vn[:], vn[:], rv[:].rearrange("p (c o) -> p c o", o=1).broadcast_to([P, NC, P]), ALU.mult
                       ).then_inc(vn_ready, 1)
                    dve.wait_ge(filled[1], (n + 3).v)
                    split_lo(u + 4)
                    for half in range(2):
                        dve.wait_ge(emptied[half], (n + 3).v)
                        tt(us[:, HALF[half]], us[:, HALF[half]], sz[:, HALF[half]], ALU.mult).then_inc(gate_step, 1)
                    for half in range(2):
                        dve.wait_ge(sg_filled, (g * 2 + (half + 1)).v)
                        v4 = cv[:, HALF[half]].rearrange("p (c t) -> p c t", c=4)
                        stt(v4, CB[half][:].rearrange("p (c t) -> p c t", c=4),
                            prm[:, bass.ds((g + C_SGN).v, 1)],
                            sgb[:, bass.ds(g.v, 1), :].broadcast_to([P, 4, P]), ALU.mult, ALU.add).then_inc(gate_step, 1)
                    for half in range(2):
                        dve.wait_ge(gate_step, (g * 4 + (half + 3)).v)
                        tt(cv[:, HALF[half]], cv[:, HALF[half]], us[:, HALF[half]], ALU.mult).then_inc(y_prod, 1)
                    for half in range(2):
                        dve.wait_ge(y_hi, (g * 2 + (2 * NB + half + 1)).v)
                        tt(yL[:, bass.ds(g.v, 1), HALF[half]], cv[:, HALF[half]],
                           f32(yH[:, bass.ds(g.v, 1), HALF[half]]), ALU.subtract).then_inc(y_lo, 1)
            dve.wait_ge(x1_in, 16)
            with dve.Fori(0, NB // 2) as i:
                for a in range(2):
                    residual(None, Lin(N_B2 + a, i, 2),
                             lambda h, a=a: xT[:, bass.ds(Lin(a, i, 2).v, 1), h], mod_col(2 * NB + a, i, 2),
                             lambda: None)
                    split_lo(Lin(U_B2 + a + 2, i, 2))
            for par in range(2):
                for head in range(2):
                    for prt in range(2):
                        last = nc.vector.memset(Q[par][head][prt][ROWS[1 - head], :].bitcast(F32), 0.0)
            last.then_inc(q_zeroed, 1)
            h_of_x(1, y_saved, 12)

            def negated(b, a):
                s = the_step(a)
                dve.wait_ge(z_copied, upto(b, a).v)
                if upto(b, a - 3).positive:
                    dve.wait_ge(sp_lo, upto(b, a - 3).v)
                ts(e[a % 3][:, s["c0"]:HT].bitcast(U32), zs[a % 4][:, s["c0"]:HT].bitcast(U32), SIGN, None,
                   ALU.bitwise_or).then_inc(e_neg, 1)

            def softplus(b, a):
                s = the_step(a)
                v = e[a % 3][:, s["c0"]:HT]
                dve.wait_ge(e_ln, upto(b, a).v)
                stt(v, zs[a % 4][:, s["c0"]:HT], 0.0, v, ALU.max, ALU.add
                    ).then_inc(sp_raw if s["diagonal"] else sp_ready, 1)
                if s["diagonal"]:
                    dve.wait_ge(sp_raw, diagonals_upto(b, a).v)
                    d = e[a % 3][:, s["c0"]:s["c0"] + P]
                    tt(d, d, strict[:], ALU.mult).then_inc(sp_ready, 1)
                dve.wait_ge(sp_ready, upto(b, a).v)
                if upto(b, a - 2).positive:
                    if the_step(a - 2)["last"]:
                        dve.wait_ge(u_done, upto(b, a - 2).v)
                    else:
                        dve.wait_ge(sp_free, lowers_upto(b, a - 2).v)
                copy(spH[:, a % 2, s["c0"]:HT], v).then_inc(sp_hi, 1)

            def exponent(b, a):
                s = the_step(a)
                v = zs[a % 4][:, s["c0"]:HT]
                dve.wait_ge(u_done, upto(b, a).v)
                tt(v, v, CB[s["chain"] % 2][:, s["c0"]:HT], ALU.subtract
                   ).then_inc(arg_raw if s["diagonal"] else arg_ready, 1)
                if s["diagonal"]:
                    dve.wait_ge(arg_raw, diagonals_upto(b, a).v)
                    d = zs[a % 4][:, s["c0"]:s["c0"] + P]
                    tt(d, d, cap[:], ALU.min).then_inc(arg_ready, 1)

            def gated(b, par, a):
                s, own = the_step(a), b + a // STEPS
                mine, sums = ROWS[s["head"]], own * 4 + (s["chain"] + 1)
                dve.wait_ge(o_shifted, sums.v)
                tt(osh[mine, :], OB[s["chain"] % 2][mine, :], osh[mine, :], ALU.add).then_inc(o_sum, 1)
                dve.wait_ge(o_sum, sums.v)
                dve.wait_ge(gz_ready, (own * 2 + 2).v)
                d = gz[par][mine, HALF[s["half"]]]
                tt(d, d, osh[mine, :], ALU.mult).then_inc(y_ready, 1)

            def pair(p, par, first, end):
                b = p - 1
                n = p * C_FILLS + N_C
                for t in slots(end):
                    if first <= t + 2 < end:
                        negated(b, t + 2)
                    if first <= t + 1 < end:
                        softplus(b, t + 1)
                    if first <= t < end:
                        exponent(b, t)
                    if first <= t - 3 < end and the_step(t - 3)["last"]:
                        gated(b, par_of(par, t - 3), t - 3)
                    if end == STEPS:
                        continue
                    if t in (9, 12, 15, 18):
                        which, half = divmod((9, 12, 15, 18).index(t), 2)
                        h = HALF[half]
                        r = (qr, kr)[which]
                        gain = (qn_scaled[:], prm[:, C_KN:C_KN + 1])[which]
                        dve.wait_ge(qk_rs, (p * 4 + (2 * which + half + 1)).v)
                        stt(r[:, h], r[:, h], gain, sums_in[:, half], ALU.mult, ALU.mult).then_inc(qk_n, 1)
                        dve.wait_ge(qk_n, (p * 4 + (2 * which + half + 1)).v)
                        if which == 0:
                            for head in range(2):
                                copy(Q[par][head][0][ROWS[head], h], r[ROWS[head], h]).then_inc(q_hi, 1)
                            for head in range(2):
                                dve.wait_ge(q_hi, (p * 4 + (2 * half + head + 1)).v)
                                tt(Q[par][head][1][ROWS[head], h], r[ROWS[head], h],
                                   f32(Q[par][head][0][ROWS[head], h]), ALU.subtract).then_inc(q_lo, 1)
                        else:
                            copy(K[par][0][:, h], r[:, h]).then_inc(k_hi, 1)
                    if t in (20, 23):
                        half = (20, 23).index(t)
                        d = gz[par][:, HALF[half]]
                        dve.wait_ge(gz_sig, (p * 2 + (half + 1)).v)
                        dve.wait_ge(emptied[half], (n + 6).v)
                        tt(d, d, sums_in[:, half], ALU.mult).then_inc(gz_ready, 1)
                    if t in (21, 23):
                        half = (21, 23).index(t)
                        dve.wait_ge(v_hi, (p * 2 + (half + 1)).v)
                        src = PB[half][:].rearrange("p (j h d) -> p j h d", j=4, h=2)
                        blocks = slice(4 * half, 4 * half + 4)
                        tt(V[par][:, blocks, 0, DH:P], src[:, :, 0, :], f32(V[par][:, blocks, 0, 0:DH]), ALU.subtract)
                        tt(V[par][:, blocks, 1, 0:DH], src[:, :, 1, :], f32(V[par][:, blocks, 1, DH:P]), ALU.subtract
                           ).then_inc(emptied[half], 1)

            pair(Lin(0), 0, STEPS, 2 * STEPS)
            pair(Lin(1), 1, 0, 2 * STEPS)
            with dve.Fori(0, NP // 2 - 1) as i:
                pair(Lin(2, i, 2), 0, -STEPS, 2 * STEPS)
                pair(Lin(3, i, 2), 1, -STEPS, 2 * STEPS)
            pair(Lin(NP), 0, -STEPS, STEPS)

            for k in range(NP):
                dve.wait_ge(hh_ready, 2 * NB + k + 1)
                tt(hL[:, k], ys[:, k % 4], f32(hH[:, k]), ALU.subtract).then_inc(hl_ready, 1)
            for j in range(NB):
                residual(None, Lin(N_D + j), lambda h, j=j: xt[j % 2][:, h], mod[:, 5 * NB + j:5 * NB + j + 1],
                         lambda j=j: dve.wait_ge(xt_in[j % 2], 16 * (j // 2 + 1)))
                if j + 2 < NB:
                    split_lo(Lin(U_D + j + 2))

        @block.gpsimd
        def _(pool):
            g = nc.gpsimd

            def rows(at, src):
                pool.dma_start(prm_rows[at:at + src.shape[0], 0:src.shape[1]], src).then_inc(prm_in, 16)

            rows(C_C, c.rearrange("o (k p) -> (o k) p", p=P))
            rows(C_LN, ln_g.rearrange("l (k p) -> (l k) p", p=P))
            rows(C_ADA, ada_b.rearrange("l (k p) -> (l k) p", p=P))
            rows(C_CONV, conv_w[0].rearrange("w (k p) -> (w k) p", p=P))
            rows(C_SGN, sg_norm[0])
            for at, w in ((C_QN, q_norm), (C_KN, k_norm)):
                for head in range(2):
                    pool.dma_start(prm_rows[at:at + 1, head * DH:(head + 1) * DH], w).then_inc(prm_in, 16)

            steps_of = [0]

            def own(instruction):
                instruction.then_inc(const_step, 1)
                steps_of[0] += 1

            def own_wait():
                pool.wait_ge(const_step, steps_of[0])

            own(g.memset(ones[:], 1.0))
            own(g.memset(cap[:], 0.0))
            own_wait()
            g.affine_select(out=ident[:], in_=cap[:], compare_op=ALU.not_equal, fill=1.0, base=0,
                            pattern=[[-1, P]], channel_multiplier=1).then_inc(consts, 1)
            own(g.affine_select(out=U_f[:], in_=ones[:], compare_op=ALU.is_ge, fill=0.0, base=0,
                                pattern=[[-1, P]], channel_multiplier=1))
            own(g.affine_select(out=strict[:], in_=ones[:], compare_op=ALU.is_gt, fill=0.0, base=0,
                                pattern=[[1, P]], channel_multiplier=-1))
            own_wait()
            own(g.affine_select(out=cap[:], in_=ones[:], compare_op=ALU.is_gt, fill=-200.0, base=0,
                                pattern=[[1, P]], channel_multiplier=-1))
            own(g.memset(minus_half[:], -0.5))
            own_wait()
            g.memset(eps_t[:], EPS).then_inc(consts, 1)

            pool.wait_ge(emptied[0], NC)
            pool.wait_ge(emptied[1], NC)
            pool.dma_start(xd0.rearrange("k p t -> p k t"), xT[:]).then_inc(x_saved, 16)
            pool.wait_ge(x_saved, 16)
            pool.wait_ge(hl_ready, NB)

            def xa_load(j, at):
                s = j.base % 2
                pool.dma_start(xa[s][:], at).then_inc(xa_in[s], 16)

            xa_load(Lin(0), xd0[0])
            xa_load(Lin(1), xd0[1])
            pool.wait_ge(y_lo, 2 * NB)
            pool.dma_start(vn[:], sg_w[0].rearrange("g t s -> t g s")).then_inc(sgw_in, 16)
            pool.dma_start(sgb[:].rearrange("p g t -> p (g t)"),
                           sg_b.rearrange("o g t -> o (g t)").partition_broadcast(P)).then_inc(sgb_in, 16)
            pool.wait_ge(sgw_in, 16)
            g.affine_select(out=vn[:], in_=vn[:], compare_op=ALU.is_ge, fill=0.0, base=0,
                            pattern=[[0, G], [-1, P]], channel_multiplier=1).then_inc(sgw_masked, 1)

            def xa_store(n, at, s, turns):
                pool.wait_ge(emptied[0], (n + 1).v)
                pool.wait_ge(emptied[1], (n + 1).v)
                pool.dma_start(at, xa[s][:]).then_inc(xa_out[s], 16)

            with pool.Fori(0, NB // 2 - 1) as i:
                for a in range(2):
                    xa_store(Lin(N_A2 + a, i, 2), xd1[bass.ds(Lin(a, i, 2).v, 1)], a, i)
                    pool.wait_ge(xa_out[a], Lin(16, i, 16).v)
                    pool.dma_start(xa[a][:], xd0[bass.ds(Lin(a + 2, i, 2).v, 1)]).then_inc(xa_in[a], 16)
            for a in range(2):
                xa_store(Lin(N_A2 + NB - 2 + a), xd1[NB - 2 + a], a, 0)

            with pool.Fori(0, G) as i:
                pool.wait_ge(ssq_ready, Lin(1, i, 1).v)
                g.tensor_tensor(rv[:], ssq[:], minus_half[:], ALU.pow).then_inc(rv_ready, 1)
            pool.wait_ge(y_lo, 4 * NB)
            for a in range(2):
                pool.wait_ge(xa_out[a], 16 * (NB // 2))
            pool.dma_start(xT[:], xd1.rearrange("k p t -> p k t")).then_inc(x1_in, 16)
            pool.wait_ge(emptied[0], N_C)
            pool.wait_ge(emptied[1], N_C)
            pool.dma_start(xd2.rearrange("k p t -> p k t"), xT[:]).then_inc(y_saved, 16)


            def minus(o, i, hi):
                return g.tensor_tensor(o, i, hi.bitcast(F32), ALU.subtract)

            def softplus_lo(b, a):
                v = slice(the_step(a)["c0"], HT)
                pool.wait_ge(sp_hi, upto(b, a).v)
                minus(spL[:, a % 2, v], e[a % 3][:, v], spH[:, a % 2, v]).then_inc(sp_lo, 1)

            def weight_lo(b, a):
                v = slice(the_step(a)["c0"], HT)
                pool.wait_ge(p_hi, upto(b, a).v)
                minus(pL[:, v], zs[a % 4][:, v], pH[:, v]).then_inc(p_lo, 1)

            def pair(p, par, first, end):
                b = p - 1
                for t in slots(end):
                    if first <= t - 1 < end:
                        weight_lo(b, t - 1)
                    if first <= t + 1 < end:
                        softplus_lo(b, t + 1)
                    if first <= t - 3 < end and t % STEPS == 2:
                        own = b + (t - 3) // STEPS
                        pool.wait_ge(y_ready, (own * 4 + 4).v)
                        pool.dma_start(yd[bass.ds(own.v, 1)] if own.coef else yd[own.base],
                                       gz[par_of(par, t - 3)][:]).then_inc(y_saved, 16)
                    if end == STEPS:
                        continue
                    if t in (15, 18):
                        half = (15, 18).index(t)
                        h = HALF[half]
                        pool.wait_ge(k_hi, (p * 2 + (half + 1)).v)
                        minus(K[par][1][:, h], kr[:, h], K[par][0][:, h]).then_inc(k_lo, 1)
                    if t in SPLIT_AT:
                        kind = SPLIT_AT.index(t)
                        u = p * 4 + (U_C + kind + 2)
                        pool.wait_ge(w_hi, (u + 1).v)
                        minus(wL[:, kind % 2], raw[:, kind % 2], wH[:, kind % 2]).then_inc(w_lo, 1)

            pair(Lin(0), 0, STEPS, 2 * STEPS)
            pair(Lin(1), 1, 0, 2 * STEPS)
            with pool.Fori(0, NP // 2 - 1) as i:
                pair(Lin(2, i, 2), 0, -STEPS, 2 * STEPS)
                pair(Lin(3, i, 2), 1, -STEPS, 2 * STEPS)
            pair(Lin(NP), 0, -STEPS, STEPS)

            pool.wait_ge(y_saved, 16 * (NP + 1))
            for k in range(NP):
                if k >= 4:
                    pool.wait_ge(hl_ready, 2 * NB + k - 3)
                pool.dma_start(ys[:, k % 4], yd[k]).then_inc(ys_in[k % 4], 16)
                if k < 2:
                    pool.dma_start(xt[k][:], xd2[k]).then_inc(xt_in[k], 16)
            for j in range(NB):
                s = j % 2
                if j + 2 < NB:
                    pool.wait_ge(t_filled, 2 * j + 2)
                    pool.dma_start(xt[s][:], xd2[j + 2]).then_inc(xt_in[s], 16)
                pool.wait_ge(t_out, 2 * j + 2)
                pool.dma_start(out[0, :, j * P:(j + 1) * P].rearrange("(c p) d -> p c d", p=P), ot[s]
                               ).then_inc(stored[s], 16)
            for s in range(2):
                pool.wait_ge(stored[s], 16 * (NB // 2))


_INS = ["x", "c", "ln_g", "ada_w", "ada_b", "w_in_ab", "conv_w", "sg_norm", "sg_w", "sg_b", "w_out_ab", "w_in_c",
        "q_norm", "k_norm", "w_out_c"]


def kernel(**inputs):
    import numpy as _np
    import concourse.bacc as _bacc
    from concourse.bass_utils import run_bass_kernel_spmd as _run

    nc = _bacc.Bacc("TRN2", target_bir_lowering=False, num_devices=1)
    arrays, args = {}, []
    for name in _INS:
        a = _np.ascontiguousarray(inputs[name])
        arrays[f"in_{name}"] = a
        args.append(nc.dram_tensor(f"in_{name}", a.shape, mybir.dt.from_np(a.dtype), kind="ExternalInput").ap())
    shape = tuple(inputs["x"].shape)
    args.append(nc.dram_tensor("out_x", shape, F32, kind="ExternalOutput").ap())
    hybrid_trunk(nc, *args)
    r = _run(nc, [arrays], core_ids=[0])
    return r.results[0]["out_x"]
```

```python
from contextlib import ExitStack

import concourse.bass as bass
from concourse import mybir

F32 = mybir.dt.float32
F32R = mybir.dt.float32r
U32 = mybir.dt.uint32
ALU = mybir.AluOpType
ACT = mybir.ActivationFunctionType
AX_X = mybir.AxisListType.X

P = 128
SIGN = 0x80000000
MASKED = -2.0 ** 20
LN_EXP_SET = "natural_log_exp_and_others"
SILU_SET = "silu_and_others"


class Lin:

    def __init__(self, base, turn=0, coef=0):
        self.base, self.turn, self.coef = base, turn, coef

    def __add__(self, n):
        return Lin(self.base + n, self.turn, self.coef)

    def __sub__(self, n):
        return self + -n

    def __mul__(self, n):
        return Lin(self.base * n, self.turn, self.coef * n)

    def half(self):
        assert self.coef % 2 == 0
        return Lin(self.base // 2, self.turn, self.coef // 2)

    @property
    def v(self):
        return self.turn * self.coef + self.base if self.coef else self.base

    @property
    def positive(self):
        return self.base > 0


def hybrid_trunk(nc, x, c, ln_g, ada_w, ada_b, w_in_ab, conv_w, sg_norm, sg_w, sg_b,
                 w_out_ab, w_in_c, q_norm, k_norm, w_out_c, out):
    _, T, D = x.shape
    HT = T // 2
    NB = D // P
    NC = T // P
    CONV_W = conv_w.shape[1]
    G = sg_w.shape[1]
    DH = q_norm.shape[1]
    NP = D // (2 * DH)
    EPS = 1e-6
    NADA = 2 * 3 * NB
    NADA0 = 2 * NB
    assert T == 1024 and D == 1024 and DH == 64 and G == NB

    U_A = 0
    U_A2 = U_A + 4 * NB
    U_B = U_A2 + NB
    U_B2 = U_B + 3 * G
    U_C = U_B2 + NB
    U_D = U_C + 4 * NP
    U_LAST = U_D + NB
    N_A = NC
    N_A2 = N_A + 4 * NB
    N_B = N_A2 + NB
    N_B2 = N_B + 3 * G
    N_C = N_B2 + NB
    C_FILLS = 7
    N_D = N_C + C_FILLS * NP
    STEPS = 24

    chains = [(head, half) for head in range(2) for half in range(2)]
    steps = []
    for ci, (head, half) in enumerate(chains):
        last_block = 4 * half + 3
        for j in range(last_block, -1, -1):
            steps.append(dict(chain=ci, head=head, half=half, j=j, c0=max(0, P * j - HT * half),
                              diagonal=j >= 4 * half, first=j == last_block, last=j == 0))
    assert len(steps) == STEPS

    with ExitStack() as ctx:
        def sb(name, shape, dt=F32):
            return ctx.enter_context(nc.sbuf_tensor(name, shape, dt))

        def sem(name):
            return ctx.enter_context(nc.semaphore(name))

        def dram(name, shape):
            return nc.dram_tensor(name, shape, F32, kind="Internal").ap()

        xd0, xd1, xd2 = (dram(f"x_t{i}", [NB, P, T]) for i in range(3))
        yd = dram("y_t", [NP, P, T])

        with ExitStack() as start:
            xn, x_raw, start_R2, _, _, ada_acc, sq_sum = (
                start.enter_context(nc.sbuf_tensor(name, shape, F32)) for name, shape in (
                    ("xn", [P, NB, T]), ("x_raw", [P, NC, D]), ("start_R2", [P, 16 * T]),
                    ("start_raw", [P, 2 * T]), ("start_wH", [P, 2 * T]), ("ada_acc", [P, 2 * T]),
                    ("sq_sum", [P, 2, HT])))
        ada_raw = start_R2[:].rearrange("p (k n) -> p k n", k=NB)
        h_f = start_R2[:, 0:NB * T].rearrange("p (k t) -> p k t", k=NB)
        hH = sb("hH", [P, NB, T], F32R)
        hL = sb("hL", [P, NB, T], F32R)
        R2 = sb("R2", [P, 16 * T], F32R)
        yH = R2[:, 0:8 * T].rearrange("p (k t) -> p k t", k=NB)
        yL = R2[:, 8 * T:16 * T].rearrange("p (k t) -> p k t", k=NB)
        QP = 6 * T
        Q, K, KL = ([[R2[:, par * QP + (3 * head + part) * T:par * QP + (3 * head + part + 1) * T]
                      for head in range(2)] for par in range(2)] for part in range(3))
        V = [R2[:, 12 * T + par * 2 * T:12 * T + (par + 1) * 2 * T].rearrange(
            "p (j h d) -> p j h d", j=NC, h=2) for par in range(2)]
        raw = sb("raw", [P, 2, NB, P])
        wH = sb("wH", [P, 2, NB, P], F32R)
        wL = sb("wL", [P, 2, NB, P], F32R)
        spH = sb("spH", [P, 2, HT], F32R)
        spL = sb("spL", [P, 2, HT], F32R)
        pH = sb("pH", [P, HT], F32R)
        pL = sb("pL", [P, HT], F32R)
        sums_in = sb("sums_in", [P, 2, HT])
        FA = sb("FA", [P, 8 * T + 8])
        xT = FA[:, 0:8 * T].rearrange("p (k t) -> p k t", k=NB)
        cs = FA[:, 0:T]
        cx = FA[:, T:2 * T + 2]
        cv = FA[:, 2 * T + 4:3 * T + 4]
        sz = FA[:, 3 * T + 4:4 * T + 4]
        vT = cs
        vn = FA[:, T:2 * T].rearrange("p (c d) -> p c d", c=NC)
        us = FA[:, 4 * T + 4:5 * T + 4]
        xa = [FA[:, (4 + s) * T + 4:(5 + s) * T + 4] for s in range(2)]
        WT = FA[:, 6 * T + 4:7 * T + 4].rearrange("p (g t) -> p g t", g=G)
        sgb = FA[:, 7 * T + 4:8 * T + 4].rearrange("p (g t) -> p g t", g=G)
        zs = [FA[:, s * HT:(s + 1) * HT] for s in range(4)]
        e = [FA[:, (4 + s) * HT:(5 + s) * HT] for s in range(3)]
        osh = FA[:, 7 * HT:8 * HT]
        gz = [FA[:, (4 + s) * T:(5 + s) * T] for s in range(2)]
        qr = FA[:, 6 * T:7 * T]
        kr = FA[:, 7 * T:8 * T]
        y_in = x_raw[:]
        xo = [start_R2[:, s * T:(s + 1) * T] for s in (0, 1, 2, 3, 4, 5, 12, 13)]
        ot = [FA[:, c * T:(c + 1) * T] for c in range(NC)]

        ident = sb("ident", [P, P])
        ones = sb("ones", [P, P])
        pair_ones = sb("pair_ones", [P, P])
        mask = sb("mask", [P, P])
        mask_r = sb("mask_r", [P, P], F32R)
        ident_r = sb("ident_r", [P, P], F32R)
        ada_in = [FA[:, (6 + s) * T + 4:(7 + s) * T + 4] for s in range(2)]
        ada_sum = sums_in[:].rearrange("p a t -> p (a t)")
        U_f = sb("U_f", [P, P])
        U_r = sb("U_r", [P, P], F32R)
        Uc_r = sb("Uc_r", [P, P], F32R)
        prm_rows = sb("prm_rows", [P, P])
        prm = sb("prm", [P, P])
        C_C, C_LN, C_ADA = 0, NB, 3 * NB
        C_CONV = C_ADA + NADA
        C_SGN = C_CONV + CONV_W * NB
        C_QN = C_SGN + G
        C_KN = C_QN + 1
        NPRM = C_KN + 1
        mod = sb("mod", [P, NADA])
        gs = sb("gs", [P, 2 * NB])
        ca = sb("ca", [P, 3, NB])

        ssq = sb("ssq", [P, NC])
        rv = sb("rv", [P, NC])
        minus_half = sb("minus_half", [P, NC])
        eps_t = sb("eps_t", [P, 1])
        qn_scaled = sb("qn_scaled", [P, 1])

        def bank(name):
            return ctx.enter_context(nc.psum_tensor(name, [P, HT], F32))

        PB = [bank("P0"), bank("P1")]
        ZB = [bank("Z0"), bank("Z1")]
        CB = [bank("C0"), bank("C1")]
        OB = [bank("O0"), bank("O1")]
        MB = OB[0]

        raw_in = [sem(f"raw_in{s}") for s in range(2)]
        w_hi, w_lo = sem("w_hi"), sem("w_lo")
        filled = [sem(f"filled{b}") for b in range(2)]
        emptied = [sem(f"emptied{b}") for b in range(2)]
        x_in = [sem(f"x_in{s}") for s in range(NC // 2)]
        ada_in0 = [sem(f"ada_in0_{k}") for k in range(NB)]
        ada_in1 = [sem(f"ada_in1_{s}") for s in range(2)]
        ada_used0 = sem("ada_used0")
        ada_used = sem("ada_used")
        ada_done = sem("ada_done")
        mod_ready = sem("mod_ready")
        prm_in, prm_tr, prm_ready = sem("prm_in"), sem("prm_tr"), sem("prm_ready")
        consts = sem("consts")
        ce, xn_ready, xn_ready_p = sem("ce"), sem("xn_ready"), sem("xn_ready_p")
        sq_ready, sq_added, sum_done, rs_ready = (sem(n) for n in ("sq_ready", "sq_added", "sum_done", "rs_ready"))
        ht_ready, hh_ready = sem("ht_ready"), sem("hh_ready")
        hl_ready = [sem("hl_even"), sem("hl_odd")]
        x_saved = sem("x_saved")
        y_hi, y_lo = sem("y_hi"), sem("y_lo")
        xa_in = [sem(f"xa_in{s}") for s in range(2)]
        xa_out = [sem(f"xa_out{s}") for s in range(2)]
        sgw_in, sgw_masked, sgw_tr, wt_ready = sem("sgw_in"), sem("sgw_masked"), sem("sgw_tr"), sem("wt_ready")
        v_turned, ssq_ready, rv_ready, vn_ready = sem("v_turned"), sem("ssq_ready"), sem("rv_ready"), sem("vn_ready")
        sg_filled = sem("sg_filled")
        x1_in = [sem(f"x1_in{s}") for s in range(2)]
        y_prod, conv_step, gate_step, vn_step = sem("y_prod"), sem("conv_step"), sem("gate_step"), sem("vn_step")
        start_step, rms_ln, k_zeroed = sem("start_step"), sem("rms_ln"), sem("k_zeroed")
        gz_exp, e_exp, sp_free = (sem(n) for n in ("gz_exp", "e_exp", "sp_free"))
        o_sum, const_step, sgb_in = sem("o_sum"), sem("const_step"), sem("sgb_in")
        qk_sq, qk_rs, qk_n = sem("qk_sq"), sem("qk_rs"), sem("qk_n")
        q_hi, q_lo, k_hi, k_lo, v_hi = (sem(n) for n in ("q_hi", "q_lo", "k_hi", "k_lo", "v_hi"))
        gz_ln, gz_sig, gz_ready = sem("gz_ln"), sem("gz_sig"), sem("gz_ready")
        z_filled, z_copied, e_neg, e_ln = sem("z_filled"), sem("z_copied"), sem("e_neg"), sem("e_ln")
        sp_ready, sp_hi, sp_lo = sem("sp_ready"), sem("sp_hi"), sem("sp_lo")
        u_done, arg_ready, w_ready = sem("u_done"), sem("arg_ready"), sem("w_ready")
        p_hi, p_lo, pv_done = sem("p_hi"), sem("p_lo"), sem("pv_done")
        o_shifted, y_ready = sem("o_shifted"), sem("y_ready")
        y_saved = sem("y_saved")
        YS = NP - 2
        ys_in = [sem(f"ys_in{k}") for k in range(YS)]
        xo_in = [sem(f"xo_in{j}") for j in range(NB)]
        y7_hi, y7_lo = sem("y7_hi"), sem("y7_lo")
        d_filled, d_out = sem("d_filled"), sem("d_out")
        t_filled = sem("t_filled")
        t_out = [sem(f"t_out{s}") for s in range(2)]
        stored = sem("stored")

        HALF = [slice(0, HT), slice(HT, T)]
        ROWS = [slice(0, DH), slice(DH, P)]
        SUMS_AT, TURN_AT, SPLIT_AT = (8, 11, 14, 17), (20, 23), (4, 10, 16, 21)
        PRM_AT = 3
        XN_DVE = 5
        LOWERS = sum(not s["last"] for s in steps)

        def the_step(a):
            return steps[a % STEPS]

        def upto(b, a):
            return b * STEPS + (a + 1)

        def lowers_upto(b, a):
            return (b + a // STEPS) * LOWERS + sum(not s["last"] for s in steps[:a % STEPS + 1])

        def par_of(par, a):
            return 1 - par if 0 <= a < STEPS else par

        def slots(end):
            return range(STEPS + OUT_FROM) if end == STEPS else range(STEPS)

        OUT_FROM = 4
        out_parts = [(half, k, kind) for half in range(2) for k in range(NP - 1) for kind in range(3)]
        OUT_THIRD = len(out_parts) // 3
        OUT_SPLIT = {1: (0, 1), 2: (2, 3), 3: (4, 5, 6)}



        def cols(w, at, n=P):
            return w[:, bass.ds(at, n)].rearrange("(k p) n -> p k n", p=P)

        W_AB, W_C, W_OC = w_in_ab[0], w_in_c[0], w_out_c[0]
        W_OA, W_OB = w_out_ab[0, 0:D, :], w_out_ab[0, D:2 * D, :]
        A_B, A_C, A_X, A_Z, B_U, B_V, B_Z = (D * i for i in range(7))

        block = ctx.enter_context(nc.Block())

        @block.sync
        def _(sp):
            def load_unit(u, w, at):
                src = cols(w, at if isinstance(at, int) else sp.snap(at))
                slot = u.base % 2
                sp.wait_ge(w_hi, (u - 1).v)
                sp.wait_ge(w_lo, (u - 1).v)
                sp.dma_start(raw[:, slot], src).then_inc(raw_in[slot], 16)

            AHEAD = 3
            arrived = x_in + ada_in0
            for n in range(len(arrived)):
                if n >= AHEAD:
                    sp.wait_ge(arrived[n - AHEAD], 16)
                if n < NC // 2:
                    src = x[0, 2 * n * P:(2 * n + 2) * P, :].rearrange("(c t) n -> t c n", t=P)
                    sp.dma_start(x_raw[:, 2 * n:2 * n + 2, :], src).then_inc(x_in[n], 16)
                else:
                    k = n - NC // 2
                    sp.dma_start(ada_raw[:, k], ada_w[0, k * P:(k + 1) * P, 0:2 * D]).then_inc(ada_in0[k], 16)
            for m, w_at in enumerate((A_C, A_X)):
                sp.dma_start(raw[:, m], cols(W_AB, w_at)).then_inc(raw_in[m], 16)

            for a in range(2):
                for k, w_at in enumerate((A_C, A_X, A_Z, A_B)):
                    if a or k >= 2:
                        load_unit(Lin(U_A + 4 * a + k), W_AB, a * P + w_at)
            with sp.Fori(2, NB // 2 + 1) as i:
                for a in range(2):
                    for k, w_at in enumerate((A_C, A_X, A_Z, A_B)):
                        load_unit(Lin(U_A - 8 + 4 * a + k, i, 8), W_AB, i * (2 * P) + (w_at + (a - 2) * P))

            def load_pairs(u0, w):
                with sp.Fori(0, NB // 2) as i:
                    for a in range(2):
                        load_unit(Lin(u0 + a, i, 2), w, i * (2 * P) + a * P)

            load_pairs(U_A2, W_OA)
            with sp.Fori(0, G // 2) as i:
                for a in range(6):
                    w_at = (B_V, B_U, B_Z)[a % 3]
                    load_unit(Lin(U_B + a, i, 6), W_AB, i * (2 * P) + (w_at + (a // 3) * P))
            load_pairs(U_B2, W_OB)
            with sp.Fori(0, NP) as i:
                for a in range(4):
                    load_unit(Lin(U_C + a, i, 4), W_C, i * P + a * D)
            for j in range(4):
                load_unit(Lin(U_D + j), W_OC, j * P)
            for half in range(2):
                sp.wait_ge(filled[half], N_C + (NP - 1) * C_FILLS + 6)
            sp.wait_ge(y_saved, 16 * (NB + YS))
            for k in range(YS):
                sp.dma_start(y_in[:, k], yd[k]).then_inc(ys_in[k], 16)
            sp.wait_ge(pv_done, (NP - 1) * STEPS)
            for j in range(NB):
                sp.dma_start(xo[j], xd2[j]).then_inc(xo_in[j], 16)
            for j in range(4, NB):
                load_unit(Lin(U_D + j), W_OC, j * P)
            sp.wait_ge(w_hi, U_LAST - 1)
            sp.wait_ge(w_lo, U_LAST - 1)
            sp.dma_start(raw[:, 0], W_OC[(NP - 1) * P:NP * P, :].rearrange("p (j n) -> p j n", n=P)
                         ).then_inc(raw_in[0], 16)
            for ch in range(NC):
                for s in range(2):
                    sp.wait_ge(t_out[s], ch + 1)
                sp.dma_start(out[0, ch * P:(ch + 1) * P, :], ot[ch]).then_inc(stored, 16)
            sp.wait_ge(stored, 16 * NC)

        @block.tensor
        def _(pe):
            mm, turn = nc.tensor.matmul, nc.tensor.transpose

            def products(half, slot, H, L, ks):
                h, acc = HALF[half], PB[half][:]
                for k in ks:
                    mm(acc, wH[:, slot, k], H[:, k, h], start=k == 0, stop=False)
                    mm(acc, wH[:, slot, k], L[:, k, h], start=False, stop=False)
                    last = mm(acc, wL[:, slot, k], H[:, k, h], start=False, stop=k == NB - 1)
                return last

            def wait_split(u):
                pe.wait_ge(w_hi, (u + 1).v)
                pe.wait_ge(w_lo, (u + 1).v)

            def unit(u, n, H, L):
                wait_split(u)
                for half in range(2):
                    pe.wait_ge(emptied[half], n.v)
                    products(half, u.base % 2, H, L, range(NB)).then_inc(filled[half], 1)

            def first_unit(u, n, H, L, hi_there, lo_there):
                wait_split(u)
                slot = u.base % 2
                for k in range(NB):
                    hi_there(k)
                    for half in range(2):
                        if k == 0:
                            pe.wait_ge(emptied[half], n.v)
                        h, acc = HALF[half], PB[half][:]
                        mm(acc, wH[:, slot, k], H[:, k, h], start=k == 0, stop=False)
                        mm(acc, wL[:, slot, k], H[:, k, h], start=False, stop=False)
                for k in range(NB):
                    lo_there(k)
                    for half in range(2):
                        last = mm(PB[half][:], wH[:, slot, k], L[:, k, HALF[half]], start=False, stop=k == NB - 1)
                        if k == NB - 1:
                            last.then_inc(filled[half], 1)

            def h_hi_there(layer):
                return lambda k: pe.wait_ge(hh_ready, NB * layer + k + 1)

            def h_lo_there(layer):
                return lambda k: pe.wait_ge(hl_ready[k % 2], NB // 2 * layer + k // 2 + 1)

            def y_hi_there(base):
                return lambda k: pe.wait_ge(y_hi, base + 2 * (k + 1))

            def y_lo_there(base):
                return lambda k: pe.wait_ge(y_lo, base + 2 * (k + 1))

            def ada_columns(done, src, dst):
                pe.wait_ge(*done)
                for m in range(src.shape[1] // P):
                    last = mm(dst(m), src[:, m * P:(m + 1) * P], ones[:, 0:1], start=True, stop=True)
                last.then_inc(ada_done, 1)

            def channel_sums(layer, k, first=False, last=False):
                for half in range(2):
                    pe.wait_ge(sq_ready, (k * 2 + (2 * NB * layer + half + 1)).v)
                    mm(CB[half][:], ones[:], sums_in[:, half], start=first, stop=last).then_inc(sum_done, 1)

            pe.wait_ge(consts, 1)
            for ch in range(NC):
                pe.wait_ge(x_in[ch // 2], 16)
                for half in range(2):
                    if ch:
                        pe.wait_ge(emptied[half], ch)
                    for k in range(4):
                        last = turn(PB[half][:, k * P:(k + 1) * P], x_raw[:, ch, (4 * half + k) * P:(4 * half + k + 1) * P], ident[:])
                    last.then_inc(filled[half], 1)
                if ch == PRM_AT:
                    pe.wait_ge(prm_in, 16 * 9)
                    turn(ZB[0][:, 0:NPRM], prm_rows[0:NPRM, :], ident[0:NPRM, 0:NPRM]).then_inc(prm_tr, 1)
            pe.wait_ge(consts, 2)
            for k in range(NB):
                channel_sums(0, Lin(k), k == 0, k == NB - 1)
            ada_columns((ada_used0, NB), ada_acc[:], lambda m: MB[:, m:m + 1])

            pe.wait_ge(mod_ready, 1)

            def conv_units(i, streamed):
                for a in range(2):
                    for k in range(4):
                        u, n = Lin(U_A + 4 * a + k, i, 8), Lin(N_A + 4 * a + k, i, 8)
                        if streamed and not (a or k):
                            first_unit(u, n, hH, hL, h_hi_there(0), h_lo_there(0))
                        else:
                            unit(u, n, hH, hL)
                ada_columns((ada_used, Lin(NB, i, NB).v), ada_sum,
                            lambda m: MB[:, bass.ds(Lin(NADA0 + m, i, NB).v, 1)])

            conv_units(0, True)
            with pe.Fori(1, NB // 2) as i:
                conv_units(i, False)
            first_unit(Lin(U_A2), Lin(N_A2), yH, yL, y_hi_there(0), y_lo_there(0))
            unit(Lin(U_A2 + 1), Lin(N_A2 + 1), yH, yL)
            with pe.Fori(1, NB // 2) as i:
                for a in range(2):
                    unit(Lin(U_A2 + a, i, 2), Lin(N_A2 + a, i, 2), yH, yL)
            pe.wait_ge(sgw_masked, 1)
            for g in range(G):
                last = turn(ZB[g // 4][:, (g % 4) * P:(g % 4 + 1) * P], vn[:, g, :], ident[:])
                if g % 4 == 3:
                    last.then_inc(sgw_tr, 1)
            pe.wait_ge(wt_ready, 2)

            with pe.Fori(0, G // 2) as i:
                for a in range(2):
                    u, n = Lin(U_B + 3 * a, i, 6), Lin(N_B + 3 * a, i, 6)
                    g = Lin(a, i, 2)
                    unit(u, n, hH, hL)
                    unit(u + 1, n + 1, hH, hL)
                    pe.wait_ge(emptied[0], (n + 1).v)
                    pe.wait_ge(emptied[1], (n + 1).v)
                    for half in range(2):
                        for q in range(4):
                            ch = 4 * half + q
                            last = turn(ZB[half][:, q * P:(q + 1) * P], vT[:, ch * P:(ch + 1) * P], ident[:])
                        last.then_inc(v_turned, 1)
                    unit(u + 2, n + 2, hH, hL)
                    pe.wait_ge(vn_ready, (g + 1).v)
                    for half in range(2):
                        for q in range(4):
                            ch = 4 * half + q
                            last = mm(CB[half][:, q * P:(q + 1) * P], vn[:, ch, :], WT[:, bass.ds(g.v, 1), :],
                                      start=True, stop=True)
                        last.then_inc(sg_filled, 1)
            first_unit(Lin(U_B2), Lin(N_B2), yH, yL, y_hi_there(2 * NB), y_lo_there(2 * NB))
            unit(Lin(U_B2 + 1), Lin(N_B2 + 1), yH, yL)
            with pe.Fori(1, NB // 2) as i:
                for a in range(2):
                    unit(Lin(U_B2 + a, i, 2), Lin(N_B2 + a, i, 2), yH, yL)
            for half in range(2):
                pe.wait_ge(sq_added, 2 * (NB - 3) + half + 1)
                mm(CB[half][:], ones[:], sq_sum[:, half], start=True, stop=False)
            channel_sums(1, Lin(NB - 1), last=True)

            def part(p, hu, third):
                kind, half = hu // 2, hu % 2
                if third == 0:
                    if half == 0:
                        wait_split(p * 4 + (U_C + kind))
                    pe.wait_ge(emptied[half], (p * C_FILLS + (N_C + (0, 1, 3, 5)[kind])).v)
                last = products(half, kind % 2, hH, hL, ((0, 1, 2), (3, 4, 5), (6, 7))[third])
                if third == 2:
                    last.then_inc(filled[half], 1)

            def norm_sum(p, which, half):
                pe.wait_ge(emptied[half], (p * C_FILLS + (N_C + (2, 4)[which])).v)
                pe.wait_ge(qk_sq, (p * 4 + (2 * which + half + 1)).v)
                mm(PB[half][:], pair_ones[:], sums_in[:, half], start=True, stop=True).then_inc(filled[half], 1)

            def turn_v(p, half):
                pe.wait_ge(emptied[half], (p * C_FILLS + (N_C + 6)).v)
                for q in range(4):
                    ch = 4 * half + q
                    last = turn(PB[half][:, q * P:(q + 1) * P], qr[:, ch * P:(ch + 1) * P], ident[:])
                last.then_inc(filled[half], 1)

            def scores(b, par, a):
                s, own = the_step(a), b + a // STEPS
                if a % STEPS == 0:
                    pe.wait_ge(q_lo, (own * 4 + 4).v)
                    pe.wait_ge(k_lo, (own * 4 + 4).v)
                if upto(b, a - 2).positive:
                    pe.wait_ge(z_copied, upto(b, a - 2).v)
                keys = slice(s["j"] * P, (s["j"] + 1) * P)
                qs = slice(s["half"] * HT + s["c0"], (s["half"] + 1) * HT)
                o = ZB[a % 2][:, s["c0"]:HT]
                q, k, kl = (x[par][s["head"]] for x in (Q, K, KL))
                mm(o, k[:, keys], q[:, qs], start=True, stop=False)
                if s["diagonal"]:
                    mm(ZB[a % 2][:, s["c0"]:s["c0"] + P], ident_r[:], mask_r[:], start=False, stop=False,
                       skip_group_check=True)
                mm(o, kl[:, keys], q[:, qs], start=False, stop=True).then_inc(z_filled, 1)

            def suffix(b, a, upper):
                s = the_step(a)
                if upper:
                    pe.wait_ge(sp_lo, upto(b, a).v)
                else:
                    pe.wait_ge(arg_ready, upto(b, a).v)
                o, w = CB[s["chain"] % 2][:, s["c0"]:HT], U_r if upper else Uc_r
                mm(o, w[:], spH[:, a % 2, s["c0"]:HT], start=upper and s["first"], stop=False, skip_group_check=True)
                mm(o, w[:], spL[:, a % 2, s["c0"]:HT], start=False, stop=upper and s["last"],
                   skip_group_check=True).then_inc(u_done if upper else sp_free, 1)

            def weighted_v(b, par, a):
                s, own = the_step(a), b + a // STEPS
                if a % STEPS == 0:
                    for half in range(2):
                        pe.wait_ge(emptied[half], (own * C_FILLS + (N_C + C_FILLS)).v)
                if s["first"] and (own * 4 + (s["chain"] - 1)).positive:
                    pe.wait_ge(o_sum, (own * 4 + (s["chain"] - 1)).v)
                pe.wait_ge(p_lo, upto(b, a).v)
                o, w = OB[s["chain"] % 2][:, s["c0"]:HT], V[par][:, s["j"], s["head"], :]
                mm(o, w, pH[:, s["c0"]:HT], start=s["first"], stop=False, skip_group_check=True)
                mm(o, w, pL[:, s["c0"]:HT], start=False, stop=s["last"],
                   skip_group_check=True).then_inc(pv_done, 1)

            parts = [(hu, third) for hu in range(8) for third in range(3)]

            def out_part(d):
                j, third = divmod(d, 3)
                slot = (U_D + j) % 2
                if third == 0:
                    wait_split(Lin(U_D + j))
                for half, k, kind in out_parts[third * OUT_THIRD:(third + 1) * OUT_THIRD]:
                    if k == 0 and kind == 0:
                        pe.wait_ge(emptied[half], N_D + j)
                    if j == 0 and half == 0:
                        pe.wait_ge(hh_ready, 2 * NB + k + 1)
                        pe.wait_ge(hl_ready[k % 2], NB + k // 2 + 1)
                    w, r = ((wH, hH), (wH, hL), (wL, hH))[kind]
                    last = mm(PB[half][:], w[:, slot, k], r[:, k, HALF[half]], start=k == 0 and kind == 0,
                              stop=k == NP - 2 and kind == 2)
                    if k == NP - 2 and kind == 2:
                        last.then_inc(filled[half], 1)

            def pair(p, par, first, end, ahead=True):
                b = p - 1
                if first == STEPS:
                    first_unit(Lin(U_C), Lin(N_C), hH, hL, h_hi_there(1), h_lo_there(1))
                for t in slots(end):
                    if first <= t - 2 < end:
                        weighted_v(b, par_of(par, t - 2), t - 2)
                    if first <= t + 3 < end:
                        scores(b, par_of(par, t + 3), t + 3)
                    if first <= t < end:
                        suffix(b, t, True)
                    if end == STEPS and t >= OUT_FROM:
                        out_part(t - OUT_FROM)
                    if end > STEPS:
                        for hu, third in parts[t + 2:t + 3]:
                            if hu >= 2 or first < STEPS:
                                part(p, hu, third)
                        if ahead and t >= STEPS - 2:
                            part(p + 1, *parts[t - (STEPS - 2)])
                        if t in SUMS_AT:
                            norm_sum(p, *divmod(SUMS_AT.index(t), 2))
                        if t in TURN_AT:
                            turn_v(p, TURN_AT.index(t))
                    if first <= t < end and not the_step(t)["last"]:
                        suffix(b, t, False)

            pe.wait_ge(k_zeroed, 1)
            pair(Lin(0), 0, STEPS, 2 * STEPS)
            pair(Lin(1), 1, 0, 2 * STEPS)
            with pe.Fori(0, NP // 2 - 2) as i:
                pair(Lin(2, i, 2), 0, -STEPS, 2 * STEPS)
                pair(Lin(3, i, 2), 1, -STEPS, 2 * STEPS)
            pair(Lin(NP - 2), 0, -STEPS, 2 * STEPS)
            pair(Lin(NP - 1), 1, -STEPS, 2 * STEPS, ahead=False)
            pair(Lin(NP), 0, -STEPS, STEPS, ahead=False)

            D_BANKS = PB + CB
            wait_split(Lin(U_LAST))

            def last_rows(half, j):
                n = half * NB + j
                if n < 2:
                    pe.wait_ge(emptied[n], N_D + NB)
                if n >= 4:
                    pe.wait_ge(d_out, n - 3)
                h, acc = HALF[half], D_BANKS[n % 4][:]
                mm(acc, wH[:, 0, j], hH[:, NP - 1, h], start=True, stop=False)
                mm(acc, wH[:, 0, j], hL[:, NP - 1, h], start=False, stop=False)
                mm(acc, wL[:, 0, j], hH[:, NP - 1, h], start=False, stop=True).then_inc(d_filled, 1)

            def turn_chunk(ch):
                for s in range(2):
                    if ch:
                        pe.wait_ge(t_out[s], ch)
                    for q in range(4):
                        j = 4 * s + q
                        pe.wait_ge(d_out, (ch // 4) * NB + j + 1)
                        last = turn(ZB[s][:, q * P:(q + 1) * P], xo[j][:, ch * P:(ch + 1) * P], ident[:])
                    last.then_inc(t_filled, 1)

            for half in range(2):
                pe.wait_ge(y7_lo, half + 1)
                for j in range(NB):
                    last_rows(half, j)
                    if half == 1 and j % 2:
                        turn_chunk(j // 2)
            for ch in range(NC // 2, NC):
                turn_chunk(ch)

        @block.scalar
        def _(act):
            f = nc.scalar.activation

            def copy(o, i):
                return nc.scalar.activation(o, i, ACT.Copy)

            def split_hi(u):
                slot = u.base % 2
                act.wait_ge(raw_in[slot], (u.half() * 16 + 16).v)
                copy(wH[:, slot], raw[:, slot]).then_inc(w_hi, 1)

            def unit_done(n):
                act.wait_ge(filled[1], (n + 1).v)

            nc.scalar.preload_act_table_set(LN_EXP_SET)
            for ch in range(NC):
                act.wait_ge(filled[1], ch + 1)
                copy(xT[:, 4:8, ch * P:(ch + 1) * P], PB[1][:].rearrange("p (k t) -> p k t", k=4)
                     ).then_inc(emptied[1], 1)
                if ch == PRM_AT + 1:
                    act.wait_ge(prm_ready, 1)
                    f(ca[:, 0, :], prm[:, C_C:C_C + NB], ACT.Exp, scale=-1.0).then_inc(ce, 1)

            def squares(layer, k):
                for half in range(2):
                    dst = sums_in[:, half]
                    if layer == 0 and k.base:
                        act.wait_ge(sum_done, 2 * k.base + half - 1)
                    elif layer and not (k.coef or k.base):
                        dst = sq_sum[:, half]
                    elif layer and (k.coef or k.base > 1):
                        act.wait_ge(sq_added, (k * 2 + (half - 3)).v)
                    src = xT[:, bass.ds(k.v, 1), HALF[half]] if k.coef else xT[:, k.base, HALF[half]]
                    f(dst, src, ACT.Square).then_inc(sq_ready, 1)

            def rms_of_x(layer):
                for half in range(2):
                    act.wait_ge(sum_done, 2 * NB + 2 * layer - 1 + half)
                    f(sums_in[:, half], CB[half][:], ACT.Ln, bias=eps_t[:], scale=1.0 / D).then_inc(rms_ln, 1)
                    act.wait_ge(rms_ln, 2 * layer + half + 1)
                    f(sums_in[:, half], sums_in[:, half], ACT.Exp, scale=-0.5).then_inc(rs_ready, 1)

            def h_hi(layer, of):
                for k in range(NB):
                    act.wait_ge(ht_ready, NB * layer + k + 1)
                    of(k).then_inc(hh_ready, 1)

            act.wait_ge(emptied[0], NC)
            act.wait_ge(emptied[1], NC)
            act.wait_ge(consts, 2)
            for k in range(NB):
                squares(0, Lin(k))
            rms_of_x(0)
            nc.scalar.preload_act_table_set(SILU_SET)
            for m in range(2):
                split_hi(Lin(U_A + m))
            h_hi(0, lambda k: copy(hH[:, k], h_f[:, k]))
            act.wait_ge(x_saved, 16)
            for s in range(2):
                act.wait_ge(hl_ready[s], NB // 2)

            with act.Fori(0, NB) as i:
                u, n = Lin(U_A, i, 4), Lin(N_A, i, 4)

                for half in range(2):
                    act.wait_ge(filled[half], (n + 1).v)
                    copy(cs[:, HALF[half]], PB[half][:]).then_inc(emptied[half], 1)
                split_hi(u + 2)
                unit_done(n + 1)
                split_hi(u + 3)
                for half in range(2):
                    act.wait_ge(filled[half], (n + 3).v)
                    f(sz[:, HALF[half]], PB[half][:], ACT.Silu).then_inc(emptied[half], 1)
                split_hi(u + 4)
                unit_done(n + 3)
                split_hi(u + 5)
                for half in range(2):
                    act.wait_ge(emptied[half], (n + 4).v)
                    copy(yH[:, bass.ds(i, 1), HALF[half]], cv[:, HALF[half]]).then_inc(y_hi, 1)
            with act.Fori(0, NB // 2) as i:
                for a in range(2):
                    unit_done(Lin(N_A2 + a, i, 2))
                    split_hi(Lin(U_A2 + a + 2, i, 2))
            with act.Fori(0, G // 2) as i:
                for a in range(2):
                    u, n = Lin(U_B + 3 * a, i, 6), Lin(N_B + 3 * a, i, 6)
                    for half in range(2):
                        act.wait_ge(filled[half], (n + 1).v)
                        copy(vT[:, HALF[half]], PB[half][:]).then_inc(emptied[half], 1)
                    split_hi(u + 2)
                    unit_done(n + 1)
                    split_hi(u + 3)
                    for half in range(2):
                        act.wait_ge(filled[half], (n + 3).v)
                        f(sz[:, HALF[half]], PB[half][:], ACT.Silu).then_inc(emptied[half], 1)
                    split_hi(u + 4)
                    for half in range(2):
                        act.wait_ge(y_prod, Lin(2 * a + half + 1, i, 4).v)
                        copy(yH[:, bass.ds(Lin(a, i, 2).v, 1), HALF[half]], cv[:, HALF[half]]).then_inc(y_hi, 1)
            def finished_block(i, a):
                n = Lin(N_B2 + a, i, 2)
                unit_done(n)
                split_hi(Lin(U_B2 + a + 2, i, 2))
                for half in range(2):
                    act.wait_ge(emptied[half], (n + 1).v)
                squares(1, Lin(a, i, 2) if not isinstance(i, int) else Lin(a))

            finished_block(0, 0)
            finished_block(0, 1)
            with act.Fori(1, NB // 2) as i:
                for a in range(2):
                    finished_block(i, a)
            nc.scalar.preload_act_table_set(LN_EXP_SET)
            rms_of_x(1)
            h_hi(1, lambda k: f(hH[:, k], xT[:, k], ACT.Identity, bias=mod[:, 3 * NB + k:3 * NB + k + 1]))

            def z_copy(b, a):
                s = the_step(a)
                act.wait_ge(z_filled, upto(b, a).v)
                if upto(b, a - 4).positive:
                    act.wait_ge(p_lo, upto(b, a - 4).v)
                copy(zs[a % 4][:, s["c0"]:HT], ZB[a % 2][:, s["c0"]:HT]).then_inc(z_copied, 1)

            def exp_abs(b, a):
                v = e[a % 3][:, the_step(a)["c0"]:HT]
                act.wait_ge(e_neg, upto(b, a).v)
                f(v, v, ACT.Exp).then_inc(e_exp, 1)

            def ln_abs(b, a):
                v = e[a % 3][:, the_step(a)["c0"]:HT]
                act.wait_ge(e_exp, upto(b, a).v)
                f(v, v, ACT.Ln, bias=1.0).then_inc(e_ln, 1)

            def weight(b, a):
                v = zs[a % 4][:, the_step(a)["c0"]:HT]
                act.wait_ge(arg_ready, upto(b, a).v)
                f(v, v, ACT.Exp).then_inc(w_ready, 1)

            def o_shift(b, a):
                s = the_step(a)
                act.wait_ge(pv_done, upto(b, a).v)
                mine, other = ROWS[s["head"]], ROWS[1 - s["head"]]
                copy(osh[mine, :], OB[s["chain"] % 2][other, :]).then_inc(o_shifted, 1)

            def pair(p, par, first, end):
                b = p - 1
                n = p * C_FILLS + N_C
                for t in slots(end):
                    if first <= t + 2 < end:
                        z_copy(b, t + 2)
                    if first <= t - 1 < end:
                        weight(b, t - 1)
                    if first <= t + 2 < end:
                        exp_abs(b, t + 2)
                        ln_abs(b, t + 2)
                    if first <= t - 2 < end and the_step(t - 2)["last"]:
                        o_shift(b, t - 2)
                    if end == STEPS:
                        for k in OUT_SPLIT.get(t, ()):
                            if k < YS:
                                act.wait_ge(ys_in[k], 16)
                                copy(hH[:, k], y_in[:, k]).then_inc(hh_ready, 1)
                            else:
                                act.wait_ge(y_ready, k * 4 + 4)
                                copy(hH[:, k], gz[k % 2]).then_inc(hh_ready, 1)
                        if t > OUT_FROM and (t - OUT_FROM) % 3 == 0:
                            j = (t - OUT_FROM) // 3 - 1
                            unit_done(Lin(N_D + j))
                            split_hi(Lin(U_D + j + 2))
                        continue
                    if t in (2, 3):
                        half = (2, 3).index(t)
                        act.wait_ge(filled[half], (n + 1).v)
                        if p.coef or p.base:
                            act.wait_ge(gz_ready, (p * 2 + (half - 1)).v)
                        f(sums_in[:, half], PB[half][:], ACT.Square).then_inc(qk_sq, 1)
                        copy(qr[:, HALF[half]], PB[half][:]).then_inc(emptied[half], 1)
                    if t in (7, 10):
                        half = (7, 10).index(t)
                        act.wait_ge(filled[half], (n + 2).v)
                        copy(kr[:, HALF[half]], PB[half][:]).then_inc(emptied[half], 1)
                    if t in (9, 12, 15, 18):
                        which, half = divmod((9, 12, 15, 18).index(t), 2)
                        act.wait_ge(filled[half], (n + (3, 5)[which]).v)
                        f(sums_in[:, half], PB[half][:], ACT.Ln, bias=eps_t[:], scale=1.0 / DH
                          ).then_inc(emptied[half], 1)
                        act.wait_ge(emptied[half], (n + (3, 5)[which]).v)
                        f(sums_in[:, half], sums_in[:, half], ACT.Exp, scale=-0.5).then_inc(qk_rs, 1)
                    if t in (11, 14):
                        half = (11, 14).index(t)
                        act.wait_ge(qk_n, (p * 4 + (half + 1)).v)
                        act.wait_ge(emptied[half], (n + 2).v)
                        f(sums_in[:, half], kr[:, HALF[half]], ACT.Square).then_inc(qk_sq, 1)
                    if t in (13, 16):
                        half = (13, 16).index(t)
                        act.wait_ge(filled[half], (n + 4).v)
                        act.wait_ge(q_lo, (p * 4 + (2 * half + 2)).v)
                        copy(qr[:, HALF[half]], PB[half][:]).then_inc(emptied[half], 1)
                    if t in (19, 22):
                        half = (19, 22).index(t)
                        act.wait_ge(filled[half], (n + 6).v)
                        act.wait_ge(qk_n, (p * 4 + (half + 3)).v)
                        f(sums_in[:, half], PB[half][:], ACT.Exp, scale=-1.0).then_inc(gz_exp, 1)
                        if p.base > 1:
                            act.wait_ge(y_saved, (p * 16 + (NB - 1) * 16).v)
                        copy(gz[par][:, HALF[half]], PB[half][:]).then_inc(emptied[half], 1)
                    if t in (20, 23):
                        half = (20, 23).index(t)
                        act.wait_ge(gz_exp, (p * 2 + (half + 1)).v)
                        f(sums_in[:, half], sums_in[:, half], ACT.Ln, bias=1.0).then_inc(gz_ln, 1)
                        act.wait_ge(gz_ln, (p * 2 + (half + 1)).v)
                        f(sums_in[:, half], sums_in[:, half], ACT.Exp, scale=-1.0).then_inc(gz_sig, 1)
                    if t in (21, 23):
                        half = (21, 23).index(t)
                        act.wait_ge(filled[half], (n + 7).v)
                        src = PB[half][:].rearrange("p (j h d) -> p j h d", j=4, h=2)
                        blocks = slice(4 * half, 4 * half + 4)
                        copy(V[par][:, blocks, 0, 0:DH], src[:, :, 0, :])
                        copy(V[par][:, blocks, 1, DH:P], src[:, :, 1, :]).then_inc(v_hi, 1)
                    if t in SPLIT_AT:
                        kind = SPLIT_AT.index(t)
                        unit_done(n + (0, 1, 3, 5)[kind])
                        split_hi(p * 4 + (U_C + kind + 2))

            pair(Lin(0), 0, STEPS, 2 * STEPS)
            pair(Lin(1), 1, 0, 2 * STEPS)
            with act.Fori(0, NP // 2 - 1) as i:
                pair(Lin(2, i, 2), 0, -STEPS, 2 * STEPS)
                pair(Lin(3, i, 2), 1, -STEPS, 2 * STEPS)
            pair(Lin(NP), 0, -STEPS, STEPS)

            for half in range(2):
                act.wait_ge(y_ready, (NP - 1) * 4 + 3 + half)
                copy(hH[:, NP - 1, HALF[half]], gz[1][:, HALF[half]]).then_inc(y7_hi, 1)
            for ch in range(NC):
                for s in range(2 if ch < NC // 2 else 1):
                    act.wait_ge(t_filled, 2 * ch + s + 1)
                    copy(ot[ch][:, s * HT:(s + 1) * HT], ZB[s][:]).then_inc(t_out[s], 1)

        @block.vector
        def _(dve):
            tt, ts, stt, copy = (nc.vector.tensor_tensor, nc.vector.tensor_scalar,
                                 nc.vector.scalar_tensor_tensor, nc.vector.tensor_copy)

            def f32(ap):
                return ap.bitcast(F32)

            def split_lo(u):
                slot = u.base % 2
                dve.wait_ge(w_hi, (u + 1).v)
                tt(wL[:, slot], raw[:, slot], f32(wH[:, slot]), ALU.subtract).then_inc(w_lo, 1)

            for o, i, value in ((0, 0, 1.0), (0, 1, 0.0), (1, 0, 0.0), (1, 1, 1.0)):
                nc.vector.memset(pair_ones[ROWS[o], ROWS[i]], value)
            dve.wait_ge(consts, 2)
            copy(U_r[:], U_f[:]).then_inc(start_step, 1)
            ts(Uc_r[:], U_f[:], -1.0, 1.0, ALU.mult, ALU.add).then_inc(start_step, 1)
            copy(ident_r[:], ident[:])
            copy(mask_r[:], mask[:])
            for ch in range(NC):
                dve.wait_ge(filled[0], ch + 1)
                copy(xT[:, 0:4, ch * P:(ch + 1) * P], PB[0][:].rearrange("p (k t) -> p k t", k=4)
                     ).then_inc(emptied[0], 1)
                if ch == PRM_AT:
                    dve.wait_ge(prm_tr, 1)
                    copy(prm[:, 0:NPRM], ZB[0][:, 0:NPRM]).then_inc(prm_ready, 1)
                    dve.wait_ge(prm_ready, 1)
                    ts(qn_scaled[:], prm[:, C_QN:C_QN + 1], float(DH) ** -0.5, None, ALU.mult).then_inc(start_step, 1)
                if ch == PRM_AT + 2:
                    dve.wait_ge(ce, 1)
                    ts(ca[:, 1, :], ca[:, 0, :], 1.0, None, ALU.add).then_inc(start_step, 1)
                    dve.wait_ge(start_step, 4)
                    nc.vector.reciprocal(ca[:, 2, :], ca[:, 1, :]).then_inc(start_step, 1)
                    dve.wait_ge(start_step, 5)
                    tt(ca[:, 0, :], ca[:, 2, :], prm[:, C_C:C_C + NB], ALU.mult).then_inc(start_step, 1)
            for k in range(NB):
                dve.wait_ge(ada_in0[k], 16)
                if k == 0:
                    dve.wait_ge(start_step, 6)
                    ts(ada_acc[:], ada_raw[:, k], ca[:, 0, k:k + 1], None, ALU.mult).then_inc(ada_used0, 1)
                else:
                    dve.wait_ge(ada_used0, k)
                    stt(ada_acc[:], ada_raw[:, k], ca[:, 0, k:k + 1], ada_acc[:], ALU.mult, ALU.add).then_inc(ada_used0, 1)
            dve.wait_ge(rs_ready, 2)
            for k in range(XN_DVE):
                tt(xn[:, k], xT[:, k], ada_sum, ALU.mult).then_inc(xn_ready, 1)

            def modulation(lo, hi, done):
                dve.wait_ge(ada_done, done)
                tt(mod[:, lo:hi], MB[:, lo:hi], prm[:, C_ADA + lo:C_ADA + hi], ALU.add).then_inc(mod_ready, 1)

            def norm_gain(layer, ready):
                dve.wait_ge(mod_ready, ready)
                at = 3 * NB * layer + NB
                stt(gs[:, NB * layer:NB * layer + NB], mod[:, at:at + NB], 1.0,
                    prm[:, C_LN + NB * layer:C_LN + NB * layer + NB], ALU.add, ALU.mult).then_inc(start_step, 1)

            modulation(0, NADA0, 1)
            norm_gain(0, 1)
            dve.wait_ge(start_step, 7)
            for k in range(NB):
                dve.wait_ge(*((xn_ready, k + 1) if k < XN_DVE else (xn_ready_p, k - XN_DVE + 1)))
                ts(h_f[:, k], xn[:, k], gs[:, k:k + 1], mod[:, k:k + 1], ALU.mult, ALU.add).then_inc(ht_ready, 1)
                if k == 1:
                    split_lo(Lin(U_A))
                if k % 2:
                    dve.wait_ge(hh_ready, k)
                    tt(hL[:, k - 1], h_f[:, k - 1], f32(hH[:, k - 1]), ALU.subtract).then_inc(hl_ready[0], 1)
            split_lo(Lin(U_A + 1))
            for s in range(2):
                dve.wait_ge(hl_ready[s], NB // 2)
            dve.wait_ge(x_saved, 16)

            nc.vector.memset(cx[:, 0:2], 0.0).then_inc(start_step, 1)
            dve.wait_ge(start_step, 8)

            def ada_block(i, k):
                dve.wait_ge(ada_in1[k % 2], (i * 64 + 16 * (k // 2 + 1)).v)
                c_k = ca[:, 0, k:k + 1]
                if k == 0:
                    dve.wait_ge(ada_done, (i + 1).v)
                    ts(ada_sum, ada_in[0], c_k, None, ALU.mult).then_inc(ada_used, 1)
                else:
                    dve.wait_ge(ada_used, (i * NB + k).v)
                    stt(ada_sum, ada_in[k % 2], c_k, ada_sum, ALU.mult, ALU.add).then_inc(ada_used, 1)

            def conv_block(i, a):
                u, n = Lin(U_A + 4 * a, i, 8), Lin(N_A + 4 * a, i, 8)
                j = Lin(a, i, 2)

                def conv_done(k):
                    dve.wait_ge(conv_step, (j * 4 + k).v)

                def tap(w):
                    return prm[:, bass.ds((j + (C_CONV + w * NB)).v, 1)]

                split_lo(u + 2)
                for half in range(2):
                    dve.wait_ge(filled[half], (n + 2).v)
                    tt(cx[:, 2 + half * HT:2 + (half + 1) * HT], cs[:, HALF[half]], PB[half][:], ALU.mult
                       ).then_inc(emptied[half], 1)
                split_lo(u + 3)
                ada_block(Lin(0, i, 1), 4 * a)
                dve.wait_ge(emptied[0], (n + 2).v)
                dve.wait_ge(emptied[1], (n + 2).v)
                ts(cv[:], cx[:, 0:T], tap(0), None, ALU.mult).then_inc(conv_step, 1)
                conv_done(1)
                stt(cv[:], cx[:, 1:T + 1], tap(1), cv[:], ALU.mult, ALU.add).then_inc(conv_step, 1)
                conv_done(2)
                stt(cv[:], cx[:, 2:T + 2], tap(2), cv[:], ALU.mult, ALU.add).then_inc(conv_step, 1)
                ada_block(Lin(0, i, 1), 4 * a + 1)
                split_lo(u + 4)
                dve.wait_ge(emptied[0], (n + 3).v)
                dve.wait_ge(emptied[1], (n + 3).v)
                conv_done(3)
                tt(cv[:], cv[:], sz[:], ALU.mult).then_inc(conv_step, 1)
                ada_block(Lin(0, i, 1), 4 * a + 2)
                ada_block(Lin(0, i, 1), 4 * a + 3)
                conv_done(4)
                for half in range(2):
                    dve.wait_ge(filled[half], (n + 4).v)
                    tt(cv[:, HALF[half]], cv[:, HALF[half]], PB[half][:], ALU.mult).then_inc(emptied[half], 1)
                split_lo(u + 5)
                for half in range(2):
                    dve.wait_ge(y_hi, (j * 2 + (half + 1)).v)
                    tt(yL[:, bass.ds(j.v, 1), HALF[half]], cv[:, HALF[half]], f32(yH[:, bass.ds(j.v, 1), HALF[half]]),
                       ALU.subtract).then_inc(y_lo, 1)

            with dve.Fori(0, NB // 2) as i:
                for a in range(2):
                    conv_block(i, a)
            modulation(NADA0, NADA, 5)
            norm_gain(1, 2)

            def residual(j, n, dst, gate, loaded):
                for half in range(2):
                    dve.wait_ge(filled[half], (n + 1).v)
                    if half == 0:
                        loaded()
                    d = dst(HALF[half])
                    stt(d, PB[half][:], gate, d, ALU.mult, ALU.add).then_inc(emptied[half], 1)

            def mod_col(base, i, coef):
                return mod[:, bass.ds(Lin(base, i, coef).v, 1)]

            dve.wait_ge(mod_ready, 2)
            with dve.Fori(0, NB // 2) as i:
                for a in range(2):
                    residual(None, Lin(N_A2 + a, i, 2), lambda h, a=a: xa[a][:, h], mod_col(2 * NB + a, i, 2),
                             lambda a=a: dve.wait_ge(xa_in[a], Lin(16, i, 16).v))
                    split_lo(Lin(U_A2 + a + 2, i, 2))
            for half in range(2):
                dve.wait_ge(sgw_tr, half + 1)
                copy(WT[:, 4 * half:4 * half + 4, :], ZB[half][:].rearrange("p (g t) -> p g t", g=4)
                     ).then_inc(wt_ready, 1)
            dve.wait_ge(sgb_in, 16)
            for a in range(2):
                dve.wait_ge(xa_out[a], 16 * (NB // 2))

            with dve.Fori(0, G // 2) as i:
                for a in range(2):
                    u, n = Lin(U_B + 3 * a, i, 6), Lin(N_B + 3 * a, i, 6)
                    g = Lin(a, i, 2)
                    split_lo(u + 2)
                    for half in range(2):
                        dve.wait_ge(filled[half], (n + 2).v)
                        copy(us[:, HALF[half]], PB[half][:]).then_inc(emptied[half], 1)
                    split_lo(u + 3)
                    for half in range(2):
                        dve.wait_ge(v_turned, (g * 2 + (half + 1)).v)
                        copy(vn[:, 4 * half:4 * half + 4, :], ZB[half][:].rearrange("p (c d) -> p c d", c=4)
                             ).then_inc(vn_step, 1)
                    sq = vT[:].rearrange("p (c d) -> p c d", c=NC)
                    dve.wait_ge(vn_step, (g * 4 + 2).v)
                    tt(sq, vn[:], vn[:], ALU.mult).then_inc(vn_step, 1)
                    dve.wait_ge(vn_step, (g * 4 + 3).v)
                    nc.vector.tensor_reduce(ssq[:], sq, AX_X, ALU.add).then_inc(vn_step, 1)
                    dve.wait_ge(vn_step, (g * 4 + 4).v)
                    ts(ssq[:], ssq[:], 1.0 / P, EPS, ALU.mult, ALU.add).then_inc(ssq_ready, 1)
                    dve.wait_ge(rv_ready, (g + 1).v)
                    tt(vn[:], vn[:], rv[:].rearrange("p (c o) -> p c o", o=1).broadcast_to([P, NC, P]), ALU.mult
                       ).then_inc(vn_ready, 1)
                    dve.wait_ge(filled[1], (n + 3).v)
                    split_lo(u + 4)
                    for half in range(2):
                        dve.wait_ge(emptied[half], (n + 3).v)
                        tt(us[:, HALF[half]], us[:, HALF[half]], sz[:, HALF[half]], ALU.mult).then_inc(gate_step, 1)
                    for half in range(2):
                        dve.wait_ge(sg_filled, (g * 2 + (half + 1)).v)
                        v4 = cv[:, HALF[half]].rearrange("p (c t) -> p c t", c=4)
                        stt(v4, CB[half][:].rearrange("p (c t) -> p c t", c=4),
                            prm[:, bass.ds((g + C_SGN).v, 1)],
                            sgb[:, bass.ds(g.v, 1), :].broadcast_to([P, 4, P]), ALU.mult, ALU.add).then_inc(gate_step, 1)
                    for half in range(2):
                        dve.wait_ge(gate_step, (g * 4 + (half + 3)).v)
                        tt(cv[:, HALF[half]], cv[:, HALF[half]], us[:, HALF[half]], ALU.mult).then_inc(y_prod, 1)
                    for half in range(2):
                        dve.wait_ge(y_hi, (g * 2 + (2 * NB + half + 1)).v)
                        tt(yL[:, bass.ds(g.v, 1), HALF[half]], cv[:, HALF[half]],
                           f32(yH[:, bass.ds(g.v, 1), HALF[half]]), ALU.subtract).then_inc(y_lo, 1)
            with dve.Fori(0, NB // 2) as i:
                for a in range(2):
                    residual(None, Lin(N_B2 + a, i, 2),
                             lambda h, a=a: xT[:, bass.ds(Lin(a, i, 2).v, 1), h], mod_col(2 * NB + a, i, 2),
                             lambda a=a: dve.wait_ge(x1_in[a], Lin(16, i, 16).v))
                    split_lo(Lin(U_B2 + a + 2, i, 2))
            for par in range(2):
                for head in range(2):
                    last = nc.vector.memset(KL[par][head][ROWS[1 - head], :].bitcast(F32), 0.0)
            last.then_inc(k_zeroed, 1)
            dve.wait_ge(start_step, 9)
            dve.wait_ge(rs_ready, 4)
            dve.wait_ge(y_saved, 16 * NB)
            for k in range(NB):
                stt(xT[:, k], xT[:, k], gs[:, NB + k:NB + k + 1], ada_sum, ALU.mult, ALU.mult).then_inc(ht_ready, 1)
            for k in range(NB):
                dve.wait_ge(hh_ready, NB + k + 1)
                stt(hL[:, k], xT[:, k], mod[:, 3 * NB + k:3 * NB + k + 1], f32(hH[:, k]),
                    ALU.add, ALU.subtract).then_inc(hl_ready[k % 2], 1)

            def negated(b, a):
                s = the_step(a)
                dve.wait_ge(z_copied, upto(b, a).v)
                if upto(b, a - 3).positive:
                    dve.wait_ge(sp_lo, upto(b, a - 3).v)
                ts(e[a % 3][:, s["c0"]:HT].bitcast(U32), zs[a % 4][:, s["c0"]:HT].bitcast(U32), SIGN, None,
                   ALU.bitwise_or).then_inc(e_neg, 1)

            def softplus(b, a):
                s = the_step(a)
                v = e[a % 3][:, s["c0"]:HT]
                dve.wait_ge(e_ln, upto(b, a).v)
                stt(v, zs[a % 4][:, s["c0"]:HT], 0.0, v, ALU.max, ALU.add).then_inc(sp_ready, 1)
                dve.wait_ge(sp_ready, upto(b, a).v)
                if upto(b, a - 2).positive:
                    if the_step(a - 2)["last"]:
                        dve.wait_ge(u_done, upto(b, a - 2).v)
                    else:
                        dve.wait_ge(sp_free, lowers_upto(b, a - 2).v)
                copy(spH[:, a % 2, s["c0"]:HT], v).then_inc(sp_hi, 1)

            def exponent(b, a):
                s = the_step(a)
                v = zs[a % 4][:, s["c0"]:HT]
                dve.wait_ge(u_done, upto(b, a).v)
                tt(v, v, CB[s["chain"] % 2][:, s["c0"]:HT], ALU.subtract).then_inc(arg_ready, 1)

            def weight_hi(b, a):
                v = slice(the_step(a)["c0"], HT)
                dve.wait_ge(w_ready, upto(b, a).v)
                if upto(b, a - 1).positive:
                    dve.wait_ge(pv_done, upto(b, a - 1).v)
                copy(pH[:, v], zs[a % 4][:, v]).then_inc(p_hi, 1)

            def gated(b, par, a):
                s, own = the_step(a), b + a // STEPS
                mine, sums = ROWS[s["head"]], own * 4 + (s["chain"] + 1)
                dve.wait_ge(o_shifted, sums.v)
                tt(osh[mine, :], OB[s["chain"] % 2][mine, :], osh[mine, :], ALU.add).then_inc(o_sum, 1)
                dve.wait_ge(o_sum, sums.v)
                dve.wait_ge(gz_ready, (own * 2 + 2).v)
                d = gz[par][mine, HALF[s["half"]]]
                tt(d, d, osh[mine, :], ALU.mult).then_inc(y_ready, 1)

            def out_sum(n):
                j, half = divmod(n, 2)
                dve.wait_ge(filled[half], N_D + j + 1)
                if half == 0:
                    dve.wait_ge(xo_in[j], 16)
                d = xo[j][:, HALF[half]]
                stt(d, PB[half][:], mod[:, 5 * NB + j:5 * NB + j + 1], d, ALU.mult, ALU.add).then_inc(emptied[half], 1)

            def pair(p, par, first, end):
                b = p - 1
                n = p * C_FILLS + N_C
                for t in slots(end):
                    if end == STEPS and t > OUT_FROM:
                        j, third = divmod(t - OUT_FROM, 3)
                        if third == 0:
                            out_sum(2 * j - 1)
                        if third == 2:
                            out_sum(2 * j)
                    if first <= t + 2 < end:
                        negated(b, t + 2)
                    if first <= t - 1 < end:
                        weight_hi(b, t - 1)
                    if first <= t + 1 < end:
                        softplus(b, t + 1)
                    if first <= t < end:
                        exponent(b, t)
                    if first <= t - 3 < end and the_step(t - 3)["last"]:
                        gated(b, par_of(par, t - 3), t - 3)
                    if end == STEPS:
                        for k in OUT_SPLIT.get(t - 1, ()):
                            dve.wait_ge(hh_ready, 2 * NB + k + 1)
                            tt(hL[:, k], y_in[:, k] if k < YS else gz[k % 2], f32(hH[:, k]), ALU.subtract
                               ).then_inc(hl_ready[k % 2], 1)
                        continue
                    if t in (10, 13, 16, 19):
                        which, half = divmod((10, 13, 16, 19).index(t), 2)
                        h = HALF[half]
                        r = (qr, kr)[which]
                        gain = (qn_scaled[:], prm[:, C_KN:C_KN + 1])[which]
                        dve.wait_ge(qk_rs, (p * 4 + (2 * which + half + 1)).v)
                        stt(r[:, h], r[:, h], gain, sums_in[:, half], ALU.mult, ALU.mult).then_inc(qk_n, 1)
                        dve.wait_ge(qk_n, (p * 4 + (2 * which + half + 1)).v)
                        if which == 0:
                            for head in range(2):
                                own = ROWS[head]
                                copy(Q[par][head][own, h], r[own, h]).then_inc(q_hi, 1)
                        else:
                            for head in range(2):
                                own, other = ROWS[head], ROWS[1 - head]
                                copy(K[par][head][own, h], r[own, h])
                                copy(K[par][head][other, h], r[own, h]).then_inc(k_hi, 1)
                    if t in (17, 20):
                        half = (17, 20).index(t)
                        h = HALF[half]
                        for head in range(2):
                            own = ROWS[head]
                            dve.wait_ge(k_hi, (p * 4 + (2 * half + head + 1)).v)
                            tt(KL[par][head][own, h], kr[own, h], f32(K[par][head][own, h]), ALU.subtract
                               ).then_inc(k_lo, 1)
                    if t in (11, 14):
                        half = (11, 14).index(t)
                        h = HALF[half]
                        for head in range(2):
                            dve.wait_ge(q_hi, (p * 4 + (2 * half + head + 1)).v)
                            own, other = ROWS[head], ROWS[1 - head]
                            tt(Q[par][head][other, h], qr[own, h], f32(Q[par][head][own, h]), ALU.subtract
                               ).then_inc(q_lo, 1)
                    if t in (21, 23):
                        half = (21, 23).index(t)
                        d = gz[par][:, HALF[half]]
                        dve.wait_ge(gz_sig, (p * 2 + (half + 1)).v)
                        dve.wait_ge(emptied[half], (n + 6).v)
                        tt(d, d, sums_in[:, half], ALU.mult).then_inc(gz_ready, 1)
                    if t in (21, 23):
                        half = (21, 23).index(t)
                        dve.wait_ge(v_hi, (p * 2 + (half + 1)).v)
                        src = PB[half][:].rearrange("p (j h d) -> p j h d", j=4, h=2)
                        blocks = slice(4 * half, 4 * half + 4)
                        tt(V[par][:, blocks, 0, DH:P], src[:, :, 0, :], f32(V[par][:, blocks, 0, 0:DH]), ALU.subtract)
                        tt(V[par][:, blocks, 1, 0:DH], src[:, :, 1, :], f32(V[par][:, blocks, 1, DH:P]), ALU.subtract
                           ).then_inc(emptied[half], 1)

            pair(Lin(0), 0, STEPS, 2 * STEPS)
            pair(Lin(1), 1, 0, 2 * STEPS)
            with dve.Fori(0, NP // 2 - 1) as i:
                pair(Lin(2, i, 2), 0, -STEPS, 2 * STEPS)
                pair(Lin(3, i, 2), 1, -STEPS, 2 * STEPS)
            pair(Lin(NP), 0, -STEPS, STEPS)

            for half in range(2):
                dve.wait_ge(y7_hi, half + 1)
                h = HALF[half]
                tt(hL[:, NP - 1, h], gz[1][:, h], f32(hH[:, NP - 1, h]), ALU.subtract).then_inc(y7_lo, 1)
            out_sum(2 * NB - 1)
            D_BANKS = PB + CB
            for n in range(2 * NB):
                half, j = divmod(n, NB)
                dve.wait_ge(d_filled, n + 1)
                if n == 0:
                    for b in range(2):
                        dve.wait_ge(emptied[b], N_D + NB)
                d = xo[j][:, HALF[half]]
                stt(d, D_BANKS[n % 4][:], mod[:, 5 * NB + j:5 * NB + j + 1], d, ALU.mult, ALU.add).then_inc(d_out, 1)
            for ch in range(NC // 2, NC):
                dve.wait_ge(t_filled, 2 * ch + 2)
                copy(ot[ch][:, HT:T], ZB[1][:]).then_inc(t_out[1], 1)

        @block.gpsimd
        def _(pool):
            g = nc.gpsimd

            def rows(at, src):
                pool.dma_start(prm_rows[at:at + src.shape[0], 0:src.shape[1]], src).then_inc(prm_in, 16)

            rows(C_C, c.rearrange("o (k p) -> (o k) p", p=P))
            rows(C_LN, ln_g.rearrange("l (k p) -> (l k) p", p=P))
            rows(C_ADA, ada_b.rearrange("l (k p) -> (l k) p", p=P))
            rows(C_CONV, conv_w[0].rearrange("w (k p) -> (w k) p", p=P))
            rows(C_SGN, sg_norm[0])
            for at, w in ((C_QN, q_norm), (C_KN, k_norm)):
                for head in range(2):
                    pool.dma_start(prm_rows[at:at + 1, head * DH:(head + 1) * DH], w).then_inc(prm_in, 16)

            steps_of = [0]

            def own(instruction):
                instruction.then_inc(const_step, 1)
                steps_of[0] += 1

            def own_wait():
                pool.wait_ge(const_step, steps_of[0])

            own(g.memset(ones[:], 1.0))
            own(g.memset(mask[:], 0.0))
            own_wait()
            g.affine_select(out=ident[:], in_=mask[:], compare_op=ALU.not_equal, fill=1.0, base=0,
                            pattern=[[-1, P]], channel_multiplier=1).then_inc(consts, 1)
            own(g.affine_select(out=U_f[:], in_=ones[:], compare_op=ALU.is_ge, fill=0.0, base=0,
                                pattern=[[-1, P]], channel_multiplier=1))
            own_wait()
            pool.wait_ge(consts, 1)
            own(g.affine_select(out=mask[:], in_=mask[:], compare_op=ALU.is_gt, fill=MASKED, base=0,
                                pattern=[[1, P]], channel_multiplier=-1))
            own(g.memset(minus_half[:], -0.5))
            own_wait()
            g.memset(eps_t[:], EPS).then_inc(consts, 1)

            pool.wait_ge(emptied[0], NC)
            pool.wait_ge(emptied[1], NC)
            pool.wait_ge(ada_in0[NB - 1], 16)
            pool.dma_start(xd0.rearrange("k p t -> p k t"), xT[:]).then_inc(x_saved, 16)
            pool.wait_ge(rs_ready, 2)
            for k in range(XN_DVE, NB):
                g.tensor_tensor(xn[:, k], xT[:, k], ada_sum, ALU.mult).then_inc(xn_ready_p, 1)
            for k in range(1, NB, 2):
                pool.wait_ge(hh_ready, k + 1)
                g.tensor_tensor(hL[:, k], h_f[:, k], hH[:, k].bitcast(F32), ALU.subtract).then_inc(hl_ready[1], 1)
            pool.wait_ge(x_saved, 16)
            for s in range(2):
                pool.wait_ge(hl_ready[s], NB // 2)

            def xa_load(j, at):
                s = j.base % 2
                pool.dma_start(xa[s][:], at).then_inc(xa_in[s], 16)

            xa_load(Lin(0), xd0[0])
            xa_load(Lin(1), xd0[1])

            def ada_block(i, k, w, at):
                if i.coef or k >= 2:
                    pool.wait_ge(ada_used, (i * NB + (k - 1)).v)
                pool.dma_start(ada_in[k % 2], w[k * P:(k + 1) * P, at]).then_inc(ada_in1[k % 2], 16)

            for k in range(NB):
                ada_block(Lin(0), k, ada_w[0], slice(2 * D, 3 * D))
            with pool.Fori(2, NB // 2 + 1) as i:
                for k in range(NB):
                    ada_block(Lin(-1, i, 1), k, ada_w[1], bass.ds(i * D - 2 * D, D))
            pool.wait_ge(y_lo, 2 * NB)
            pool.dma_start(vn[:], sg_w[0].rearrange("g t s -> t g s")).then_inc(sgw_in, 16)
            pool.dma_start(sgb[:].rearrange("p g t -> p (g t)"),
                           sg_b.rearrange("o g t -> o (g t)").partition_broadcast(P)).then_inc(sgb_in, 16)
            pool.wait_ge(sgw_in, 16)
            g.affine_select(out=vn[:], in_=vn[:], compare_op=ALU.is_ge, fill=0.0, base=0,
                            pattern=[[0, G], [-1, P]], channel_multiplier=1).then_inc(sgw_masked, 1)

            def xa_store(n, at, s, turns):
                pool.wait_ge(emptied[0], (n + 1).v)
                pool.wait_ge(emptied[1], (n + 1).v)
                pool.dma_start(at, xa[s][:]).then_inc(xa_out[s], 16)

            with pool.Fori(0, NB // 2 - 1) as i:
                for a in range(2):
                    xa_store(Lin(N_A2 + a, i, 2), xd1[bass.ds(Lin(a, i, 2).v, 1)], a, i)
                    pool.wait_ge(xa_out[a], Lin(16, i, 16).v)
                    pool.dma_start(xa[a][:], xd0[bass.ds(Lin(a + 2, i, 2).v, 1)]).then_inc(xa_in[a], 16)
            for a in range(2):
                xa_store(Lin(N_A2 + NB - 2 + a), xd1[NB - 2 + a], a, 0)

            with pool.Fori(0, G) as i:
                pool.wait_ge(ssq_ready, Lin(1, i, 1).v)
                g.tensor_tensor(rv[:], ssq[:], minus_half[:], ALU.pow).then_inc(rv_ready, 1)
            pool.wait_ge(y_lo, 4 * NB)
            for a in range(2):
                pool.wait_ge(xa_out[a], 16 * (NB // 2))
            def x1_load(j, at):
                pool.dma_start(xT[:, bass.ds(j.v, 1)] if j.coef else xT[:, j.base], at).then_inc(x1_in[j.base % 2], 16)

            def x2_store(i, a):
                for half in range(2):
                    pool.wait_ge(emptied[half], Lin(N_B2 + a + 1, i, 2).v)
                j = Lin(a, i, 2)
                pool.dma_start(xd2[bass.ds(j.v, 1)].rearrange("o p t -> p o t"), xT[:, bass.ds(j.v, 1)]
                               ).then_inc(y_saved, 16)

            x1_load(Lin(0), xd1[0])
            x1_load(Lin(1), xd1[1])
            def add_squares(j):
                for half in range(2):
                    pool.wait_ge(sq_ready, (j * 2 + (2 * NB + half + 1)).v)
                    g.tensor_tensor(sq_sum[:, half], sq_sum[:, half], sums_in[:, half], ALU.add).then_inc(sq_added, 1)

            with pool.Fori(0, NB // 2 - 1) as i:
                for a in range(2):
                    x2_store(i, a)
                    pool.wait_ge(x1_in[a], Lin(16, i, 16).v)
                    x1_load(Lin(a + 2, i, 2), xd1[bass.ds(Lin(a + 2, i, 2).v, 1)].rearrange("o p t -> p o t"))
                    add_squares(Lin(a + 1, i, 2))
            for a in range(2):
                x2_store(NB // 2 - 1, a)


            def minus(o, i, hi):
                return g.tensor_tensor(o, i, hi.bitcast(F32), ALU.subtract)

            def softplus_lo(b, a):
                v = slice(the_step(a)["c0"], HT)
                pool.wait_ge(sp_hi, upto(b, a).v)
                minus(spL[:, a % 2, v], e[a % 3][:, v], spH[:, a % 2, v]).then_inc(sp_lo, 1)

            def weight_lo(b, a):
                v = slice(the_step(a)["c0"], HT)
                pool.wait_ge(p_hi, upto(b, a).v)
                minus(pL[:, v], zs[a % 4][:, v], pH[:, v]).then_inc(p_lo, 1)

            def pair(p, par, first, end):
                b = p - 1
                for t in slots(end):
                    if first <= t - 1 < end:
                        weight_lo(b, t - 1)
                    if first <= t + 1 < end:
                        softplus_lo(b, t + 1)
                    if end == STEPS and t > OUT_FROM and (t - OUT_FROM) % 3 == 0:
                        u = Lin(U_D + (t - OUT_FROM) // 3 + 1)
                        pool.wait_ge(w_hi, (u + 1).v)
                        minus(wL[:, u.base % 2], raw[:, u.base % 2], wH[:, u.base % 2]).then_inc(w_lo, 1)
                    if first <= t - 3 < end and t == 2 and end > STEPS:
                        own = b + (t - 3) // STEPS
                        pool.wait_ge(y_ready, (own * 4 + 4).v)
                        pool.dma_start(yd[bass.ds(own.v, 1)] if own.coef else yd[own.base],
                                       gz[par_of(par, t - 3)][:]).then_inc(y_saved, 16)
                    if end == STEPS:
                        continue
                    if t - 1 in SPLIT_AT:
                        kind = SPLIT_AT.index(t - 1)
                        u = p * 4 + (U_C + kind + 2)
                        pool.wait_ge(w_hi, (u + 1).v)
                        ks = slice(0, NB // 2)
                        minus(wL[:, kind % 2, ks], raw[:, kind % 2, ks], wH[:, kind % 2, ks])
                    if t - 2 in SPLIT_AT:
                        kind = SPLIT_AT.index(t - 2)
                        ks = slice(NB // 2, NB)
                        minus(wL[:, kind % 2, ks], raw[:, kind % 2, ks], wH[:, kind % 2, ks]).then_inc(w_lo, 1)

            pair(Lin(0), 0, STEPS, 2 * STEPS)
            pair(Lin(1), 1, 0, 2 * STEPS)
            with pool.Fori(0, NP // 2 - 1) as i:
                pair(Lin(2, i, 2), 0, -STEPS, 2 * STEPS)
                pair(Lin(3, i, 2), 1, -STEPS, 2 * STEPS)
            pair(Lin(NP), 0, -STEPS, STEPS)

            pool.wait_ge(y_saved, 16 * (NB + YS))


_INS = ["x", "c", "ln_g", "ada_w", "ada_b", "w_in_ab", "conv_w", "sg_norm", "sg_w", "sg_b", "w_out_ab", "w_in_c",
        "q_norm", "k_norm", "w_out_c"]


def kernel(**inputs):
    import numpy as _np
    import concourse.bacc as _bacc
    from concourse.bass_utils import run_bass_kernel_spmd as _run

    nc = _bacc.Bacc("TRN2", target_bir_lowering=False, num_devices=1)
    arrays, args = {}, []
    for name in _INS:
        a = _np.ascontiguousarray(inputs[name])
        arrays[f"in_{name}"] = a
        args.append(nc.dram_tensor(f"in_{name}", a.shape, mybir.dt.from_np(a.dtype), kind="ExternalInput").ap())
    shape = tuple(inputs["x"].shape)
    args.append(nc.dram_tensor("out_x", shape, F32, kind="ExternalOutput").ap())
    hybrid_trunk(nc, *args)
    r = _run(nc, [arrays], core_ids=[0])
    return r.results[0]["out_x"]
```
